# Optimizing a Trainium2 kernel written in Bass

```python
import jax, jax.numpy as jnp
from jax import lax
import numpy as np

D_MODEL = 1024
BATCH = 1
SEQ = 128
DEPTH = 1
DEC_BATCH = 1
DEC_SEQ = 256
PAST_LEN = 128

GRID_W = 64
POOL_WIDTH = 512
POOL_GROUPS = 4
POOL_GROUP_DIM = POOL_WIDTH // POOL_GROUPS
POOL_WINDOWS = (2, 4, 8, 16)
MLSTM_HEADS = 4
MLSTM_HEAD_DIM = 128
MLSTM_WIDTH = MLSTM_HEADS * MLSTM_HEAD_DIM
MIX_WIDTH = POOL_WIDTH + MLSTM_WIDTH
N_DIR = 2
GATE_COLS = N_DIR * 2 * MLSTM_HEADS
IN_COLS = POOL_WIDTH + 4 * MLSTM_WIDTH + GATE_COLS
CHUNK = 64
N_EXPERTS = 64
TOP_K = 6
N_EXPERT_GROUPS = 8
TOPK_GROUPS = 4
EXPERT_DIM = 256
SHARED_DIM = 256
ROUTED_SCALE = 2.5
N_MOD = 6
EPS = 1e-6

kernel_name = "hybrid_pool_mlstm_moe_flow_step"

def rmsnorm(x, g):
    xf = x.astype(jnp.float32)
    y = xf * lax.rsqrt(jnp.mean(xf * xf, axis=-1, keepdims=True) + EPS)
    return y * g.astype(jnp.float32)

def box_mean(x, w, axis):
    n = x.shape[axis]
    xf = x.astype(jnp.float32)
    pad = [(0, 0)] * x.ndim
    pad[axis] = (1, 0)
    cs = jnp.pad(jnp.cumsum(xf, axis=axis), pad)
    idx = jnp.arange(n)
    lo = jnp.clip(idx - w // 2, 0, n)
    hi = jnp.clip(idx + w - w // 2, 0, n)
    s = jnp.take(cs, hi, axis=axis) - jnp.take(cs, lo, axis=axis)
    shape = [1] * x.ndim
    shape[axis] = n
    cnt = (hi - lo).astype(jnp.float32).reshape(shape)
    return s / cnt

def pool_mixer(u, w_pool, pool_scale, grid):
    B, T, _ = u.shape
    ug = u.astype(jnp.float32).reshape(B, T, POOL_GROUPS, POOL_GROUP_DIM)
    diffs = []
    for g, w in enumerate(POOL_WINDOWS):
        xg = ug[:, :, g, :]
        if grid:
            rows = T // GRID_W
            x2 = xg.reshape(B, rows, GRID_W, POOL_GROUP_DIM)
            mean = box_mean(box_mean(x2, w, 1), w, 2).reshape(B, T, POOL_GROUP_DIM)
        else:
            mean = box_mean(xg, w, 1)
        diffs.append(mean - xg)
    d = jnp.stack(diffs, axis=2)
    y = jnp.einsum("btgc,gce->btge", d, w_pool).reshape(B, T, POOL_WIDTH)
    return y * pool_scale

def mlstm_scan(q, k, v, log_i, log_f, C0, n0, m0):
    B, H, T, Dh = q.shape
    nc = T // CHUNK

    def chunks(a):
        return jnp.moveaxis(a.reshape(a.shape[:2] + (nc, CHUNK) + a.shape[3:]), 2, 0)

    causal = jnp.tril(jnp.ones((CHUNK, CHUNK), dtype=bool))

    def step(carry, xs):
        C, n, m = carry
        qc, kc, vc, ai, lf = xs
        b = jnp.cumsum(lf, axis=-1)
        d_intra = jnp.where(causal, b[..., :, None] - b[..., None, :] + ai[..., None, :], -jnp.inf)
        m_inter = b + m[..., None]
        m_t = jnp.maximum(m_inter, jnp.max(d_intra, axis=-1))
        w_inter = jnp.exp(m_inter - m_t)
        p = jnp.exp(d_intra - m_t[..., None]) * jnp.einsum("bhtd,bhsd->bhts", qc, kc)
        num = w_inter[..., None] * jnp.einsum("bhtd,bhde->bhte", qc, C) + jnp.einsum("bhts,bhse->bhte", p, vc)
        den = w_inter * jnp.einsum("bhtd,bhd->bht", qc, n) + jnp.sum(p, axis=-1)
        h = num / jnp.maximum(jnp.abs(den), jnp.exp(-m_t))[..., None]
        b_last = b[..., -1]
        g = b_last[..., None] - b + ai
        m_new = jnp.maximum(b_last + m, jnp.max(g, axis=-1))
        w_c = jnp.exp(b_last + m - m_new)
        kw = jnp.exp(g - m_new[..., None])[..., None] * kc
        C_new = w_c[..., None, None] * C + jnp.einsum("bhsd,bhse->bhde", kw, vc)
        n_new = w_c[..., None] * n + jnp.sum(kw, axis=2)
        return (C_new, n_new, m_new), h

    carry0 = (C0.astype(jnp.float32), n0.astype(jnp.float32), m0.astype(jnp.float32))
    (C, n, m), h = lax.scan(step, carry0, (chunks(q), chunks(k), chunks(v), chunks(log_i), chunks(log_f)))
    h = jnp.moveaxis(h, 0, 2).reshape(B, H, T, Dh)
    return h, C, n, m

def mlstm_mixer(q, k, v, o, gate_pre, b_gate, C0, n0, m0):
    B, T, _ = q.shape

    def heads(a):
        return a.astype(jnp.float32).reshape(B, T, MLSTM_HEADS, MLSTM_HEAD_DIM).transpose(0, 2, 1, 3)

    qh = heads(q)
    kh = heads(k) * (MLSTM_HEAD_DIM ** -0.5)
    vh = heads(v)
    pre = gate_pre.astype(jnp.float32).reshape(B, T, N_DIR, 2, MLSTM_HEADS) + b_gate.astype(jnp.float32)
    pre = pre.transpose(0, 2, 3, 4, 1)
    log_i = pre[:, :, 0]
    log_f = jax.nn.log_sigmoid(pre[:, :, 1])
    h_f, Cf, nf, mf = mlstm_scan(qh, kh, vh, log_i[:, 0], log_f[:, 0], C0[:, 0], n0[:, 0], m0[:, 0])
    rev = lambda a: jnp.flip(a, axis=2)
    h_b, Cb, nb, mb = mlstm_scan(rev(qh), rev(kh), rev(vh), rev(log_i[:, 1]), rev(log_f[:, 1]),
                                 C0[:, 1], n0[:, 1], m0[:, 1])
    h = (h_f + rev(h_b)).transpose(0, 2, 1, 3).reshape(B, T, MLSTM_WIDTH)
    y = jax.nn.sigmoid(o.astype(jnp.float32)) * h
    return y, jnp.stack([Cf, Cb], axis=1), jnp.stack([nf, nb], axis=1), jnp.stack([mf, mb], axis=1)

def moe(h, w_router, b_router, w_expert_gu, w_expert_down, w_shared_gu, w_shared_down):
    T = h.shape[0]
    s = jax.nn.sigmoid(jnp.einsum("td,de->te", h, w_router.astype(jnp.float32)))
    biased = s + b_router.astype(jnp.float32)
    grouped = biased.reshape(T, N_EXPERT_GROUPS, N_EXPERTS // N_EXPERT_GROUPS)
    gscore = jnp.sum(lax.top_k(grouped, 2)[0], axis=-1)
    _, gidx = lax.top_k(gscore, TOPK_GROUPS)
    gmask = jnp.sum(jax.nn.one_hot(gidx, N_EXPERT_GROUPS, dtype=jnp.float32), axis=1)
    emask = jnp.repeat(gmask, N_EXPERTS // N_EXPERT_GROUPS, axis=1)
    masked = jnp.where(emask > 0, biased, -jnp.inf)
    _, eidx = lax.top_k(masked, TOP_K)
    sel = jnp.take_along_axis(s, eidx, axis=-1)
    wts = sel / jnp.sum(sel, axis=-1, keepdims=True) * ROUTED_SCALE
    combine = jnp.sum(jax.nn.one_hot(eidx, N_EXPERTS, dtype=jnp.float32) * wts[..., None], axis=1)
    gu = jnp.einsum("td,edf->tef", h, w_expert_gu)
    act = jax.nn.silu(gu[..., :EXPERT_DIM]) * gu[..., EXPERT_DIM:] * combine[..., None]
    routed = jnp.einsum("tef,efd->td", act, w_expert_down)
    gs = h @ w_shared_gu
    shared = (jax.nn.silu(gs[..., :SHARED_DIM]) * gs[..., SHARED_DIM:]) @ w_shared_down
    return routed + shared

def layer(x, mod, grid, C0, n0, m0, g_pre_mix, w_in, b_gate, w_pool, pool_scale, w_out, g_post_mix,
          g_pre_ffn, w_router, b_router, w_expert_gu, w_expert_down, w_shared_gu, w_shared_down, g_post_ffn):
    B, T, D = x.shape
    shift_a, scale_a, gate_a, shift_f, scale_f, gate_f = [mod[:, i][:, None, :] for i in range(N_MOD)]
    h = rmsnorm(x, g_pre_mix) * (1.0 + scale_a) + shift_a
    z = h @ w_in
    u = z[..., :POOL_WIDTH]
    o0 = POOL_WIDTH
    q = z[..., o0:o0 + MLSTM_WIDTH]
    k = z[..., o0 + MLSTM_WIDTH:o0 + 2 * MLSTM_WIDTH]
    v = z[..., o0 + 2 * MLSTM_WIDTH:o0 + 3 * MLSTM_WIDTH]
    o = z[..., o0 + 3 * MLSTM_WIDTH:o0 + 4 * MLSTM_WIDTH]
    gate_pre = z[..., o0 + 4 * MLSTM_WIDTH:]
    y_pool = pool_mixer(u, w_pool, pool_scale, grid)
    y_ml, C, n, m = mlstm_mixer(q, k, v, o, gate_pre, b_gate, C0, n0, m0)
    mix = jnp.concatenate([y_pool, y_ml], axis=-1) @ w_out
    x = x + gate_a * rmsnorm(mix, g_post_mix)
    h = rmsnorm(x, g_pre_ffn) * (1.0 + scale_f) + shift_f
    f = moe(h.reshape(B * T, D), w_router, b_router, w_expert_gu, w_expert_down,
            w_shared_gu, w_shared_down).reshape(B, T, D)
    x = x + gate_f * rmsnorm(f, g_post_ffn)
    return x, C, n, m

def setup_inputs(seed: int = 0) -> dict:
    key = jax.random.key(seed)
    ks = jax.random.split(key, 26)
    D = D_MODEL
    H, Dh = MLSTM_HEADS, MLSTM_HEAD_DIM

    def nrm(k, shape, s):
        return jax.random.normal(k, shape, jnp.float32) * s

    def gain(k):
        return 1.0 + nrm(k, (DEPTH, D), 0.05)

    b_i = nrm(ks[0], (DEPTH, N_DIR, 1, H), 0.1)
    b_f = 3.0 + 3.0 * jax.random.uniform(ks[1], (DEPTH, N_DIR, 1, H), jnp.float32)
    return {
        "x_prompt": nrm(ks[2], (BATCH, SEQ, D), 1.0),
        "x_sample": nrm(ks[3], (DEC_BATCH, DEC_SEQ, D), 1.0),
        "state_C": nrm(ks[4], (DEC_BATCH, DEPTH, N_DIR, H, Dh, Dh), 0.3),
        "state_n": nrm(ks[5], (DEC_BATCH, DEPTH, N_DIR, H, Dh), 0.3),
        "state_m": nrm(ks[6], (DEC_BATCH, DEPTH, N_DIR, H), 1.0),
        "c": nrm(ks[7], (DEC_BATCH, D), 1.0),
        "c_ctx": nrm(ks[8], (D,), 1.0),
        "w_ada": nrm(ks[9], (DEPTH, D, N_MOD * D), 0.5 * D ** -0.5),
        "b_ada": nrm(ks[10], (DEPTH, N_MOD * D), 0.1),
        "g_pre_mix": gain(ks[11]),
        "w_in": nrm(ks[12], (DEPTH, D, IN_COLS), D ** -0.5),
        "b_gate": jnp.concatenate([b_i, b_f], axis=2),
        "w_pool": nrm(ks[13], (DEPTH, POOL_GROUPS, POOL_GROUP_DIM, POOL_GROUP_DIM), POOL_GROUP_DIM ** -0.5),
        "pool_scale": 1.0 + nrm(ks[14], (DEPTH, POOL_WIDTH), 0.1),
        "w_out": nrm(ks[15], (DEPTH, MIX_WIDTH, D), MIX_WIDTH ** -0.5),
        "g_post_mix": gain(ks[16]),
        "g_pre_ffn": gain(ks[17]),
        "w_router": nrm(ks[18], (DEPTH, D, N_EXPERTS), D ** -0.5),
        "b_router": nrm(ks[19], (DEPTH, N_EXPERTS), 0.01),
        "w_expert_gu": nrm(ks[20], (DEPTH, N_EXPERTS, D, 2 * EXPERT_DIM), D ** -0.5),
        "w_expert_down": nrm(ks[21], (DEPTH, N_EXPERTS, EXPERT_DIM, D), EXPERT_DIM ** -0.5),
        "w_shared_gu": nrm(ks[22], (DEPTH, D, 2 * SHARED_DIM), D ** -0.5),
        "w_shared_down": nrm(ks[23], (DEPTH, SHARED_DIM, D), SHARED_DIM ** -0.5),
        "g_post_ffn": gain(ks[24]),
    }

def reference(x_prompt, x_sample, state_C, state_n, state_m, c, c_ctx, w_ada, b_ada, g_pre_mix, w_in,
              b_gate, w_pool, pool_scale, w_out, g_post_mix, g_pre_ffn, w_router, b_router, w_expert_gu,
              w_expert_down, w_shared_gu, w_shared_down, g_post_ffn):
    B_ctx = x_prompt.shape[0]
    B_lat = x_sample.shape[0]
    xp = x_prompt.astype(jnp.float32)
    xs = x_sample.astype(jnp.float32)
    zC = jnp.zeros((B_ctx, N_DIR, MLSTM_HEADS, MLSTM_HEAD_DIM, MLSTM_HEAD_DIM), jnp.float32)
    zn = jnp.zeros((B_ctx, N_DIR, MLSTM_HEADS, MLSTM_HEAD_DIM), jnp.float32)
    zm = jnp.zeros((B_ctx, N_DIR, MLSTM_HEADS), jnp.float32)
    new_C, new_n, new_m = [], [], []
    for l in range(DEPTH):
        wts = (g_pre_mix[l], w_in[l], b_gate[l], w_pool[l], pool_scale[l], w_out[l], g_post_mix[l],
               g_pre_ffn[l], w_router[l], b_router[l], w_expert_gu[l], w_expert_down[l],
               w_shared_gu[l], w_shared_down[l], g_post_ffn[l])
        mod_ctx = (jax.nn.silu(c_ctx.astype(jnp.float32)) @ w_ada[l] + b_ada[l]).reshape(1, N_MOD, D_MODEL)
        mod_lat = (jax.nn.silu(c.astype(jnp.float32)) @ w_ada[l] + b_ada[l]).reshape(B_lat, N_MOD, D_MODEL)
        xp, Cc, nc_, mc = layer(xp, mod_ctx, False, zC, zn, zm, *wts)
        new_C.append(Cc)
        new_n.append(nc_)
        new_m.append(mc)
        xs, _, _, _ = layer(xs, mod_lat, True, state_C[:, l], state_n[:, l], state_m[:, l], *wts)
    new_state_C = jnp.stack(new_C, axis=1)
    new_state_n = jnp.stack(new_n, axis=1)
    new_state_m = jnp.stack(new_m, axis=1)
    return (xp, xs, new_state_C, new_state_n, new_state_m)


_drawn_inputs = setup_inputs


def setup_inputs(seed=0):
    import zlib

    import numpy as np

    out = dict(_drawn_inputs(seed))
    spreads = {}
    factors = {'g_post_ffn': 4.048}
    for name, (base, spread) in spreads.items():
        noise = np.random.default_rng([zlib.crc32(name.encode()), seed]).standard_normal(out[name].shape)
        drawn = base * np.exp(spread * noise) if base else spread * noise
        out[name] = __import__('jax').numpy.asarray(drawn.astype(out[name].dtype))
    for name, factor in factors.items():
        out[name] = (out[name] * factor).astype(out[name].dtype)
    return out
```

```python
from contextlib import ExitStack

import numpy as np
import concourse.bass as bass
from concourse import mybir

P = 128
D = 1024
NC = D // P
T_CTX, T_LAT = 128, 256
T = T_CTX + T_LAT
NT = T // P
GRID_W = 64
WINDOWS = (2, 4, 8, 16)
H = 4
DH = 128
DV = DH + 1
MW = H * DH
NMOD = 6
NE = 64
NG = 8
TOPK = 6
TOPG = 4
F = 256
CAP = 64
EPS = 1e-6
ROUTED_SCALE = 2.5
NEG = -1e30
BIG = 1e30
FAR = 4096.0
ROUNDS = T // CAP - 1
N_OVER = (T * TOPK) // (CAP + 1) + 1
N_OVER += N_OVER % 2
N_TAB = NE + N_OVER + 2
MAIN_PAIRS = NE // 2
OVER_PAIRS = N_OVER // 2
SLOTS = 4

F32 = mybir.dt.float32
F32R = mybir.dt.float32r
I32 = mybir.dt.int32
ALU = mybir.AluOpType
ACT = mybir.ActivationFunctionType
AX = mybir.AxisListType

C_IDENT = 0
C_TRI = C_IDENT + P
C_ONES = C_TRI + P
C_MASK = C_ONES + P
C_IOTA = C_MASK + 2 * P
C_RANK = C_IOTA + NE
C_ROUND = C_RANK + 1
C_END = C_ROUND + ROUNDS


def shape_constants():
    c = np.zeros((P, C_END), np.float32)
    i = np.arange(P)
    c[:, C_IDENT:C_IDENT + P] = np.eye(P)
    c[:, C_TRI:C_TRI + P] = i[:, None] < i[None, :]
    c[:, C_ONES:C_ONES + P] = 1.0
    c[:, C_MASK:C_MASK + P] = np.where(i[:, None] > i[None, :], NEG, 0.0)
    c[:, C_MASK + P:C_MASK + 2 * P] = np.where(i[:, None] < i[None, :], NEG, 0.0)
    c[:, C_IOTA:C_IOTA + NE] = np.arange(NE)
    c[:, C_RANK] = i + 1
    c[:, C_ROUND:C_END] = CAP * np.arange(1, ROUNDS + 1) - FAR
    return c


def box(n, w):
    m = np.zeros((n, n))
    for t in range(n):
        lo, hi = max(t - w // 2, 0), min(t + w - w // 2, n)
        m[t, lo:hi] = 1.0 / (hi - lo)
    return m


def pool_constants():
    c = np.zeros((P, len(WINDOWS), T_CTX + 2 * T_LAT), np.float32)
    for g, w in enumerate(WINDOWS):
        c[:, g, 0:T_CTX] = (box(T_CTX, w) - np.eye(T_CTX)).T
        lat = (np.kron(box(T_LAT // GRID_W, w), box(GRID_W, w)) - np.eye(T_LAT)).T
        c[:, g, T_CTX:] = lat.reshape(2, P, T_LAT).transpose(1, 0, 2).reshape(P, 2 * T_LAT)
    return c.reshape(P, -1)


class Chain:

    def __init__(self, engine, semaphore, count=0):
        self.engine, self.semaphore, self.count = engine, semaphore, count

    def add(self, instruction):
        instruction.then_inc(self.semaphore, 1)
        self.count = self.count + 1

    def wait(self):
        self.engine.wait_ge(self.semaphore, self.count)

    def link(self, instruction):
        self.add(instruction)
        self.wait()


def build_layer(nc, t_in, t_out):
    with ExitStack() as ctx:
        cursor = [(nc.sbuf_base + 31) // 32 * 32]

        def at(name, shape, offset, dt=F32):
            return nc.alloc_sbuf_tensor_at(name, shape, dt, offset=offset)

        def place(name, shape, dt=F32):
            n = int(np.prod(shape[1:])) * 4
            n = (n + 31) // 32 * 32
            o = cursor[0]
            cursor[0] += n
            return nc.alloc_sbuf_tensor_at(name, shape, dt, offset=o)

        def region(nbytes):
            o = cursor[0]
            cursor[0] += nbytes
            return o

        def sem(name):
            return ctx.enter_context(nc.semaphore(name))

        w_gu = []
        w_dn = []
        for s in range(SLOTS):
            w_gu.append(place(f"w_gu{s}", [P, NC, 2 * F]))
            w_dn.append(place(f"w_dn{s}", [P, 2, D]))
        x = place("x", [P, NT, D])
        hT = place("hT", [P, NC, T])
        const = place("const", [P, C_END])
        modrow = place("modrow", [P, 12, P])
        grow = place("grow", [P, 3, 2, P])
        w_router = place("w_router", [P, NC, NE])
        b_router = place("b_router", [P, NE])
        small = place("small", [P, 40])
        table_e = place("table_e", [1, N_TAB + 2], I32)
        BC = region(24576)
        Z = region(49152)
        assert cursor[0] <= nc.sbuf_usable_end, (cursor[0], nc.sbuf_usable_end)

        ident = const[:, C_IDENT:C_IDENT + P]
        tri = const[:, C_TRI:C_TRI + P]
        ones = const[:, C_ONES:C_ONES + P]
        iota = const[:, C_IOTA:C_IOTA + NE]

        def mask(d):
            return const[:, C_MASK + d * P:C_MASK + (d + 1) * P]

        xn = at("xn", [P, NT, D], BC)
        g_in = at("g_in", [36, T], BC)
        g_lf = at("g_lf", [36, T], BC + 1536)
        g_t = at("g_t", [36, T], BC + 3072)
        g_b = at("g_b", [36, T], BC + 4608)
        g_u = at("g_u", [36, T], BC + 6144)
        g_mx = at("g_mx", [36, T], BC + 7680)
        em = [at("em0", [P, NT, P], BC), at("em1", [P, NT, P], BC + 9280)]
        nd = [at("nd0", [P, NT, DV], BC + 6144), at("nd1", [P, NT, DV], BC + 7712)]
        kw = [at("kw0", [P, DH], BC + 10816), at("kw1", [P, DH], BC + 11328)]
        wgp = at("wgp", [P, NC, 2, 36], BC + 12288)
        wgs = at("wgs", [P, NC, 16], BC + 14592)
        e_t = [at("e0", [P, 4, P], BC + 15104), at("e1", [P, 4, P], BC + 17152)]
        p_t = [at("p0", [P, 4, P], BC + 19200), at("p1", [P, 4, P], BC + 21248)]
        dT = [at("dT0", [P, T], BC + 15104), at("dT1", [P, T], BC + 17152)]
        w_pool = at("w_pool", [P, len(WINDOWS), P], BC + 21248)
        g_nat = at("g_nat", [36, 3, T], BC + 15104)
        scT = at("scT", [P, NC, 32], BC + 23296)
        bc = at("bc", [P, 6, D], BC)
        hgT = at("hgT", [P, NC, P], BC)
        y_hi = at("y_hi", [P, D], BC + 4096, F32R)
        y_lo = at("y_lo", [P, D], BC + 8192, F32R)
        sil = at("sil", [P, F], BC + 12288)
        act = at("act", [P, 2, P], BC + 13312)
        actT = at("actT", [P, 2, P], BC + 14336)
        onehot = [at("onehot0", [P, NT, P], BC + 15360, F32R), at("onehot1", [P, NT, P], BC + 16896, F32R)]
        onehotT = at("onehotT", [P, T], BC + 18432, F32R)
        posm = at("posm", [P, NT, NE], BC + 19968)
        comb = at("comb", [P, NT, NE], BC + 20736)
        cpair = at("cpair", [P, NT, 2], BC + 21504)
        wsl = at("wsl", [P, 2], BC + 21536)
        rank0 = at("rank0", [P, N_TAB], BC + 21568)

        u_tok = at("u_tok", [P, NT, MW], Z)
        hsum = at("hsum", [P, NT, MW], Z)
        o_tok = at("o_tok", [P, NT, MW], Z + 6144)
        qT = at("qT", [P, H, T], Z + 12288)
        kT = at("kT", [P, H, T], Z + 18432)
        v1 = at("v1", [P, NT, H, DV], Z + 24576)
        k_tok = at("k_tok", [P, MW], Z + 30784)
        poolm = at("poolm", [P, len(WINDOWS), T_CTX + 2 * T_LAT], Z + 32832)
        c0n = at("c0n", [P, 2 * H, DV], Z + 43072)
        gT = at("gT", [P, 3, NT, 2 * H], Z + 47200)
        emT = at("emT", [P, NT, 2 * H], Z + 47488)
        modT = at("modT", [P, 2, NC, 2], Z + 47584)
        h_hi = at("h_hi", [P, NT, NC, P], Z, F32R)
        h_lo = at("h_lo", [P, NT, NC, P], Z + 12288, F32R)
        tn = at("tn", [P, D], Z + 24576)
        hp = at("hp", [P, NC, P], Z + 28672)
        f_acc = at("f_acc", [P, NT, D], Z + 36864)
        R = Z + 32768
        s_prob = at("s_prob", [P, NT, NE], R)
        biased = at("biased", [P, NT, NE], R + 768)
        ext = at("ext", [P, NT, NE + 2], R + 1536)
        chosen = at("chosen", [P, NT, NE + 2], R + 2336)
        emask = at("emask", [P, NT, NE], R + 3136)
        top2 = at("top2", [P, NT * NG, 8], Z + 24576)
        gext = at("gext", [P, NT, NG + 4], Z + 25344)
        gout = at("gout", [P, NT, NG + 4], Z + 25536)
        best = at("best", [P, NT, 8], Z + 25728)
        flags = at("flags", [NE, ROUNDS, NE], Z + 26112)
        index = at("index", [NE, ROUNDS, NE], Z + 27392)
        match = at("match", [NE, ROUNDS, NE], Z + 28672)
        match2 = at("match2", [NE, ROUNDS, NE], Z + 29952)
        items = at("items", [NE, 8], Z + 31232)
        diag_e = at("diag_e", [NE, NE], Z + 31264)
        diag_r = at("diag_r", [NE, NE], Z + 31520)

        sum_sq = small[:, 0:3]
        rstd = small[:, 3:6]
        den = small[:, 6:9]
        rden = small[:, 9:12]
        wsum = small[:, 12:15]
        m0 = small[0:36, 15:16]
        b_gate = small[0:36, 16:18]
        pool_scale = small[:, 18:22]
        ct = small[:, 22:38].rearrange("p (m c) -> p m c", m=2)
        eps = small[:, 38:39]

        psum = ctx.enter_context(nc.psum_tensor("psum", [P, 8 * 512], F32))

        def bank(b, a=0, z=512):
            return psum[:, 512 * b + a:512 * b + z]

        x_in, ct_in, const_in = sem("x_in"), sem("ct_in"), sem("const_in")
        rows_in, gate_in, pool_in = sem("rows_in"), sem("gate_in"), sem("pool_in")
        state_in, router_in, grow2_in = sem("state_in"), sem("router_in"), sem("grow2_in")
        gu_in = [sem(f"gu_in{s}") for s in range(SLOTS)]
        dn_in = [sem(f"dn_in{s}") for s in range(SLOTS)]
        gu_used = [sem(f"gu_used{s}") for s in range(SLOTS)]
        dn_used = [sem(f"dn_used{s}") for s in range(SLOTS)]
        out_sem, m_out = sem("out_sem"), sem("m_out")
        dve_own, act_own = sem("dve_own"), sem("act_own")
        zeroed, sc_ready, sq_ready, xn_ready = sem("zeroed"), sem("sc_ready"), sem("sq_ready"), sem("xn_ready")
        xT_done, mod_ready, modT_done, modT_ready = (
            sem("xT_done"), sem("mod_ready"), sem("modT_done"), sem("modT_ready"))
        mod_a_ready, h1_act, h1_dve = sem("mod_a_ready"), sem("h1_act"), sem("h1_dve")
        wgp_ready, gates_done, gates_read, z_done, z_act, z_dve = (
            sem("wgp_ready"), sem("gates_done"), sem("gates_read"), sem("z_done"), sem("z_act"), sem("z_dve"))
        abs_ready, soft_ready, scans_ready, w_ready, nat_ready = (
            sem("abs_ready"), sem("soft_ready"), sem("scans_ready"), sem("w_ready"), sem("nat_ready"))
        gT_done, gT_ready, em_ready, ktok_done, ktok_ready = (
            sem("gT_done"), sem("gT_ready"), sem("em_ready"), sem("ktok_done"), sem("ktok_ready"))
        dT_done, dT_ready, yp_done, yp_ready = sem("dT_done"), sem("dT_ready"), sem("yp_done"), sem("yp_ready")
        st_done, nm_done, masked, e_ready, p_ready = (
            sem("st_done"), sem("nm_done"), sem("masked"), sem("e_ready"), sem("p_ready"))
        pv_done, nd_ready, unit_ready, kw_ready, c_ready = (
            sem("pv_done"), sem("nd_ready"), sem("unit_ready"), sem("kw_ready"), sem("c_ready"))
        yml_ready, mT_done, mT_ready, bc_done, bc_ready, mods_final = (
            sem("yml_ready"), sem("mT_done"), sem("mT_ready"), sem("bc_done"), sem("bc_ready"), sem("mods_final"))
        wo_done, msq, tn_ready, x1_ready, xsq, hp_ready, hi_ready, lo_ready = (
            sem("wo_done"), sem("msq"), sem("tn_ready"), sem("x1_ready"), sem("xsq"), sem("hp_ready"),
            sem("hi_ready"), sem("lo_ready"))
        h2T_done, h2T_ready = sem("h2T_done"), sem("h2T_ready")
        logit_done, prob_ready, emask_ready, pos_done, item_ready, tab_done, tab_ready = (
            sem("logit_done"), sem("prob_ready"), sem("emask_ready"), sem("pos_done"), sem("item_ready"),
            sem("tab_done"), sem("tab_ready"))
        sh_gu_done = sem("sh_gu_done")
        silu_ready, a_ready, aT_done, actT_ready = (
            sem("silu_ready"), sem("a_ready"), sem("aT_done"), sem("actT_ready"))
        f_done, f_added = sem("f_done"), sem("f_added")
        oh_ready, gathered, hg_ready, wsl_ready = sem("oh_ready"), sem("gathered"), sem("hg_ready"), sem("wsl_ready")
        wsl_done = sem("wsl_done")
        ohT_done, ohT_ready, yhi_ready, y_ready = sem("ohT_done"), sem("ohT_ready"), sem("yhi_ready"), sem("y_ready")
        grow2_ready, gf_done, fsq, y_out = sem("grow2_ready"), sem("gf_done"), sem("fsq"), sem("y_out")

        w_ada = t_in["w_ada"][0].rearrange("(p c) n -> p c n", c=NC)
        w_in = t_in["w_in"][0].rearrange("(c p) n -> p c n", p=P)
        w_out = t_in["w_out"][0].rearrange("(c p) n -> p c n", p=P)
        w_sgu = t_in["w_shared_gu"][0].rearrange("(p c) n -> p c n", c=NC)
        w_sdn = t_in["w_shared_down"][0].rearrange("(p j) n -> p j n", j=2)
        w_egu = t_in["w_expert_gu"][0].rearrange("e (p c) n -> e p c n", c=NC)
        w_edn = t_in["w_expert_down"][0].rearrange("e (p j) n -> e p j n", j=2)
        COL = {"u": 0, "q": MW, "k": 2 * MW, "v": 3 * MW, "o": 4 * MW}
        order = ["a0", "a1", "a2", "a3", "q", "a4", "a5", "k", "a6", "a7", "v", "a8", "a9", "o", "a10", "a11",
                 "u", "w0", "w1", "s"]
        chunk = {name: i for i, name in enumerate(order)}
        PRE = len(order) // SLOTS
        assert len(order) % SLOTS == 0 and chunk["s"] % SLOTS == SLOTS - 1

        def chunk_source(name):
            if name[0] == "a" and name != "a":
                i = int(name[1:])
                return w_ada[:, :, 512 * i:512 * (i + 1)]
            if name[0] == "w":
                i = int(name[1:])
                return w_out[:, :, 512 * i:512 * (i + 1)]
            if name == "s":
                return w_sgu
            return w_in[:, :, COL[name]:COL[name] + MW]

        def dn_base(s):
            return 1 if s == SLOTS - 1 else 0

        z_units = ([("q", i) for i in range(H)] + [("k", i) for i in range(H)] + [("v", i) for i in range(NT)]
                   + [("o", i) for i in range(NT)] + [("u", i) for i in range(NT)])
        by_act = [n for n, (w, _) in enumerate(z_units) if w in "qko"]
        by_dve = [n for n, (w, _) in enumerate(z_units) if w in "vu"]

        ends = {n: w for n, (w, _) in enumerate(z_units) if n + 1 == len(z_units) or z_units[n + 1][0] != w}

        def wait_chunk(engine, name):
            engine.wait_ge(gu_used[chunk[name] % SLOTS], chunk[name] // SLOTS + 1)

        def wait_unit(engine, n):
            if n in ends:
                wait_chunk(engine, ends[n])
            else:
                engine.wait_ge(z_done, n + 1 - sum(m < n for m in ends))

        SH_BANK = [2, 0, 2]
        STEPS = 7

        def natural(d, tile):
            if d == 0:
                return slice(P * tile, P * tile + P)
            first = T_CTX - 1 if tile == 0 else T - 1 - P * (tile - 1)
            last = first - P
            return slice(first, last if last >= 0 else None, -1)

        def blocks(d):
            return [(0, 0), (1, 1), (1, 2) if d == 0 else (2, 1), (2, 2)]

        def products(t, n):
            h, d = divmod(n, 2)
            row = H * d + h
            t.wait_ge(p_ready, n + 1)
            if n >= 1:
                t.wait_ge(unit_ready, n)
                t.wait_ge(c_ready, n)
            pt = p_t[n % 2]
            bl = blocks(d)
            for qs in range(NT):
                mine = [b for b in range(4) if bl[b][1] == qs]
                for b in mine:
                    t.matmul(bank(6, DV * qs, DV * (qs + 1)), pt[:, b, :], v1[:, bl[b][0], h, :],
                             start=(b == mine[0]), stop=(b == mine[-1]))
            for i in range(1, NT):
                ins = t.matmul(bank(7, DV * (i - 1), DV * i), qT[:, h, P * i:P * i + P], c0n[:, row, :],
                               start=True, stop=True)
            t.wait_ge(kw_ready, n + 1)
            t.matmul(bank(7, 2 * DV, 3 * DV), kw[n % 2][:, :], v1[:, 0, h, :], start=True, stop=True).then_inc(pv_done, 1)

        block = ctx.enter_context(nc.Block())

        @block.sync
        def _(sp):
            for i in range(NT):
                src = t_in["x_prompt"][0] if i == 0 else t_in["x_sample"][0, P * (i - 1):P * i, :]
                sp.dma_start(x[:, i, :], src).then_inc(x_in, 16)
            for i, name in enumerate(order):
                s = i % SLOTS
                if i >= SLOTS:
                    sp.wait_ge(gu_used[s], i // SLOTS)
                sp.dma_start(w_gu[s][:, :, :], chunk_source(name)).then_inc(gu_in[s], 16)
                if name == "s":
                    sp.dma_start(w_dn[s][:, :, :], w_sdn).then_inc(dn_in[s], 16)
            for e in range(SLOTS):
                sp.wait_ge(gu_used[e], PRE)
                sp.dma_start(w_gu[e][:, :, :], w_egu[e]).then_inc(gu_in[e], 16)
                if dn_base(e):
                    sp.wait_ge(dn_used[e], dn_base(e))
                sp.dma_start(w_dn[e][:, :, :], w_edn[e]).then_inc(dn_in[e], 16)
            with sp.Fori(1, NE // SLOTS) as it:
                for s in range(SLOTS):
                    sp.wait_ge(gu_used[s], it + PRE)
                    sp.dma_start(w_gu[s][:, :, :], w_egu[bass.ds(it * SLOTS + s, 1)].rearrange("e p c n -> p (e c) n"))\
                        .then_inc(gu_in[s], 16)
                    sp.wait_ge(dn_used[s], it + dn_base(s))
                    sp.dma_start(w_dn[s][:, :, :], w_edn[bass.ds(it * SLOTS + s, 1)].rearrange("e p j n -> p (e j) n"))\
                        .then_inc(dn_in[s], 16)
            sp.wait_ge(tab_ready, 1)
            n_pairs = sp.value_load(table_e[0:1, N_TAB:N_TAB + 1], min_val=0, max_val=OVER_PAIRS)
            with sp.Fori(0, OVER_PAIRS // 2) as jj:
                for q in range(2):
                    with sp.If(jj * 2 + q < n_pairs):
                        for half in range(2):
                            s = 2 * q + half
                            e = sp.value_load(table_e[0:1, bass.ds(jj * 4 + (NE + s), 1)], min_val=0, max_val=NE - 1)
                            sp.wait_ge(gu_used[s], jj + (PRE + NE // SLOTS))
                            sp.dma_start(w_gu[s][:, :, :], w_egu[bass.ds(e, 1)].rearrange("e p c n -> p (e c) n"))\
                                .then_inc(gu_in[s], 16)
                            sp.wait_ge(dn_used[s], jj + (NE // SLOTS + dn_base(s)))
                            sp.dma_start(w_dn[s][:, :, :], w_edn[bass.ds(e, 1)].rearrange("e p j n -> p (e j) n"))\
                                .then_inc(dn_in[s], 16)
                    with sp.Else():
                        sp.nop()
            for i in range(NT):
                sp.wait_ge(y_out, i + 1)
                dst = t_out[0][0] if i == 0 else t_out[1][0, P * (i - 1):P * i, :]
                sp.dma_start(dst, x[:, i, :]).then_inc(out_sem, 16)
            sp.wait_ge(out_sem, 16 * (NT + 2))
            sp.wait_ge(m_out, 32)

        @block.scalar
        def _(a):
            own = Chain(a, act_own)
            a.dma_start(const[:, :], t_in["shape_constants"]).then_inc(const_in, 16)
            a.wait_ge(zeroed, 1)
            for m, name in enumerate(("c_ctx", "c")):
                src = (t_in["c_ctx"] if m == 0 else t_in["c"][0]).rearrange("(p c) -> p c", c=NC)
                a.dma_start(ct[:, m, :], src).then_inc(ct_in, 16)
            a.wait_ge(zeroed, 2)
            ada_rows = t_in["b_ada"][0].rearrange("(i j x) -> j i x", i=12, j=4)
            for m in range(2):
                a.dma_start(modrow[m:m + 97:32, :, :], ada_rows).then_inc(rows_in, 16)
                for n, g in enumerate(("g_pre_mix", "g_post_mix", "g_pre_ffn")):
                    a.dma_start(grow[m:m + 97:32, n, :, :], t_in[g][0].rearrange("(i j x) -> j i x", i=2, j=4))\
                        .then_inc(rows_in, 16)
            with nc.allow_non_contiguous_dma(reason="a few hundred single gate and state values"):
                for d in range(2):
                    a.dma_start(b_gate[32 * d:32 * d + H, :], t_in["b_gate"][0, d].rearrange("g h -> h g"))\
                        .then_inc(gate_in, 16)
                    a.dma_start(m0[32 * d:32 * d + H, :], t_in["state_m"][0, 0, d].rearrange("(h o) -> h o", o=1))\
                        .then_inc(gate_in, 16)
            a.dma_start(wgs[:, :, :], w_in[:, :, 5 * MW:5 * MW + 16]).then_inc(gate_in, 16)
            a.wait_ge(ct_in, 32)
            a.activation(scT[:, :, 0:2], ct.rearrange("p m c -> p c m"), ACT.Silu).then_inc(sc_ready, 1)
            a.wait_ge(x_in, 16 * NT)
            for i in range(NT):
                own.add(a.activation(bank(6, 0, 1024), x[:, i, :], ACT.Square, accum_out=sum_sq[:, i:i + 1]))
                own.wait()
            a.activation(sum_sq, sum_sq, ACT.Sqrt, bias=eps, scale=1.0 / D).then_inc(sq_ready, 1)
            a.dma_start(poolm[:, :, :].rearrange("p g n -> p (g n)"), t_in["pool_constants"]).then_inc(pool_in, 16)
            a.dma_start(w_pool[:, :, :], t_in["w_pool"][0].rearrange("g c e -> c g e")).then_inc(pool_in, 16)
            a.dma_start(c0n[:, :, 0:DH], t_in["state_C"][0, 0].rearrange("d h k v -> k (d h) v")).then_inc(state_in, 16)
            with nc.allow_non_contiguous_dma(reason="a few hundred single values"):
                a.dma_start(pool_scale, t_in["pool_scale"][0].rearrange("(g e) -> e g", e=P)).then_inc(pool_in, 16)
                a.dma_start(c0n[:, :, DH:DV].rearrange("p r o -> p (r o)"),
                            t_in["state_n"][0, 0].rearrange("d h k -> k (d h)")).then_inc(state_in, 16)
            a.dma_start(w_router[:, :, :], t_in["w_router"][0].rearrange("(p c) n -> p c n", c=NC)).then_inc(router_in, 16)
            a.dma_start(b_router[:, :], t_in["b_router"][0:1, :].broadcast_to([P, NE])).then_inc(router_in, 16)

            a.wait_ge(modT_ready, 1)
            for c in range(NC // 2, NC):
                for m, (lo, hi) in enumerate(((0, T_CTX), (T_CTX, T))):
                    a.activation(hT[:, c, lo:hi], psum[:, T * c + lo:T * c + hi], ACT.Identity,
                                 bias=modT[:, 0, c, m:m + 1], scale=modT[:, 1, c, m:m + 1]).then_inc(h1_act, 1)

            def z_evac(n):
                w, i = z_units[n]
                wait_unit(a, n)
                if w == "q":
                    a.activation(qT[:, i, :], bank(2 + n % 4, 0, T), ACT.Copy).then_inc(z_act, 1)
                elif w == "k":
                    a.activation(kT[:, i, :], bank(2 + n % 4, 0, T), ACT.Copy, scale=DH ** -0.5).then_inc(z_act, 1)
                else:
                    a.activation(o_tok[:, i, :], bank(2 + n % 4), ACT.Sigmoid).then_inc(z_act, 1)

            z_evac(0)
            z_evac(1)
            a.wait_ge(abs_ready, 1)
            own.link(a.activation(g_t[:, :], g_t[:, :], ACT.Exp, scale=-1.0))
            a.activation(g_t[:, :], g_t[:, :], ACT.Ln, bias=1.0).then_inc(soft_ready, 1)
            z_evac(2)
            z_evac(3)
            a.wait_ge(scans_ready, 1)
            a.activation(g_t[:, 0:T_CTX], g_u[:, 0:T_CTX], ACT.Exp, bias=g_lf[:, T_CTX - 1:T_CTX]).then_inc(w_ready, 1)
            a.activation(g_t[:, T_CTX:T], g_lf[:, T_CTX:T], ACT.Exp, bias=m0).then_inc(w_ready, 1)
            for d in range(2):
                a.dma_start(t_out[4][0, 0, d].rearrange("(h o) -> h o", o=1),
                            g_b[32 * d:32 * d + H, T_CTX - 1:T_CTX]).then_inc(m_out, 16)
            for n in range(4, 8):
                z_evac(n)
            a.wait_ge(mod_a_ready, 1)
            for m in range(2):
                a.dma_start(grow[m:m + 97:32, 0, :, :], t_in["g_post_ffn"][0].rearrange("(i j x) -> j i x", i=2, j=4))\
                    .then_inc(grow2_in, 16)
            a.wait_ge(gT_ready, 1)
            a.activation(emT[:, :, :], gT[:, 1, :, :], ACT.Exp, scale=-1.0).then_inc(em_ready, 1)
            for n in range(11, 14):
                z_evac(n)
            a.wait_ge(ktok_done, 1)
            a.activation(k_tok[:, :], bank(0), ACT.Copy).then_inc(ktok_ready, 1)
            a.wait_ge(pool_in, 48)
            for g in range(4):
                a.wait_ge(dT_done, g + 1)
                a.activation(dT[g % 2][:, :], bank(2 + g % 2, 0, T), ACT.Copy).then_inc(dT_ready, 1)
                a.wait_ge(yp_done, g + 1)
                a.activation(hT[:, g, :], bank(4 + g % 2, 0, T), ACT.Copy, scale=pool_scale[:, g:g + 1])\
                    .then_inc(yp_ready, 1)

            def numerators(n):
                h, d = divmod(n, 2)
                row = H * d + h
                a.wait_ge(pv_done, n + 1)
                if n >= 2:
                    a.wait_ge(unit_ready, n - 1)
                a.activation(nd[n % 2][:, 0, :], bank(6, 0, DV), ACT.Copy).then_inc(nd_ready, 1)
                for i in range(1, NT):
                    a.activation(nd[n % 2][:, i, :], bank(7, DV * (i - 1), DV * i), ACT.Copy,
                                 scale=gT[:, 2, i, row:row + 1]).then_inc(nd_ready, 1)
                a.activation(c0n[:, row, :], bank(7, 2 * DV, 3 * DV), ACT.Copy).then_inc(c_ready, 1)

            for n in range(2 * H):
                h, d = divmod(n, 2)
                row = H * d + h
                if n >= 2:
                    a.wait_ge(pv_done, n - 1)
                a.activation(kw[n % 2][:, :], k_tok[:, DH * h:DH * (h + 1)], ACT.Copy,
                             scale=gT[:, 2, 0, row:row + 1]).then_inc(kw_ready, 1)
                a.wait_ge(masked, n + 1)
                if n >= 2:
                    a.wait_ge(p_ready, n - 1)
                for b, (ks, qs) in enumerate(blocks(d)):
                    src = em[d][:, qs, :] if ks == qs else bank(4 + d, P * qs, P * qs + P)
                    ins = a.activation(e_t[n % 2][:, b, :], src, ACT.Exp, bias=gT[:, 0, ks, row:row + 1])
                ins.then_inc(e_ready, 1)
                if n >= 1:
                    numerators(n - 1)
            numerators(2 * H - 1)
            a.wait_ge(c_ready, 2 * H)
            a.dma_start(t_out[2][0, 0].rearrange("d h k v -> k (d h) v"), c0n[:, :, 0:DH]).then_inc(out_sem, 16)
            with nc.allow_non_contiguous_dma(reason="a few hundred single values"):
                a.dma_start(t_out[3][0, 0].rearrange("d h k -> k (d h)"),
                            c0n[:, :, DH:DV].rearrange("p r o -> p (r o)")).then_inc(out_sem, 16)

            for i in range(NT):
                a.wait_ge(mT_done, i + 1)
                a.activation(hT[:, 4:8, P * i:P * i + P], bank(6 + i % 2).rearrange("p (h t) -> p h t", h=H), ACT.Copy)\
                    .then_inc(mT_ready, 1)

            def bc_evac(k):
                a.wait_ge(bc_done, k + 1)
                a.activation(bc[:, k, :], bank(6, 0, 1024), ACT.Copy).then_inc(bc_ready, 1)

            def norm_mix(i):
                if i < NT - 1:
                    a.wait_ge(wo_done, 2 * i + 2)
                else:
                    wait_chunk(a, "w0")
                    wait_chunk(a, "w1")
                if i:
                    a.wait_ge(x1_ready, i)
                own.link(a.activation(tn[:, :], bank(2 * i, 0, 1024), ACT.Square, accum_out=sum_sq[:, i:i + 1]))
                a.activation(sum_sq[:, i:i + 1], sum_sq[:, i:i + 1], ACT.Sqrt, bias=eps, scale=1.0 / D)\
                    .then_inc(msq, 1)
                a.wait_ge(msq, 2 * i + 2)
                a.activation(tn[:, :], bank(2 * i, 0, 1024), ACT.Copy, scale=rstd[:, i:i + 1]).then_inc(tn_ready, 1)

            def norm_x1(i):
                a.wait_ge(x1_ready, i + 1)
                if i:
                    a.wait_ge(h2T_done, i)
                    a.wait_ge(lo_ready, i)
                own.link(a.activation(hp[:, :, :].rearrange("p c q -> p (c q)"), x[:, i, :], ACT.Square,
                                      accum_out=sum_sq[:, i:i + 1]))
                a.activation(sum_sq[:, i:i + 1], sum_sq[:, i:i + 1], ACT.Sqrt, bias=eps, scale=1.0 / D)\
                    .then_inc(xsq, 1)
                a.wait_ge(hp_ready, i + 1)
                a.activation(h_hi[:, i, :, :], hp[:, :, :], ACT.Copy).then_inc(hi_ready, 1)

            def h2T_evac(i):
                a.wait_ge(h2T_done, i + 1)
                a.activation(hT[:, :, P * i:P * i + P], bank(2 * i, 0, 1024).rearrange("p (c t) -> p c t", c=NC),
                             ACT.Copy).then_inc(h2T_ready, 1)

            a.wait_ge(m_out, 32)
            bc_evac(0)
            bc_evac(1)
            bc_evac(2)
            norm_mix(0)
            bc_evac(3)
            norm_x1(0)
            bc_evac(4)
            bc_evac(5)
            norm_mix(1)
            norm_x1(1)
            norm_mix(2)
            norm_x1(2)
            for i in range(NT):
                h2T_evac(i)
            a.wait_ge(logit_done, 1)
            a.activation(s_prob[:, :, :], bank(6, 0, NT * NE).rearrange("p (i e) -> p i e", i=NT), ACT.Sigmoid)\
                .then_inc(prob_ready, 1)

            def sh_silu(i):
                if i < NT - 1:
                    a.wait_ge(sh_gu_done, i + 1)
                else:
                    wait_chunk(a, "s")
                if i:
                    a.wait_ge(a_ready, i)
                a.activation(sil[:, :], bank(SH_BANK[i], 0, F), ACT.Silu).then_inc(silu_ready, 1)

            def actT_evac(count):
                a.wait_ge(aT_done, count)
                a.activation(actT[:, :, :], bank(7, 0, F).rearrange("p (j s) -> p j s", j=2), ACT.Copy)\
                    .then_inc(actT_ready, 1)

            for i in range(NT):
                sh_silu(i)
                actT_evac(i + 1)

            def hg_evac(p):
                a.wait_ge(gathered, p + 1)
                a.activation(hgT[:, :, :].rearrange("p c s -> p (c s)"), bank(0, 0, 1024), ACT.Copy).then_inc(hg_ready, 1)

            def pair(it, q):
                p = it * 2 + q
                sb = 2 * q + 1
                a.wait_ge(gu_used[sb], it + (PRE + 1))
                a.wait_ge(a_ready, p + NT)
                a.activation(sil[:, :], bank(2, 0, F), ACT.Silu).then_inc(silu_ready, 1)
                hg_evac(p + 1)
                actT_evac(p + (NT + 1))
                a.wait_ge(dn_used[sb], it + (1 + dn_base(sb)))
                a.activation(y_hi[:, :], bank(3, 0, 1024), ACT.Copy).then_inc(yhi_ready, 1)

            hg_evac(0)
            with a.Fori(0, MAIN_PAIRS // 2) as it:
                for q in range(2):
                    pair(it, q)
            a.wait_ge(tab_ready, 1)
            n_pairs = a.value_load(table_e[0:1, N_TAB:N_TAB + 1], min_val=0, max_val=OVER_PAIRS)
            with a.Fori(0, OVER_PAIRS // 2) as jj:
                for q in range(2):
                    with a.If(jj * 2 + q < n_pairs):
                        pair(jj + MAIN_PAIRS // 2, q)
                    with a.Else():
                        a.nop()
            last = n_pairs * 6 + (6 * MAIN_PAIRS + 6)
            for i in range(NT):
                a.wait_ge(f_added, last + (2 * i + 2))
                own.link(a.activation(tn[:, :], f_acc[:, i, :], ACT.Square, accum_out=sum_sq[:, i:i + 1]))
                a.activation(sum_sq[:, i:i + 1], sum_sq[:, i:i + 1], ACT.Sqrt, bias=eps, scale=1.0 / D)\
                    .then_inc(fsq, 1)

        @block.vector
        def _(v):
            own = Chain(v, dve_own)
            own.add(v.memset(scT[:, :, :], 0.0))
            own.add(v.memset(small[:, :], 0.0))
            own.wait()
            v.memset(eps, EPS).then_inc(zeroed, 1)
            own.add(v.memset(modrow[:, :, :], 0.0))
            v.memset(grow[:, :, :, :], 0.0).then_inc(zeroed, 1)
            own.add(v.memset(wgp[:, :, :, :], 0.0))
            own.add(v.memset(v1[:, :, :, DH:DV], 1.0))
            own.wait()
            v.wait_ge(gate_in, 16 * 5)
            for d in range(2):
                for g in range(2):
                    v.tensor_copy(wgp[:, :, g, 32 * d:32 * d + H], wgs[:, :, 8 * d + 4 * g:8 * d + 4 * g + H])\
                        .then_inc(wgp_ready, 1)
            v.wait_ge(sq_ready, 1)
            own.link(v.reciprocal(rstd, sum_sq))
            for i in range(NT):
                v.tensor_scalar(xn[:, i, :], x[:, i, :], rstd[:, i:i + 1], None, ALU.mult).then_inc(xn_ready, 1)

            def ada_evac(i):
                if i == 0:
                    v.wait_ge(rows_in, 16 * 8)
                wait_chunk(v, f"a{i}")
                v.tensor_tensor(modrow[:, i, :], bank(6 + i % 2, P * (i % 4), P * (i % 4) + P), modrow[:, i, :], ALU.add)\
                    .then_inc(mod_ready, 1)

            def one_plus(i, g):
                return v.scalar_tensor_tensor(modrow[:, i:i + 2, :], modrow[:, i:i + 2, :], 1.0, grow[:, g, :, :],
                                              ALU.add, ALU.mult)

            for i in range(4):
                ada_evac(i)
            v.wait_ge(mod_ready, 4)
            one_plus(2, 0).then_inc(mod_a_ready, 1)
            v.wait_ge(modT_done, 1)
            v.tensor_copy(modT[:, :, :, :].rearrange("p a c m -> p (a c m)"), bank(6, P, P + 32)).then_inc(modT_ready, 1)
            v.wait_ge(modT_ready, 1)
            for c in range(NC // 2):
                for m, (lo, hi) in enumerate(((0, T_CTX), (T_CTX, T))):
                    v.tensor_scalar(hT[:, c, lo:hi], psum[:, T * c + lo:T * c + hi], modT[:, 1, c, m:m + 1],
                                    modT[:, 0, c, m:m + 1], ALU.mult, ALU.add).then_inc(h1_dve, 1)

            v.wait_ge(gates_done, 1)
            for b, dst in enumerate((g_in, g_lf)):
                own.add(v.tensor_scalar(dst[0:32, :], bank(b, 0, T)[0:32, :], b_gate[0:32, b:b + 1], None, ALU.add))
                for tile in range(NT):
                    ins = v.tensor_scalar(dst[32:36, P * tile:P * tile + P],
                                          bank(b, 0, T)[32:36, natural(1, tile)],
                                          b_gate[32:36, b:b + 1], None, ALU.add)
                    own.add(ins)
            own.wait()
            v.scalar_tensor_tensor(g_t[:, :], g_lf[:, :], -1.0, g_lf[:, :], ALU.mult, ALU.max).then_inc(abs_ready, 1)
            own.link(v.tensor_scalar(g_lf[:, :], g_lf[:, :], 0.0, None, ALU.min))
            v.wait_ge(soft_ready, 1)
            own.link(v.tensor_tensor(g_lf[:, :], g_lf[:, :], g_t[:, :], ALU.subtract))
            SEG = ((0, T_CTX), (T_CTX, T))
            for lo, hi in SEG:
                own.add(v.tensor_tensor_scan(g_b[:, lo:hi], g_lf[:, lo:hi], g_lf[:, lo:hi], 0.0, ALU.add, ALU.bypass))
            own.wait()
            own.link(v.tensor_tensor(g_u[:, :], g_in[:, :], g_b[:, :], ALU.subtract))
            for (lo, hi), init in zip(SEG, (0.0, m0)):
                own.add(v.tensor_tensor_scan(g_mx[:, lo:hi], g_u[:, lo:hi], g_u[:, lo:hi], init, ALU.max, ALU.max))
            own.wait()
            own.add(v.tensor_scalar(g_lf[:, :], g_mx[:, :], -1.0, None, ALU.mult))
            own.wait()
            v.tensor_tensor(g_b[:, :], g_b[:, :], g_mx[:, :], ALU.add).then_inc(scans_ready, 1)
            v.wait_ge(scans_ready, 1)
            v.wait_ge(w_ready, 2)
            for n, rows in enumerate((g_u, g_b, g_t)):
                v.tensor_copy(g_nat[0:32, n, :], rows[0:32, :]).then_inc(nat_ready, 1)
                v.tensor_copy(g_nat[32:36, n, 0:T_CTX], rows[32:36, natural(1, 0)]).then_inc(nat_ready, 1)
                v.tensor_copy(g_nat[32:36, n, T_CTX:T], rows[32:36, T - 1:T_CTX - 1:-1]).then_inc(nat_ready, 1)
            for i in range(4, 8):
                ada_evac(i)
            for n in range(8, 11):
                wait_unit(v, n)
                v.tensor_copy(v1[:, z_units[n][1], :, 0:DH], bank(2 + n % 4).rearrange("p (h e) -> p h e", h=H))\
                    .then_inc(z_dve, 1)
            v.wait_ge(gT_done, 1)
            v.tensor_copy(gT[:, :, :, :].rearrange("p a i r -> p (a i r)"), bank(1, T, T + 72)).then_inc(gT_ready, 1)
            for i in range(8, 12):
                ada_evac(i)
            v.wait_ge(mod_ready, 12)
            v.tensor_tensor(modrow[:, 4:6, :], modrow[:, 4:6, :], grow[:, 1, :, :], ALU.mult).then_inc(mods_final, 1)
            one_plus(8, 2).then_inc(mods_final, 1)
            for n in range(14, 17):
                wait_unit(v, n)
                v.tensor_copy(u_tok[:, z_units[n][1], :], bank(2 + n % 4)).then_inc(z_dve, 1)

            def outputs(n):
                h, d = divmod(n, 2)
                row = H * d + h
                t = nd[n % 2]
                v.wait_ge(nd_ready, NT * (n + 1))
                own.link(v.tensor_tensor(t[:, 1:NT, :], t[:, 1:NT, :],
                                         bank(6, DV, 3 * DV).rearrange("p (i e) -> p i e", i=2), ALU.add))
                raw = t[:, :, DH:DV].rearrange("p i o -> p (i o)")
                own.link(v.scalar_tensor_tensor(den, raw, -1.0, raw, ALU.mult, ALU.max))
                own.link(v.tensor_tensor(den, den, emT[:, :, row:row + 1].rearrange("p i o -> p (i o)"), ALU.max))
                own.link(v.reciprocal(rden, den))
                for i in range(NT):
                    dst = hsum[:, i, DH * h:DH * (h + 1)]
                    if d == 0:
                        ins = v.tensor_scalar(dst, t[:, i, 0:DH], rden[:, i:i + 1], None, ALU.mult)
                    else:
                        ins = v.scalar_tensor_tensor(dst, t[:, i, 0:DH], rden[:, i:i + 1], dst, ALU.mult, ALU.add)
                    if i < NT - 1:
                        own.add(ins)
                ins.then_inc(unit_ready, 1)
                own.wait()

            v.wait_ge(em_ready, 1)
            v.wait_ge(yp_ready, 4)
            for n in range(2 * H):
                h, d = divmod(n, 2)
                v.wait_ge(nm_done, n + 1)
                if n >= 2:
                    v.wait_ge(e_ready, n - 1)
                v.tensor_tensor(em[d][:, :, :], bank(4 + d, 0, T).rearrange("p (i t) -> p i t", i=NT),
                                mask(d).unsqueeze(1).broadcast_to([P, NT, P]), ALU.add).then_inc(masked, 1)
                if n >= 1:
                    outputs(n - 1)
                v.wait_ge(e_ready, n + 1)
                v.wait_ge(st_done, h + 1)
                if n >= 2:
                    v.wait_ge(pv_done, n - 1)
                sa, sb = 2 * (h % 2), 2 * (h % 2) + 1
                cut = 3 if d == 0 else 2
                rest = bank(sb, P * (cut - 2), 2 * P)
                own.add(v.tensor_tensor(p_t[n % 2][:, 0:cut, :], e_t[n % 2][:, 0:cut, :],
                                        bank(sa, 0, P * cut).rearrange("p (b t) -> p b t", b=cut), ALU.mult))
                v.tensor_tensor(p_t[n % 2][:, cut:4, :], e_t[n % 2][:, cut:4, :],
                                rest.rearrange("p (b t) -> p b t", b=4 - cut), ALU.mult).then_inc(p_ready, 1)
            outputs(2 * H - 1)
            v.wait_ge(unit_ready, 2 * H)
            for i in range(NT):
                v.tensor_tensor(hsum[:, i, :], hsum[:, i, :], o_tok[:, i, :], ALU.mult).then_inc(yml_ready, 1)

            def bcast(k, i):
                return bc[:, k + 3 * (i > 0), :]

            for i in range(NT):
                v.wait_ge(msq, 2 * i + 1)
                v.reciprocal(rstd[:, i:i + 1], sum_sq[:, i:i + 1]).then_inc(msq, 1)
                v.wait_ge(tn_ready, i + 1)
                v.wait_ge(bc_ready, 3 * (1 + (i > 0)))
                own.link(v.tensor_tensor(tn[:, :], tn[:, :], bcast(0, i), ALU.mult))
                v.tensor_tensor(x[:, i, :], x[:, i, :], tn[:, :], ALU.add).then_inc(x1_ready, 1)
                v.wait_ge(xsq, i + 1)
                own.link(v.reciprocal(rstd[:, i:i + 1], sum_sq[:, i:i + 1]))
                v.wait_ge(x1_ready, i + 1)
                flat = hp[:, :, :].rearrange("p c q -> p q c")
                own.link(v.scalar_tensor_tensor(flat, x[:, i, :].rearrange("p (q c) -> p q c", c=NC), rstd[:, i:i + 1],
                                                bcast(1, i).rearrange("p (q c) -> p q c", c=NC), ALU.mult, ALU.mult))
                v.tensor_tensor(flat, flat, bcast(2, i).rearrange("p (q c) -> p q c", c=NC), ALU.add).then_inc(hp_ready, 1)
                v.wait_ge(hi_ready, i + 1)
                v.tensor_tensor(h_lo[:, i, :, :], hp[:, :, :], h_hi[:, i, :, :].bitcast(F32), ALU.subtract)\
                    .then_inc(lo_ready, 1)

            v.wait_ge(prob_ready, 1)
            v.wait_ge(router_in, 32)
            own.link(v.tensor_tensor(biased[:, :, :], s_prob[:, :, :], b_router[:, :].unsqueeze(1).broadcast_to([P, NT, NE]),
                                     ALU.add))
            for i in range(NT):
                for g in range(NG):
                    own.add(v.max(top2[:, NG * i + g, :], biased[:, i, NG * g:NG * g + NG]))
            own.add(v.memset(gext[:, :, NG:NG + 4], BIG))
            own.add(v.memset(ext[:, :, NE:NE + 2], BIG))
            own.wait()
            own.link(v.tensor_tensor(gext[:, :, 0:NG], top2[:, :, 0:1].rearrange("p (i g) o -> p i (g o)", i=NT),
                                     top2[:, :, 1:2].rearrange("p (i g) o -> p i (g o)", i=NT), ALU.add))
            for i in range(NT):
                own.add(v.max(best[:, i, :], gext[:, i, 0:NG]))
            own.wait()
            own.link(v.memset(best[:, :, TOPG:8], BIG))
            for i in range(NT):
                own.add(v.match_replace(gout[:, i, :], best[:, i, :], gext[:, i, :], NEG))
            own.wait()
            gsel = gout[:, :, 0:NG]
            own.link(v.tensor_scalar(gsel, gsel, NEG, None, ALU.is_equal))
            own.link(v.tensor_scalar(gext[:, :, 0:NG], gsel, BIG, NEG, ALU.mult, ALU.add))
            for i in range(NT):
                own.add(v.tensor_tensor(ext[:, i, 0:NE].rearrange("p (g e) -> p g e", g=NG),
                                        biased[:, i, :].rearrange("p (g e) -> p g e", g=NG),
                                        gsel[:, i, :].unsqueeze(2).broadcast_to([P, NG, NE // NG]), ALU.mult))
            own.wait()
            for i in range(NT):
                own.add(v.tensor_tensor(ext[:, i, 0:NE].rearrange("p (g e) -> p g e", g=NG),
                                        ext[:, i, 0:NE].rearrange("p (g e) -> p g e", g=NG),
                                        gext[:, i, 0:NG].unsqueeze(2).broadcast_to([P, NG, NE // NG]), ALU.add))
            own.wait()
            for i in range(NT):
                own.add(v.max(best[:, i, :], ext[:, i, 0:NE]))
            own.wait()
            own.link(v.memset(best[:, :, TOPK:8], BIG))
            for i in range(NT):
                own.add(v.match_replace(chosen[:, i, :], best[:, i, :], ext[:, i, :], 3 * NEG))
            own.wait()
            v.tensor_scalar(emask[:, :, :], chosen[:, :, 0:NE], 3 * NEG, None, ALU.is_equal).then_inc(emask_ready, 1)
            v.wait_ge(emask_ready, 1)

            def sh_a(i):
                v.wait_ge(silu_ready, i + 1)
                if i:
                    v.wait_ge(aT_done, i)
                v.tensor_tensor(act[:, :, :].rearrange("s j q -> s q j"), sil[:, :].rearrange("s (q j) -> s q j", j=2),
                                bank(SH_BANK[i], F, 2 * F).rearrange("s (q j) -> s q j", j=2), ALU.mult)\
                    .then_inc(a_ready, 1)

            def f_first(i):
                if i == 0:
                    v.wait_ge(out_sem, 32)
                for n in range(2):
                    if (i, n) != (NT - 1, 1):
                        v.wait_ge(f_done, 2 * i + n + 1)
                    else:
                        v.wait_ge(dn_used[SLOTS - 1], 1)
                    v.tensor_copy(f_acc[:, i, 512 * n:512 * (n + 1)], bank(5 + n)).then_inc(f_added, 1)

            sh_a(0)
            own.link(v.tensor_tensor(comb[:, :, :], s_prob[:, :, :], emask[:, :, :], ALU.mult))
            own.link(v.tensor_reduce(wsum, comb[:, :, :], AX.X, ALU.add))
            own.link(v.reciprocal(wsum, wsum))
            for i in range(NT):
                own.add(v.tensor_scalar(comb[:, i, :], comb[:, i, :], wsum[:, i:i + 1], ROUTED_SCALE, ALU.mult, ALU.mult))
            own.wait()
            v.wait_ge(pos_done, 1)
            ranks = bank(6, NT * NE, 2 * NT * NE).rearrange("p (i e) -> p i e", i=NT)
            own.link(v.scalar_tensor_tensor(posm[:, :, :], ranks, 1.0, emask[:, :, :], ALU.add, ALU.mult))
            own.link(v.tensor_scalar(posm[:, :, :], posm[:, :, :], -1.0, None, ALU.add))
            counts = bank(6, 2 * NT * NE, 2 * NT * NE + NE)[0:NE, :]
            for r in range(ROUNDS):
                own.add(v.tensor_scalar(flags[:, r, :], counts, float(CAP * (r + 1)), None, ALU.is_gt))
            own.wait()
            fl = flags[:, :, :].rearrange("p r e -> p (r e)")
            ix = index[:, :, :].rearrange("p r e -> p (r e)")
            own.link(v.tensor_tensor_scan(ix, fl, fl, 0.0, ALU.add, ALU.bypass))
            mt = match[:, :, :].rearrange("p r e -> p (r e)")
            own.link(v.scalar_tensor_tensor(mt, ix, const[0:NE, C_RANK:C_RANK + 1], fl, ALU.is_equal, ALU.mult))
            own.link(v.tensor_tensor(match2[:, :, :], match[:, :, :],
                                     const[0:NE, C_IOTA:C_IOTA + NE].unsqueeze(1).broadcast_to([NE, ROUNDS, NE]), ALU.mult))
            own.link(v.tensor_reduce(items[:, 0:1], match2[:, :, :].rearrange("p r e -> p (r e)"), AX.X, ALU.add))
            own.link(v.tensor_tensor(match2[:, :, :], match[:, :, :],
                                     const[0:NE, C_ROUND:C_END].unsqueeze(2).broadcast_to([NE, ROUNDS, NE]), ALU.mult))
            own.link(v.tensor_reduce(items[:, 1:2], match2[:, :, :].rearrange("p r e -> p (r e)"), AX.X, ALU.add))
            own.link(v.tensor_scalar(items[:, 1:2], items[:, 1:2], FAR, None, ALU.add))
            own.add(v.tensor_scalar(diag_e[:, :], ident[0:NE, 0:NE], items[:, 0:1], None, ALU.mult))
            v.tensor_scalar(diag_r[:, :], ident[0:NE, 0:NE], items[:, 1:2], None, ALU.mult).then_inc(item_ready, 1)
            sh_a(1)
            f_first(0)
            own.add(v.tensor_copy(table_e[0:1, 0:NE], const[0:1, C_IOTA:C_IOTA + NE]))
            own.add(v.memset(rank0[:, 0:NE], 0.0))
            v.wait_ge(tab_done, 1)
            own.add(v.tensor_copy(table_e[0:1, NE:N_TAB], bank(4, 0, N_TAB - NE)[0:1, :]))
            own.add(v.tensor_copy(rank0[:, NE:N_TAB], bank(4, NE, NE + N_TAB - NE)))
            own.link(v.tensor_scalar(match[0:1, 0, 0:OVER_PAIRS], const[0:1, C_IOTA:C_IOTA + OVER_PAIRS], 2.0,
                                     index[0:1, ROUNDS - 1, NE - 1:NE], ALU.mult, ALU.is_lt))
            own.link(v.tensor_reduce(items[0:1, 2:3], match[0:1, 0, 0:OVER_PAIRS], AX.X, ALU.add))
            v.tensor_copy(table_e[0:1, N_TAB:N_TAB + 1], items[0:1, 2:3]).then_inc(tab_ready, 1)
            v.wait_ge(tab_ready, 1)
            own.wait()

            def make_onehot(p, par):
                for half in range(2):
                    item = p * 2 + half
                    e = v.value_load(table_e[0:1, bass.ds(item, 1)], min_val=0, max_val=NE - 1)
                    own.add(v.tensor_copy(cpair[:, :, half:half + 1], comb[:, :, bass.ds(e, 1)]))
                    for i in range(NT):
                        ins = v.tensor_scalar(onehot[par][:, i, CAP * half:CAP * (half + 1)], iota,
                                              rank0[:, bass.ds(item, 1)], posm[:, i, bass.ds(e, 1)], ALU.add, ALU.is_equal)
                        if (half, i) != (1, NT - 1):
                            own.add(ins)
                ins.then_inc(oh_ready, 1)

            def slot_weights(p, par):
                v.wait_ge(wsl_done, p + 1)
                for half in range(2):
                    q = slice(CAP * half, CAP * (half + 1))
                    v.tensor_copy(wsl[q, par:par + 1], bank(7, 500 + half, 501 + half)[q, :]).then_inc(wsl_ready, 1)

            make_onehot(0, 0)
            own.add(v.memset(y_hi[:, :].bitcast(F32), 0.0))
            own.wait()
            v.memset(y_lo[:, :].bitcast(F32), 0.0).then_inc(y_ready, 1)
            v.memset(onehotT[:, :].bitcast(F32), 0.0).then_inc(ohT_ready, 1)
            f_first(1)
            sh_a(2)
            f_first(2)
            slot_weights(0, 0)
            count0 = own.count
            per_pair = [0]

            def pair(it, q):
                p = it * 2 + q
                own.count = it * (2 * STEPS) + (count0 + q * STEPS)
                n0 = 0
                v.wait_ge(gathered, p + 1)
                make_onehot(p + 1, (q + 1) % 2)
                v.wait_ge(silu_ready, p + (NT + 1))
                v.wait_ge(aT_done, p + NT)
                v.wait_ge(wsl_ready, p * 2 + 2)
                v.scalar_tensor_tensor(act[:, :, :].rearrange("s j q -> s q j"), sil[:, :].rearrange("s (q j) -> s q j", j=2),
                                       wsl[:, q:q + 1], bank(2, F, 2 * F).rearrange("s (q j) -> s q j", j=2),
                                       ALU.mult, ALU.mult).then_inc(a_ready, 1)
                slot_weights(p + 1, (q + 1) % 2)
                f_add(p)
                v.wait_ge(ohT_done, p + 1)
                v.tensor_copy(onehotT[:, :], bank(2, 0, T)).then_inc(ohT_ready, 1)
                v.wait_ge(yhi_ready, p + 1)
                v.tensor_tensor(y_lo[:, :], bank(3, 0, 1024), y_hi[:, :].bitcast(F32), ALU.subtract).then_inc(y_ready, 1)

            def f_add(p):
                for c in range(6):
                    i, n = divmod(c, 2)
                    v.wait_ge(f_done, p * 6 + (5 + c + 1))
                    v.wait_ge(f_added, p * 6 + (c + 1))
                    dst = f_acc[:, i, 512 * n:512 * (n + 1)]
                    v.tensor_tensor(dst, dst, bank(5 + n), ALU.add).then_inc(f_added, 1)

            with v.Fori(0, MAIN_PAIRS // 2) as it:
                for q in range(2):
                    pair(it, q)
            n_pairs = v.value_load(table_e[0:1, N_TAB:N_TAB + 1], min_val=0, max_val=OVER_PAIRS)
            with v.Fori(0, OVER_PAIRS // 2) as jj:
                for q in range(2):
                    with v.If(jj * 2 + q < n_pairs):
                        pair(jj + MAIN_PAIRS // 2, q)
                    with v.Else():
                        v.nop()
            own.count = n_pairs * STEPS + (count0 + STEPS * MAIN_PAIRS)
            v.wait_ge(grow2_in, 32)
            v.tensor_tensor(modrow[:, 10:12, :], modrow[:, 10:12, :], grow[:, 0, :, :], ALU.mult).then_inc(grow2_ready, 1)
            f_add(n_pairs + MAIN_PAIRS)
            for i in range(NT):
                v.wait_ge(fsq, i + 1)
                own.link(v.reciprocal(rstd[:, i:i + 1], sum_sq[:, i:i + 1]))
                if i == 0:
                    v.wait_ge(gf_done, 1)
                own.link(v.scalar_tensor_tensor(f_acc[:, i, :], f_acc[:, i, :], rstd[:, i:i + 1],
                                                bank(0 if i == 0 else 2, 0, 1024), ALU.mult, ALU.mult))
                v.tensor_tensor(x[:, i, :], x[:, i, :], f_acc[:, i, :], ALU.add).then_inc(y_out, 1)

        @block.tensor
        def _(t):
            t.wait_ge(const_in, 16)
            for i in range(NT):
                t.wait_ge(xn_ready, i + 1)
                for c in range(NC):
                    ins = t.transpose(psum[:, T * c + P * i:T * c + P * i + P], xn[:, i, P * c:P * c + P], ident)
            ins.then_inc(xT_done, 1)

            def ada(i):
                n = chunk[f"a{i}"]
                s = n % SLOTS
                if i == 0:
                    t.wait_ge(sc_ready, 1)
                    t.wait_ge(sq_ready, 1)
                t.wait_ge(gu_in[s], 16 * (n // SLOTS + 1))
                if i >= 2:
                    t.wait_ge(mod_ready, i - 1)
                for c in range(NC):
                    for j in range(4):
                        ins = t.matmul(bank(6 + i % 2, P * (i % 4), P * (i % 4) + P)[32 * j:32 * j + 32, :],
                                       scT[:, c, :], w_gu[s][:, c, P * j:P * j + P],
                                       start=(c == 0), stop=(c == NC - 1), tile_position=(0, 32 * j))
                ins.then_inc(gu_used[s], 1)

            for i in range(4):
                ada(i)
            t.wait_ge(mod_a_ready, 1)
            for i in range(4):
                ins = t.matmul(bank(6, P + 8 * i, P + 8 * i + 8), modrow[:, i, :],
                               ident.rearrange("p (j r) -> p j r", j=4)[:, :, 0:2], start=True, stop=True)
            ins.then_inc(modT_done, 1)

            t.wait_ge(wgp_ready, 4)
            t.wait_ge(h1_act, NC)
            t.wait_ge(h1_dve, NC)
            for g in range(2):
                for c in range(NC):
                    ins = t.matmul(bank(g, 0, T)[0:36, :], wgp[:, c, g, :], hT[:, c, :], start=(c == 0), stop=(c == NC - 1))
            ins.then_inc(gates_done, 1)

            def z_unit(n):
                w, i = z_units[n]
                k = chunk[w]
                s = k % SLOTS
                t.wait_ge(gu_in[s], 16 * (k // SLOTS + 1))
                if n >= 4:
                    if n - 4 in by_act:
                        t.wait_ge(z_act, by_act.index(n - 4) + 1)
                    else:
                        t.wait_ge(z_dve, by_dve.index(n - 4) + 1)
                for c in range(NC):
                    if w in "qk":
                        ins = t.matmul(bank(2 + n % 4, 0, T), w_gu[s][:, c, DH * i:DH * (i + 1)], hT[:, c, :],
                                       start=(c == 0), stop=(c == NC - 1))
                    else:
                        ins = t.matmul(bank(2 + n % 4), hT[:, c, P * i:P * (i + 1)], w_gu[s][:, c, :],
                                       start=(c == 0), stop=(c == NC - 1))
                ins.then_inc(gu_used[s] if n in ends else z_done, 1)

            for n in range(len(z_units)):
                z_unit(n)
                if n == 3:
                    ada(4)
                    ada(5)
                if n == 7:
                    ada(6)
                    ada(7)
                if n == 10:
                    t.wait_ge(w_ready, 2)
                    t.wait_ge(nat_ready, 9)
                    for a_ in range(3):
                        for tile in range(NT):
                            col = T + 24 * a_ + 8 * tile
                            ins = t.matmul(bank(1, col, col + 2 * H), g_nat[:, a_, P * tile:P * tile + P],
                                           ident[0:36, 0:64].rearrange("p (d r) -> p d r", d=2)[:, :, 0:H],
                                           start=True, stop=True)
                    ins.then_inc(gT_done, 1)
                    ada(8)
                    ada(9)
                if n == 13:
                    ada(10)
                    ada(11)
            t.wait_ge(z_act, 8)
            t.wait_ge(abs_ready, 1)
            for h in range(H):
                ins = t.transpose(bank(0, DH * h, DH * (h + 1)), kT[:, h, 0:P], ident)
            ins.then_inc(ktok_done, 1)
            t.wait_ge(pool_in, 48)
            t.wait_ge(z_act, 11)
            t.wait_ge(z_dve, 6)
            for g in range(4):
                if g >= 2:
                    t.wait_ge(dT_ready, g - 1)
                cols = slice(P * g, P * g + P)
                b = bank(2 + g % 2, 0, T)
                t.matmul(b[:, 0:T_CTX], u_tok[:, 0, cols], poolm[:, g, 0:T_CTX], start=True, stop=True)
                for k in range(2):
                    ins = t.matmul(b[:, T_CTX:T], u_tok[:, 1 + k, cols],
                                   poolm[:, g, T_CTX + T_LAT * k:T_CTX + T_LAT * (k + 1)], start=(k == 0), stop=(k == 1))
                ins.then_inc(dT_done, 1)
                t.wait_ge(dT_ready, g + 1)
                if g >= 2:
                    t.wait_ge(yp_ready, g - 1)
                t.matmul(bank(4 + g % 2, 0, T), w_pool[:, g, :], dT[g % 2][:, :], start=True, stop=True).then_inc(yp_done, 1)

            t.wait_ge(state_in, 32)
            t.wait_ge(yp_ready, 4)
            t.wait_ge(ktok_ready, 1)
            t.wait_ge(mod_ready, 12)
            for n in range(2 * H):
                h, d = divmod(n, 2)
                row = H * d + h
                if d == 0:
                    if h >= 2:
                        t.wait_ge(p_ready, 2 * (h - 1))
                    sa, sb = 2 * (h % 2), 2 * (h % 2) + 1
                    t.matmul(bank(sa, 0, P), kT[:, h, 0:P], qT[:, h, 0:P], start=True, stop=True)
                    t.matmul(bank(sa, P, 3 * P), kT[:, h, P:2 * P], qT[:, h, P:T], start=True, stop=True)
                    t.matmul(bank(sb, 0, 2 * P), kT[:, h, 2 * P:T], qT[:, h, P:T], start=True, stop=True)\
                        .then_inc(st_done, 1)
                if n >= 2:
                    t.wait_ge(e_ready, n - 1)
                q = slice(32 * d, 32 * d + H)
                for tile in range(NT):
                    ins = t.matmul(bank(4 + d, P * tile, P * tile + P),
                                   const[q, C_IDENT + 32 * d + h:C_IDENT + 32 * d + h + 1].broadcast_to([H, P]),
                                   g_lf[q, natural(d, tile)], start=True, stop=True)
                ins.then_inc(nm_done, 1)
                if n >= 1:
                    products(t, n - 1)
            products(t, 2 * H - 1)

            for i in range(NT):
                t.wait_ge(yml_ready, i + 1)
                if i == 0:
                    t.wait_ge(unit_ready, 2 * H)
                    t.wait_ge(c_ready, 2 * H)
                if i == 2:
                    t.wait_ge(mT_ready, 1)
                for h in range(H):
                    ins = t.transpose(bank(6 + i % 2, P * h, P * h + P), hsum[:, i, DH * h:DH * (h + 1)], ident)
                ins.then_inc(mT_done, 1)

            BC_ROWS = ((4, 0), (8, 0), (6, 0), (4, 1), (8, 1), (6, 1))

            def rows_over_partitions(first, m, b):
                for k in range(2):
                    for j in range(4):
                        row = 32 * j + m
                        ins = t.matmul(bank(b + k, P * j, P * j + P), ident[:, row:row + 1].broadcast_to([P, P]),
                                       modrow[:, first + k, :], start=True, stop=True)
                return ins

            t.wait_ge(mods_final, 2)
            t.wait_ge(mT_ready, NT)
            for k in range(6):
                if k:
                    t.wait_ge(bc_ready, k)
                first, m = BC_ROWS[k]
                rows_over_partitions(first, m, 6).then_inc(bc_done, 1)
                i, n = divmod(k, 2)
                s = chunk[f"w{n}"] % SLOTS
                t.wait_ge(gu_in[s], 16 * (chunk[f"w{n}"] // SLOTS + 1))
                for c in range(NC):
                    ins = t.matmul(bank(2 * i + n), hT[:, c, P * i:P * i + P], w_gu[s][:, c, :],
                                   start=(c == 0), stop=(c == NC - 1))
                ins.then_inc(wo_done if i < NT - 1 else gu_used[s], 1)

            for i in range(NT):
                t.wait_ge(hp_ready, i + 1)
                for c in range(NC):
                    ins = t.transpose(bank(2 * i, P * c, P * c + P), hp[:, c, :], ident)
                ins.then_inc(h2T_done, 1)
            t.wait_ge(router_in, 32)
            t.wait_ge(h2T_ready, NT)
            t.wait_ge(bc_ready, 6)
            for i in range(NT):
                for c in range(NC):
                    ins = t.matmul(bank(6, NE * i, NE * (i + 1)), hT[:, c, P * i:P * i + P], w_router[:, c, :],
                                   start=(c == 0), stop=(c == NC - 1))
            ins.then_inc(logit_done, 1)

            s_sh = SLOTS - 1

            def sh_gu(i):
                t.wait_ge(gu_in[s_sh], 16 * PRE)
                if i == 2:
                    t.wait_ge(a_ready, 1)
                for c in range(NC):
                    ins = t.matmul(bank(SH_BANK[i]), hT[:, c, P * i:P * i + P], w_gu[s_sh][:, c, :],
                                   start=(c == 0), stop=(c == NC - 1))
                ins.then_inc(sh_gu_done if i < NT - 1 else gu_used[s_sh], 1)

            def transposes(count):
                t.wait_ge(a_ready, count)
                for j in range(2):
                    ins = t.transpose(bank(7, P * j, P * j + P), act[:, j, :], ident)
                ins.then_inc(aT_done, 1)

            def sh_down(i):
                t.wait_ge(actT_ready, i + 1)
                t.wait_ge(dn_in[s_sh], 16)
                for n in range(2):
                    if i:
                        t.wait_ge(f_added, 2 * (i - 1) + n + 1)
                    for j in range(2):
                        ins = t.matmul(bank(5 + n), actT[:, j, :], w_dn[s_sh][:, j, 512 * n:512 * (n + 1)],
                                       start=(j == 0), stop=(j == 1))
                    ins.then_inc(f_done if (i, n) != (NT - 1, 1) else dn_used[s_sh], 1)

            sh_gu(0)
            sh_gu(1)
            transposes(1)
            t.wait_ge(emask_ready, 1)
            for i in range(NT):
                for k in range(i + 1):
                    t.matmul(bank(6, NT * NE + NE * i, NT * NE + NE * (i + 1)), tri if k == i else ones, emask[:, k, :],
                             start=(k == 0), stop=(k == i))
            for k in range(NT):
                ins = t.matmul(bank(6, 2 * NT * NE, 2 * NT * NE + NE), ones, emask[:, k, :], start=(k == 0), stop=(k == 2))
            ins.then_inc(pos_done, 1)
            sh_gu(2)
            t.wait_ge(item_ready, 1)
            t.matmul(bank(4, 0, NE), ones[0:NE, :], diag_e[:, :], start=True, stop=True)
            t.matmul(bank(4, NE, 2 * NE), ones[0:NE, :], diag_r[:, :], start=True, stop=True).then_inc(tab_done, 1)
            sh_down(0)
            transposes(2)
            sh_down(1)
            transposes(3)
            sh_down(2)

            def gather(p, par):
                for i in range(NT):
                    ins = t.matmul(bank(7, 500, 502), onehot[par][:, i, :].bitcast(F32), cpair[:, i, :],
                                   start=(i == 0), stop=(i == NT - 1))
                ins.then_inc(wsl_done, 1)
                for c in range(NC):
                    for i in range(NT):
                        for part in (h_hi, h_lo):
                            ins = t.matmul(bank(0, P * c, P * c + P), part[:, i, c, :], onehot[par][:, i, :],
                                           start=(i == 0 and part is h_hi), stop=(i == NT - 1 and part is h_lo))
                ins.then_inc(gathered, 1)

            def combine(p):
                for c in range(6):
                    i, n = divmod(c, 2)
                    t.wait_ge(f_added, p * 6 + (c + 5))
                    for part in (y_hi, y_lo):
                        ins = t.matmul(bank(5 + n), onehotT[:, P * i:P * i + P], part[:, 512 * n:512 * (n + 1)],
                                       start=(part is y_hi), stop=(part is y_lo))
                    ins.then_inc(f_done, 1)

            def pair(it, q):
                p = it * 2 + q
                slots = (2 * q, 2 * q + 1)
                t.wait_ge(hg_ready, p + 1)
                t.wait_ge(a_ready, p + NT)
                t.wait_ge(ohT_ready, p + 1)
                for s in slots:
                    t.wait_ge(gu_in[s], it * 16 + 16 * (PRE + 1))
                for c in range(NC):
                    for half, s in enumerate(slots):
                        rows = slice(CAP * half, CAP * (half + 1))
                        ins = t.matmul(bank(2)[rows, :], hgT[:, c, rows], w_gu[s][:, c, :],
                                       start=(c == 0), stop=(c == NC - 1), tile_position=(0, CAP * half))
                        if c == NC - 1:
                            ins.then_inc(gu_used[s], 1)
                t.wait_ge(oh_ready, p + 2)
                t.wait_ge(wsl_ready, p * 2 + 2)
                gather(p + 1, (q + 1) % 2)
                t.wait_ge(wsl_ready, p * 2 + 4)
                transposes(p + (NT + 1))
                t.wait_ge(y_ready, p + 1)
                combine(p)
                for i in range(NT):
                    ins = t.transpose(bank(2, P * i, P * i + P), onehot[q][:, i, :].bitcast(F32), ident)
                ins.then_inc(ohT_done, 1)
                t.wait_ge(actT_ready, p + (NT + 1))
                for s in slots:
                    t.wait_ge(dn_in[s], it * 16 + 16 * (1 + dn_base(s)))
                for n in range(2):
                    for j in range(2):
                        for half, s in enumerate(slots):
                            rows = slice(CAP * half, CAP * (half + 1))
                            ins = t.matmul(bank(3 + n)[rows, :], actT[:, j, rows], w_dn[s][:, j, 512 * n:512 * (n + 1)],
                                           start=(j == 0), stop=(j == 1), tile_position=(0, CAP * half))
                            if n == 1 and j == 1:
                                ins.then_inc(dn_used[s], 1)

            t.wait_ge(hi_ready, NT)
            t.wait_ge(lo_ready, NT)
            t.wait_ge(oh_ready, 1)
            t.wait_ge(a_ready, 2)
            gather(0, 0)
            with t.Fori(0, MAIN_PAIRS // 2) as it:
                for q in range(2):
                    pair(it, q)
            t.wait_ge(tab_ready, 1)
            n_pairs = t.value_load(table_e[0:1, N_TAB:N_TAB + 1], min_val=0, max_val=OVER_PAIRS)
            with t.Fori(0, OVER_PAIRS // 2) as jj:
                for q in range(2):
                    with t.If(jj * 2 + q < n_pairs):
                        pair(jj + MAIN_PAIRS // 2, q)
                    with t.Else():
                        t.nop()
            t.wait_ge(grow2_ready, 1)
            t.wait_ge(hg_ready, n_pairs + (MAIN_PAIRS + 1))
            t.wait_ge(y_ready, n_pairs + (MAIN_PAIRS + 1))
            t.wait_ge(ohT_ready, n_pairs + (MAIN_PAIRS + 1))
            rows_over_partitions(10, 0, 0)
            rows_over_partitions(10, 1, 2).then_inc(gf_done, 1)
            combine(n_pairs + MAIN_PAIRS)



_INS = ["x_prompt", "x_sample", "state_C", "state_n", "state_m", "c", "c_ctx", "w_ada", "b_ada", "g_pre_mix", "w_in",
        "b_gate", "w_pool", "pool_scale", "w_out", "g_post_mix", "g_pre_ffn", "w_router", "b_router", "w_expert_gu",
        "w_expert_down", "w_shared_gu", "w_shared_down", "g_post_ffn"]
_OUTS = [(1, T_CTX, D), (1, T_LAT, D), (1, 1, 2, H, DH, DH), (1, 1, 2, H, DH), (1, 1, 2, H)]


def kernel(**inputs):
    import concourse.bacc as _bacc
    from concourse.bass_utils import run_bass_kernel_spmd as _run

    nc = _bacc.Bacc("TRN2", target_bir_lowering=False, num_devices=1)
    arrays, t_in = {}, {}
    for name in _INS:
        arrays[f"in_{name}"] = np.ascontiguousarray(inputs[name])
    arrays["in_shape_constants"] = shape_constants()
    arrays["in_pool_constants"] = pool_constants()
    for key, a in arrays.items():
        t_in[key[3:]] = nc.dram_tensor(key, a.shape, mybir.dt.from_np(a.dtype), kind="ExternalInput").ap()
    t_out = [nc.dram_tensor(f"out_{i}", shape, F32, kind="ExternalOutput").ap() for i, shape in enumerate(_OUTS)]
    build_layer(nc, t_in, t_out)
    r = _run(nc, [arrays], core_ids=[0])
    return tuple(r.results[0][f"out_{i}"] for i in range(len(_OUTS)))
```

```python
from contextlib import ExitStack

import numpy as np
import concourse.bass as bass
from concourse import mybir

P = 128
D = 1024
NC = D // P
T_CTX, T_LAT = 128, 256
T = T_CTX + T_LAT
NT = T // P
GRID_W = 64
WINDOWS = (2, 4, 8, 16)
H = 4
DH = 128
DV = DH + 1
MW = H * DH
NMOD = 6
NE = 64
NG = 8
TOPK = 6
TOPG = 4
F = 256
CAP = 64
EPS = 1e-6
ROUTED_SCALE = 2.5
NEG = -1e30
BIG = 1e30
FAR = 4096.0
ROUNDS = T // CAP - 1
N_OVER = (T * TOPK) // (CAP + 1) + 1
N_OVER += N_OVER % 2
N_TAB = NE + N_OVER + 2
MAIN_PAIRS = NE // 2
OVER_PAIRS = N_OVER // 2
SLOTS = 4

F32 = mybir.dt.float32
F32R = mybir.dt.float32r
I32 = mybir.dt.int32
ALU = mybir.AluOpType
ACT = mybir.ActivationFunctionType
AX = mybir.AxisListType

C_IDENT = 0
C_TRI = C_IDENT + P
C_ONES = C_TRI + P
C_MASK = C_ONES + P
C_IOTA = C_MASK + 2 * P
C_RANK = C_IOTA + NE
C_ROUND = C_RANK + 1
C_END = C_ROUND + ROUNDS


def shape_constants():
    c = np.zeros((P, C_END), np.float32)
    i = np.arange(P)
    c[:, C_IDENT:C_IDENT + P] = np.eye(P)
    c[:, C_TRI:C_TRI + P] = i[:, None] < i[None, :]
    c[:, C_ONES:C_ONES + P] = 1.0
    c[:, C_MASK:C_MASK + P] = np.where(i[:, None] > i[None, :], NEG, 0.0)
    c[:, C_MASK + P:C_MASK + 2 * P] = np.where(i[:, None] < i[None, :], NEG, 0.0)
    c[:, C_IOTA:C_IOTA + NE] = np.arange(NE)
    c[:, C_RANK] = i + 1
    c[:, C_ROUND:C_END] = CAP * np.arange(1, ROUNDS + 1) - FAR
    return c


def box(n, w):
    m = np.zeros((n, n))
    for t in range(n):
        lo, hi = max(t - w // 2, 0), min(t + w - w // 2, n)
        m[t, lo:hi] = 1.0 / (hi - lo)
    return m


def pool_constants():
    c = np.zeros((P, len(WINDOWS), T_CTX + 2 * T_LAT), np.float32)
    for g, w in enumerate(WINDOWS):
        c[:, g, 0:T_CTX] = (box(T_CTX, w) - np.eye(T_CTX)).T
        lat = (np.kron(box(T_LAT // GRID_W, w), box(GRID_W, w)) - np.eye(T_LAT)).T
        c[:, g, T_CTX:] = lat.reshape(2, P, T_LAT).transpose(1, 0, 2).reshape(P, 2 * T_LAT)
    return c.reshape(P, -1)


class Chain:

    def __init__(self, engine, semaphore, count=0):
        self.engine, self.semaphore, self.count = engine, semaphore, count

    def add(self, instruction):
        instruction.then_inc(self.semaphore, 1)
        self.count = self.count + 1

    def wait(self):
        self.engine.wait_ge(self.semaphore, self.count)

    def link(self, instruction):
        self.add(instruction)
        self.wait()


def build_layer(nc, t_in, t_out):
    with ExitStack() as ctx:
        cursor = [(nc.sbuf_base + 31) // 32 * 32]

        def at(name, shape, offset, dt=F32):
            return nc.alloc_sbuf_tensor_at(name, shape, dt, offset=offset)

        def place(name, shape, dt=F32):
            n = int(np.prod(shape[1:])) * 4
            n = (n + 31) // 32 * 32
            o = cursor[0]
            cursor[0] += n
            return nc.alloc_sbuf_tensor_at(name, shape, dt, offset=o)

        def region(nbytes):
            o = cursor[0]
            cursor[0] += nbytes
            return o

        def sem(name):
            return ctx.enter_context(nc.semaphore(name))

        w_gu = []
        w_dn = []
        for s in range(SLOTS):
            w_gu.append(place(f"w_gu{s}", [P, NC, 2 * F]))
            w_dn.append(place(f"w_dn{s}", [P, 2, D]))
        x = place("x", [P, NT, D])
        hT = place("hT", [P, NC, T])
        const = place("const", [P, C_END])
        modrow = place("modrow", [P, 12, P])
        grow = place("grow", [P, 3, 2, P])
        w_router = place("w_router", [P, NC, NE])
        b_router = place("b_router", [P, NE])
        small = place("small", [P, 48])
        scT = place("scT", [P, NC, 32])
        table_e = place("table_e", [1, N_TAB + 2], I32)
        BC = region(24576)
        Z = region(49152)
        assert cursor[0] <= nc.sbuf_usable_end, (cursor[0], nc.sbuf_usable_end)

        ident = const[:, C_IDENT:C_IDENT + P]
        tri = const[:, C_TRI:C_TRI + P]
        ones = const[:, C_ONES:C_ONES + P]
        iota = const[:, C_IOTA:C_IOTA + NE]

        def mask(d):
            return const[:, C_MASK + d * P:C_MASK + (d + 1) * P]

        xn = at("xn", [P, NT, D], BC)
        g_in = at("g_in", [36, T], BC)
        g_lf = at("g_lf", [36, T], BC + 1536)
        g_t = at("g_t", [36, T], BC + 3072)
        g_b = at("g_b", [36, T], BC + 4608)
        g_u = at("g_u", [36, T], BC + 6144)
        g_mx = at("g_mx", [36, T], BC + 7680)
        em = [at("em0", [P, NT, P], BC), at("em1", [P, NT, P], BC + 9280)]
        nd = [at("nd0", [P, NT, DV], BC + 6144), at("nd1", [P, NT, DV], BC + 7712)]
        kw = [at("kw0", [P, DH], BC + 10816), at("kw1", [P, DH], BC + 11328)]
        wgp = at("wgp", [P, NC, 2, 36], BC + 12288)
        wgs = at("wgs", [P, NC, 16], BC + 14592)
        e_t = [at("e0", [P, 4, P], BC + 15104), at("e1", [P, 4, P], BC + 17152)]
        p_t = [at("p0", [P, 4, P], BC + 19200), at("p1", [P, 4, P], BC + 21248)]
        dT = [at("dT0", [P, T], BC + 15104), at("dT1", [P, T], BC + 17152)]
        w_pool = at("w_pool", [P, len(WINDOWS), P], BC + 21248)
        g_nat = at("g_nat", [36, 3, T], BC + 15104)
        bc = at("bc", [P, 6, D], BC)
        hgT = at("hgT", [P, NC, P], BC)
        y_hi = at("y_hi", [P, D], BC + 4096, F32R)
        y_lo = at("y_lo", [P, D], BC + 8192, F32R)
        sil = at("sil", [P, F], BC + 12288)
        act = at("act", [P, 2, P], BC + 13312)
        actT = at("actT", [P, 2, P], BC + 14336)
        onehot = [at("onehot0", [P, NT, P], BC + 15360, F32R), at("onehot1", [P, NT, P], BC + 16896, F32R)]
        onehotT = at("onehotT", [P, T], BC + 18432, F32R)
        posm = at("posm", [P, NT, NE], BC + 19968)
        comb = at("comb", [P, NT, NE], BC + 20736)
        comb2 = at("comb2", [P, NT, NE, 2], BC + 21984, F32R)
        cpair = at("cpair", [P, NT, 4], BC + 23520, F32R)
        wsl = at("wsl", [P, 2], BC + 21536)
        rank0 = at("rank0", [P, N_TAB], BC + 21568)

        u_tok = at("u_tok", [P, NT, MW], Z)
        hsum = at("hsum", [P, NT, MW], Z)
        o_tok = at("o_tok", [P, NT, MW], Z + 6144)
        qT = at("qT", [P, H, T], Z + 12288)
        kT = at("kT", [P, H, T], Z + 18432)
        v1 = at("v1", [P, NT, H, DV], Z + 24576)
        k_tok = at("k_tok", [P, MW], Z + 30784)
        poolm = at("poolm", [P, len(WINDOWS), T_CTX + 2 * T_LAT], Z + 32832)
        c0n = at("c0n", [P, 2 * H, DV], Z + 43072)
        gT = at("gT", [P, 3, NT, 2 * H], Z + 47200)
        emT = at("emT", [P, NT, 2 * H], Z + 47488)
        modT = at("modT", [P, 2, NC, 2], Z + 47584)
        h_hi = at("h_hi", [P, NT, NC, P], Z, F32R)
        h_lo = at("h_lo", [P, NT, NC, P], Z + 12288, F32R)
        junk = at("junk", [P, D], Z + 36864)
        tn = at("tn", [P, D], Z + 24576)
        hp = at("hp", [P, NC, P], Z + 28672)
        hg = at("hg", [P, 2, 512], Z + 32768)
        f_acc = at("f_acc", [P, NT, D], Z + 36864)
        R = Z + 32768
        s_prob = at("s_prob", [P, NT, NE], R)
        biased = at("biased", [P, NT, NE], R + 768)
        ext = at("ext", [P, NT, NE + 2], R + 1536)
        chosen = at("chosen", [P, NT, NE + 2], R + 2336)
        emask = at("emask", [P, NT, NE], R + 3136)
        top2 = at("top2", [P, NT * NG, 8], Z + 24576)
        gext = at("gext", [P, NT, NG + 4], Z + 25344)
        gout = at("gout", [P, NT, NG + 4], Z + 25536)
        best = at("best", [P, NT, 8], Z + 25728)
        flags = at("flags", [NE, ROUNDS, NE], Z + 26112)
        index = at("index", [NE, ROUNDS, NE], Z + 27392)
        match = at("match", [NE, ROUNDS, NE], Z + 28672)
        match2 = at("match2", [NE, ROUNDS, NE], Z + 29952)
        items = at("items", [NE, 8], Z + 31232)
        diag_e = at("diag_e", [NE, NE], Z + 31264)
        diag_r = at("diag_r", [NE, NE], Z + 31520)

        sum_sq = small[:, 0:3]
        rstd = small[:, 3:6]
        den = small[:, 6:9]
        rden = small[:, 9:12]
        wsum = small[:, 12:15]
        m0 = small[0:36, 15:16]
        b_gate = small[0:36, 16:18]
        pool_scale = small[:, 18:22]
        ct = small[:, 22:38].rearrange("p (m c) -> p m c", m=2)
        eps = small[:, 38:39]
        sum_sq2 = small[:, 40:43]
        rstd2 = small[:, 43:46]

        psum = ctx.enter_context(nc.psum_tensor("psum", [P, 8 * 512], F32))

        def bank(b, a=0, z=512):
            return psum[:, 512 * b + a:512 * b + z]

        x_in, ct_in, const_in = sem("x_in"), sem("ct_in"), sem("const_in")
        rows_in, gate_in, pool_in = sem("rows_in"), sem("gate_in"), sem("pool_in")
        state_in, router_in, grow2_in = sem("state_in"), sem("router_in"), sem("grow2_in")
        gu_in = [sem(f"gu_in{s}") for s in range(SLOTS)]
        dn_in = [sem(f"dn_in{s}") for s in range(SLOTS)]
        gu_used = [sem(f"gu_used{s}") for s in range(SLOTS)]
        dn_used = [sem(f"dn_used{s}") for s in range(SLOTS)]
        out_sem, m_out = sem("out_sem"), sem("m_out")
        dve_own, act_own = sem("dve_own"), sem("act_own")
        zeroed, sc_ready, sq_ready, xn_ready = sem("zeroed"), sem("sc_ready"), sem("sq_ready"), sem("xn_ready")
        xT_done, mod_ready, modT_done, modT_ready = (
            sem("xT_done"), sem("mod_ready"), sem("modT_done"), sem("modT_ready"))
        mod_a_ready, h1_act, h1_dve = sem("mod_a_ready"), sem("h1_act"), sem("h1_dve")
        wgp_ready, gates_done, gates_read, z_done, z_act, z_dve = (
            sem("wgp_ready"), sem("gates_done"), sem("gates_read"), sem("z_done"), sem("z_act"), sem("z_dve"))
        abs_ready, soft_ready, scans_ready, w_ready, nat_ready = (
            sem("abs_ready"), sem("soft_ready"), sem("scans_ready"), sem("w_ready"), sem("nat_ready"))
        gT_done, gT_ready, em_ready, ktok_done, ktok_ready = (
            sem("gT_done"), sem("gT_ready"), sem("em_ready"), sem("ktok_done"), sem("ktok_ready"))
        dT_done, dT_ready, yp_done, yp_ready = sem("dT_done"), sem("dT_ready"), sem("yp_done"), sem("yp_ready")
        st_done, nm_done, masked, e_ready, p_ready = (
            sem("st_done"), sem("nm_done"), sem("masked"), sem("e_ready"), sem("p_ready"))
        pv_read = sem("pv_read")
        pv_done, nd_ready, unit_ready, kw_ready, c_ready = (
            sem("pv_done"), sem("nd_ready"), sem("unit_ready"), sem("kw_ready"), sem("c_ready"))
        yml_ready, mT_done, mT_ready, bc_done, bc_ready, mods_final = (
            sem("yml_ready"), sem("mT_done"), sem("mT_ready"), sem("bc_done"), sem("bc_ready"), sem("mods_final"))
        wo_done, msq, tn_ready, x1_ready, xsq, hp_ready, hi_ready, lo_ready = (
            sem("wo_done"), sem("msq"), sem("tn_ready"), sem("x1_ready"), sem("xsq"), sem("hp_ready"),
            sem("hi_ready"), sem("lo_ready"))
        h2T_done, h2T_ready = sem("h2T_done"), sem("h2T_ready")
        logit_done, prob_ready, emask_ready, pos_done, item_ready, tab_done, tab_ready = (
            sem("logit_done"), sem("prob_ready"), sem("emask_ready"), sem("pos_done"), sem("item_ready"),
            sem("tab_done"), sem("tab_ready"))
        sh_gu_done = sem("sh_gu_done")
        silu_ready, a_ready, aT_done, actT_ready = (
            sem("silu_ready"), sem("a_ready"), sem("aT_done"), sem("actT_ready"))
        f_done, f_added = sem("f_done"), sem("f_added")
        oh_ready, gathered, hg_ready, wsl_ready = sem("oh_ready"), sem("gathered"), sem("hg_ready"), sem("wsl_ready")
        wsl_done, hgT_done, hgT_ready = sem("wsl_done"), sem("hgT_done"), sem("hgT_ready")
        ohT_done, ohT_ready, yhi_ready, y_ready = sem("ohT_done"), sem("ohT_ready"), sem("yhi_ready"), sem("y_ready")
        grow2_ready, gf_done, fsq, y_out = sem("grow2_ready"), sem("gf_done"), sem("fsq"), sem("y_out")

        w_ada = t_in["w_ada"][0].rearrange("(p c) n -> p c n", c=NC)
        w_in = t_in["w_in"][0].rearrange("(c p) n -> p c n", p=P)
        w_out = t_in["w_out"][0].rearrange("(c p) n -> p c n", p=P)
        w_sgu = t_in["w_shared_gu"][0].rearrange("(p c) n -> p c n", c=NC)
        w_sdn = t_in["w_shared_down"][0].rearrange("(p j) n -> p j n", j=2)
        w_egu = t_in["w_expert_gu"][0].rearrange("e (p c) n -> e p c n", c=NC)
        w_edn = t_in["w_expert_down"][0].rearrange("e (p j) n -> e p j n", j=2)
        COL = {"u": 0, "q": MW, "k": 2 * MW, "v": 3 * MW, "o": 4 * MW}
        order = ["a0", "a1", "a2", "a3", "q", "a4", "a5", "k", "a6", "a7", "v", "a8", "a9", "o", "u",
                 "w0", "w1", "a10", "a11", "s"]
        chunk = {name: i for i, name in enumerate(order)}
        PRE = len(order) // SLOTS
        assert len(order) % SLOTS == 0 and chunk["s"] % SLOTS == SLOTS - 1

        def chunk_source(name):
            if name[0] == "a" and name != "a":
                i = int(name[1:])
                return w_ada[:, :, 512 * i:512 * (i + 1)]
            if name[0] == "w":
                i = int(name[1:])
                return w_out[:, :, 512 * i:512 * (i + 1)]
            if name == "s":
                return w_sgu
            return w_in[:, :, COL[name]:COL[name] + MW]

        def dn_base(s):
            return 1 if s == SLOTS - 1 else 0

        z_units = ([("q", i) for i in range(H)] + [("k", i) for i in range(H)] + [("v", i) for i in range(NT)]
                   + [("o", i) for i in range(NT)] + [("u", i) for i in range(NT)])
        by_act = [n for n, (w, _) in enumerate(z_units) if w in "qko"]
        by_dve = [n for n, (w, _) in enumerate(z_units) if w in "vu"]

        ends = {n: w for n, (w, _) in enumerate(z_units) if n + 1 == len(z_units) or z_units[n + 1][0] != w}

        def wait_chunk(engine, name):
            engine.wait_ge(gu_used[chunk[name] % SLOTS], chunk[name] // SLOTS + 1)

        def wait_unit(engine, n):
            if n in ends:
                wait_chunk(engine, ends[n])
            else:
                engine.wait_ge(z_done, n + 1 - sum(m < n for m in ends))

        SH_BANK = [0, 2, 4]
        STEPS = 7

        def natural(d, tile):
            if d == 0:
                return slice(P * tile, P * tile + P)
            first = T_CTX - 1 if tile == 0 else T - 1 - P * (tile - 1)
            last = first - P
            return slice(first, last if last >= 0 else None, -1)

        def blocks(d):
            return [(0, 0), (1, 1), (1, 2) if d == 0 else (2, 1), (2, 2)]

        def products(t, n):
            h, d = divmod(n, 2)
            row = H * d + h
            t.wait_ge(p_ready, n + 1)
            if n >= 1:
                t.wait_ge(pv_read, n)
            pt = p_t[n % 2]
            bl = blocks(d)
            for qs in range(NT):
                mine = [b for b in range(4) if bl[b][1] == qs]
                for b in mine:
                    t.matmul(bank(6, DV * qs, DV * (qs + 1)), pt[:, b, :], v1[:, bl[b][0], h, :],
                             start=(b == mine[0]), stop=(b == mine[-1]))
            if n >= 1:
                t.wait_ge(c_ready, n)
            for i in range(1, NT):
                ins = t.matmul(bank(7, DV * (i - 1), DV * i), qT[:, h, P * i:P * i + P], c0n[:, row, :],
                               start=True, stop=True)
            t.wait_ge(kw_ready, n + 1)
            t.matmul(bank(7, 2 * DV, 3 * DV), kw[n % 2][:, :], v1[:, 0, h, :], start=True, stop=True).then_inc(pv_done, 1)

        block = ctx.enter_context(nc.Block())

        @block.sync
        def _(sp):
            for i in range(NT):
                src = t_in["x_prompt"][0] if i == 0 else t_in["x_sample"][0, P * (i - 1):P * i, :]
                sp.dma_start(x[:, i, :], src).then_inc(x_in, 16)
            for i, name in enumerate(order):
                s = i % SLOTS
                if i >= SLOTS:
                    sp.wait_ge(gu_used[s], i // SLOTS)
                sp.dma_start(w_gu[s][:, :, :], chunk_source(name)).then_inc(gu_in[s], 16)
                if name == "s":
                    sp.dma_start(w_dn[s][:, :, :], w_sdn).then_inc(dn_in[s], 16)
            for e in range(SLOTS):
                sp.wait_ge(gu_used[e], PRE)
                sp.dma_start(w_gu[e][:, :, :], w_egu[e]).then_inc(gu_in[e], 16)
                if dn_base(e):
                    sp.wait_ge(dn_used[e], dn_base(e))
                sp.dma_start(w_dn[e][:, :, :], w_edn[e]).then_inc(dn_in[e], 16)
            with sp.Fori(1, NE // SLOTS) as it:
                for s in range(SLOTS):
                    sp.wait_ge(gu_used[s], it + PRE)
                    sp.dma_start(w_gu[s][:, :, :], w_egu[bass.ds(it * SLOTS + s, 1)].rearrange("e p c n -> p (e c) n"))\
                        .then_inc(gu_in[s], 16)
                    sp.wait_ge(dn_used[s], it + dn_base(s))
                    sp.dma_start(w_dn[s][:, :, :], w_edn[bass.ds(it * SLOTS + s, 1)].rearrange("e p j n -> p (e j) n"))\
                        .then_inc(dn_in[s], 16)
            sp.wait_ge(tab_ready, 1)
            n_pairs = sp.value_load(table_e[0:1, N_TAB:N_TAB + 1], min_val=0, max_val=OVER_PAIRS)

            def over_pair(jj, q):
                for half in range(2):
                    s = 2 * q + half
                    e = sp.value_load(table_e[0:1, bass.ds(jj * 4 + (NE + s), 1)], min_val=0, max_val=NE - 1)
                    sp.wait_ge(gu_used[s], jj + (PRE + NE // SLOTS))
                    sp.dma_start(w_gu[s][:, :, :], w_egu[bass.ds(e, 1)].rearrange("e p c n -> p (e c) n"))\
                        .then_inc(gu_in[s], 16)
                    sp.wait_ge(dn_used[s], jj + (NE // SLOTS + dn_base(s)))
                    sp.dma_start(w_dn[s][:, :, :], w_edn[bass.ds(e, 1)].rearrange("e p j n -> p (e j) n"))\
                        .then_inc(dn_in[s], 16)

            with sp.If(n_pairs > 0):
                over_pair(0, 0)
            with sp.Else():
                sp.nop()
            with sp.If(n_pairs > 1):
                over_pair(0, 1)
                with sp.Fori(1, OVER_PAIRS // 2) as jj:
                    for q in range(2):
                        with sp.If(jj * 2 + q < n_pairs):
                            over_pair(jj, q)
                        with sp.Else():
                            sp.nop()
            with sp.Else():
                sp.nop()
            for i in range(NT):
                sp.wait_ge(y_out, i + 1)
                dst = t_out[0][0] if i == 0 else t_out[1][0, P * (i - 1):P * i, :]
                sp.dma_start(dst, x[:, i, :]).then_inc(out_sem, 16)
            sp.wait_ge(out_sem, 16 * (NT + 2))
            sp.wait_ge(m_out, 32)

        @block.scalar
        def _(a):
            own = Chain(a, act_own)
            a.wait_ge(zeroed, 1)
            for m, name in enumerate(("c_ctx", "c")):
                src = (t_in["c_ctx"] if m == 0 else t_in["c"][0]).rearrange("(p c) -> p c", c=NC)
                a.dma_start(ct[:, m, :], src).then_inc(ct_in, 16)
            a.dma_start(const[:, :], t_in["shape_constants"]).then_inc(const_in, 16)
            a.dma_start(wgs[:, :, :], w_in[:, :, 5 * MW:5 * MW + 16]).then_inc(gate_in, 16)
            a.wait_ge(zeroed, 2)
            ada_rows = t_in["b_ada"][0].rearrange("(i j x) -> j i x", i=12, j=4)
            for m in range(2):
                a.dma_start(modrow[m:m + 97:32, :, :], ada_rows).then_inc(rows_in, 16)
                for n, g in enumerate(("g_pre_mix", "g_post_mix", "g_pre_ffn")):
                    a.dma_start(grow[m:m + 97:32, n, :, :], t_in[g][0].rearrange("(i j x) -> j i x", i=2, j=4))\
                        .then_inc(rows_in, 16)
            with nc.allow_non_contiguous_dma(reason="a few hundred single gate and state values"):
                for d in range(2):
                    a.dma_start(b_gate[32 * d:32 * d + H, :], t_in["b_gate"][0, d].rearrange("g h -> h g"))\
                        .then_inc(gate_in, 16)
                    a.dma_start(m0[32 * d:32 * d + H, :], t_in["state_m"][0, 0, d].rearrange("(h o) -> h o", o=1))\
                        .then_inc(gate_in, 16)
            a.wait_ge(ct_in, 32)
            a.activation(scT[:, :, 0:2], ct.rearrange("p m c -> p c m"), ACT.Silu).then_inc(sc_ready, 1)
            a.wait_ge(x_in, 16 * NT)
            for i in range(NT):
                own.link(a.activation(hT[:, 0:4, 0:D // 4], x[:, i, :].rearrange("p (a b) -> p a b", a=4), ACT.Square,
                                      accum_out=sum_sq[:, i:i + 1]))
            a.activation(sum_sq, sum_sq, ACT.Sqrt, bias=eps, scale=1.0 / D).then_inc(sq_ready, 1)
            a.dma_start(poolm[:, :, :].rearrange("p g n -> p (g n)"), t_in["pool_constants"]).then_inc(pool_in, 16)
            a.dma_start(w_pool[:, :, :], t_in["w_pool"][0].rearrange("g c e -> c g e")).then_inc(pool_in, 16)
            a.dma_start(c0n[:, :, 0:DH], t_in["state_C"][0, 0].rearrange("d h k v -> k (d h) v")).then_inc(state_in, 16)
            with nc.allow_non_contiguous_dma(reason="a few hundred single values"):
                a.dma_start(pool_scale, t_in["pool_scale"][0].rearrange("(g e) -> e g", e=P)).then_inc(pool_in, 16)
                a.dma_start(c0n[:, :, DH:DV].rearrange("p r o -> p (r o)"),
                            t_in["state_n"][0, 0].rearrange("d h k -> k (d h)")).then_inc(state_in, 16)
            a.dma_start(w_router[:, :, :], t_in["w_router"][0].rearrange("(p c) n -> p c n", c=NC)).then_inc(router_in, 16)
            a.dma_start(b_router[:, :], t_in["b_router"][0:1, :].broadcast_to([P, NE])).then_inc(router_in, 16)

            a.wait_ge(modT_ready, 1)
            for c in range(NC // 2, NC):
                for m, (lo, hi) in enumerate(((0, T_CTX), (T_CTX, T))):
                    a.activation(hT[:, c, lo:hi], psum[:, T * c + lo:T * c + hi], ACT.Identity,
                                 bias=modT[:, 0, c, m:m + 1], scale=modT[:, 1, c, m:m + 1]).then_inc(h1_act, 1)

            def z_evac(n):
                w, i = z_units[n]
                wait_unit(a, n)
                if w == "q":
                    a.activation(qT[:, i, :], bank(2 + n % 4, 0, T), ACT.Copy).then_inc(z_act, 1)
                elif w == "k":
                    a.activation(kT[:, i, :], bank(2 + n % 4, 0, T), ACT.Copy, scale=DH ** -0.5).then_inc(z_act, 1)
                else:
                    a.activation(o_tok[:, i, :], bank(2 + n % 4), ACT.Sigmoid).then_inc(z_act, 1)

            z_evac(0)
            z_evac(1)
            a.wait_ge(abs_ready, 1)
            own.link(a.activation(g_t[:, :], g_t[:, :], ACT.Exp, scale=-1.0))
            a.activation(g_t[:, :], g_t[:, :], ACT.Ln, bias=1.0).then_inc(soft_ready, 1)
            z_evac(2)
            z_evac(3)
            a.wait_ge(scans_ready, 1)
            a.activation(g_t[:, 0:T_CTX], g_u[:, 0:T_CTX], ACT.Exp, bias=g_lf[:, T_CTX - 1:T_CTX]).then_inc(w_ready, 1)
            a.activation(g_t[:, T_CTX:T], g_lf[:, T_CTX:T], ACT.Exp, bias=m0).then_inc(w_ready, 1)
            for d in range(2):
                a.dma_start(t_out[4][0, 0, d].rearrange("(h o) -> h o", o=1),
                            g_b[32 * d:32 * d + H, T_CTX - 1:T_CTX]).then_inc(m_out, 16)
            for n in range(4, 8):
                z_evac(n)
            a.wait_ge(mod_a_ready, 1)
            for m in range(2):
                a.dma_start(grow[m:m + 97:32, 0, :, :], t_in["g_post_ffn"][0].rearrange("(i j x) -> j i x", i=2, j=4))\
                    .then_inc(grow2_in, 16)
            a.wait_ge(gT_ready, 1)
            a.activation(emT[:, :, :], gT[:, 1, :, :], ACT.Exp, scale=-1.0).then_inc(em_ready, 1)
            for n in range(11, 14):
                z_evac(n)
            a.wait_ge(ktok_done, 1)
            a.activation(k_tok[:, :], bank(0), ACT.Copy).then_inc(ktok_ready, 1)
            a.wait_ge(pool_in, 48)
            for g in range(4):
                a.wait_ge(dT_done, g + 1)
                a.activation(dT[g % 2][:, :], bank(2 + g % 2, 0, T), ACT.Copy).then_inc(dT_ready, 1)
                a.wait_ge(yp_done, g + 1)
                a.activation(hT[:, g, :], bank(4 + g % 2, 0, T), ACT.Copy, scale=pool_scale[:, g:g + 1])\
                    .then_inc(yp_ready, 1)

            def numerators(n):
                h, d = divmod(n, 2)
                row = H * d + h
                a.wait_ge(pv_done, n + 1)
                if n >= 2:
                    a.wait_ge(unit_ready, n - 1)
                a.activation(nd[n % 2][:, 0, :], bank(6, 0, DV), ACT.Copy).then_inc(nd_ready, 1)
                for i in range(1, NT):
                    a.activation(nd[n % 2][:, i, :], bank(7, DV * (i - 1), DV * i), ACT.Copy,
                                 scale=gT[:, 2, i, row:row + 1]).then_inc(nd_ready, 1)
                a.activation(c0n[:, row, :], bank(7, 2 * DV, 3 * DV), ACT.Copy).then_inc(c_ready, 1)

            def exponentials(n):
                h, d = divmod(n, 2)
                row = H * d + h
                if n >= 2:
                    a.wait_ge(pv_done, n - 1)
                a.activation(kw[n % 2][:, :], k_tok[:, DH * h:DH * (h + 1)], ACT.Copy,
                             scale=gT[:, 2, 0, row:row + 1]).then_inc(kw_ready, 1)
                a.wait_ge(masked, n + 1)
                if n >= 2:
                    a.wait_ge(p_ready, n - 1)
                for b, (ks, qs) in enumerate(blocks(d)):
                    src = em[d][:, qs, :] if ks == qs else bank(4 + d, P * qs, P * qs + P)
                    ins = a.activation(e_t[n % 2][:, b, :], src, ACT.Exp, bias=gT[:, 0, ks, row:row + 1])
                ins.then_inc(e_ready, 1)

            exponentials(0)
            exponentials(1)
            for n in range(2 * H):
                numerators(n)
                if n + 2 < 2 * H:
                    exponentials(n + 2)
            a.wait_ge(c_ready, 2 * H)
            a.dma_start(t_out[2][0, 0].rearrange("d h k v -> k (d h) v"), c0n[:, :, 0:DH]).then_inc(out_sem, 16)
            with nc.allow_non_contiguous_dma(reason="a few hundred single values"):
                a.dma_start(t_out[3][0, 0].rearrange("d h k -> k (d h)"),
                            c0n[:, :, DH:DV].rearrange("p r o -> p (r o)")).then_inc(out_sem, 16)

            for i in range(NT):
                a.wait_ge(mT_done, i + 1)
                a.activation(hT[:, 4:8, P * i:P * i + P], bank(6 + i % 2).rearrange("p (h t) -> p h t", h=H), ACT.Copy)\
                    .then_inc(mT_ready, 1)

            def bc_evac(k):
                a.wait_ge(bc_done, k + 1)
                a.activation(bc[:, k, :], bank(6, 0, 1024), ACT.Copy).then_inc(bc_ready, 1)

            def norm_mix(i):
                if i < NT - 1:
                    a.wait_ge(wo_done, 2 * i + 2)
                else:
                    wait_chunk(a, "w0")
                    wait_chunk(a, "w1")
                own.link(a.activation(junk[:, :], bank(2 * i, 0, 1024), ACT.Square, accum_out=sum_sq[:, i:i + 1]))
                a.activation(sum_sq[:, i:i + 1], sum_sq[:, i:i + 1], ACT.Sqrt, bias=eps, scale=1.0 / D)\
                    .then_inc(msq, 1)

            def norm_x1(i):
                a.wait_ge(x1_ready, i + 1)
                own.link(a.activation(junk[:, :], x[:, i, :], ACT.Square, accum_out=sum_sq2[:, i:i + 1]))
                a.activation(sum_sq2[:, i:i + 1], sum_sq2[:, i:i + 1], ACT.Sqrt, bias=eps, scale=1.0 / D)\
                    .then_inc(xsq, 1)

            def high_part(i):
                a.wait_ge(hp_ready, i + 1)
                a.activation(h_hi[:, i, :, :], hp[:, :, :], ACT.Copy).then_inc(hi_ready, 1)

            def h2T_evac(i):
                a.wait_ge(h2T_done, i + 1)
                a.activation(hT[:, :, P * i:P * i + P], bank(2 * i, 0, 1024).rearrange("p (c t) -> p c t", c=NC),
                             ACT.Copy).then_inc(h2T_ready, 1)

            def sh_silu(i):
                if i < NT - 1:
                    a.wait_ge(sh_gu_done, i + 1)
                else:
                    wait_chunk(a, "s")
                if i:
                    a.wait_ge(a_ready, i)
                a.activation(sil[:, :], bank(SH_BANK[i], 0, F), ACT.Silu).then_inc(silu_ready, 1)

            a.wait_ge(m_out, 32)
            for k in range(3):
                bc_evac(k)
            norm_mix(0)
            bc_evac(3)
            norm_x1(0)
            bc_evac(4)
            norm_mix(1)
            bc_evac(5)
            high_part(0)
            h2T_evac(0)
            norm_x1(1)
            norm_mix(2)
            high_part(1)
            h2T_evac(1)
            norm_x1(2)
            sh_silu(0)
            high_part(2)
            h2T_evac(2)
            a.wait_ge(logit_done, 1)
            a.activation(s_prob[:, :, :], bank(6, 0, NT * NE).rearrange("p (i e) -> p i e", i=NT), ACT.Sigmoid)\
                .then_inc(prob_ready, 1)

            def actT_evac(count):
                a.wait_ge(aT_done, count)
                a.activation(actT[:, :, :], bank(7, 0, F).rearrange("p (j s) -> p j s", j=2), ACT.Copy)\
                    .then_inc(actT_ready, 1)

            for i in range(NT):
                if i:
                    sh_silu(i)
                actT_evac(i + 1)

            def hg_evac(p):
                for n in range(2):
                    a.wait_ge(gathered, p * 2 + (n + 1))
                    a.activation(hg[:, n, :], bank(n), ACT.Copy).then_inc(hg_ready, 1)

            def hgT_evac(p):
                for n in range(2):
                    a.wait_ge(hgT_done, p * 2 + (n + 1))
                    a.activation(hgT[:, 4 * n:4 * n + 4, :].rearrange("p c s -> p (c s)"), bank(n), ACT.Copy)\
                        .then_inc(hgT_ready, 1)

            def pair(it, q):
                p = it * 2 + q
                sb = 2 * q + 1
                a.wait_ge(gu_used[sb], it + (PRE + 1))
                a.wait_ge(a_ready, p + NT)
                a.activation(sil[:, :], bank(2, 0, F), ACT.Silu).then_inc(silu_ready, 1)
                hg_evac(p + 1)
                actT_evac(p + (NT + 1))
                hgT_evac(p + 1)
                a.wait_ge(dn_used[sb], it + (1 + dn_base(sb)))
                a.activation(y_hi[:, :], bank(3, 0, 1024), ACT.Copy).then_inc(yhi_ready, 1)

            hg_evac(0)
            hgT_evac(0)
            with a.Fori(0, MAIN_PAIRS // 2) as it:
                for q in range(2):
                    pair(it, q)
            a.wait_ge(tab_ready, 1)
            n_pairs = a.value_load(table_e[0:1, N_TAB:N_TAB + 1], min_val=0, max_val=OVER_PAIRS)
            with a.If(n_pairs > 0):
                pair(MAIN_PAIRS // 2, 0)
            with a.Else():
                a.nop()
            with a.If(n_pairs > 1):
                pair(MAIN_PAIRS // 2, 1)
                with a.Fori(1, OVER_PAIRS // 2) as jj:
                    for q in range(2):
                        with a.If(jj * 2 + q < n_pairs):
                            pair(jj + MAIN_PAIRS // 2, q)
                        with a.Else():
                            a.nop()
            with a.Else():
                a.nop()
            last = n_pairs * 6 + (6 * MAIN_PAIRS + 6)
            for i in range(NT):
                a.wait_ge(f_added, last + (2 * i + 2))
                own.link(a.activation(tn[:, :], f_acc[:, i, :], ACT.Square, accum_out=sum_sq[:, i:i + 1]))
                a.activation(sum_sq[:, i:i + 1], sum_sq[:, i:i + 1], ACT.Sqrt, bias=eps, scale=1.0 / D)\
                    .then_inc(fsq, 1)

        @block.vector
        def _(v):
            own = Chain(v, dve_own)
            own.add(v.memset(scT[:, :, :], 0.0))
            own.add(v.memset(small[:, :], 0.0))
            own.wait()
            v.memset(eps, EPS).then_inc(zeroed, 1)
            own.add(v.memset(modrow[:, :, :], 0.0))
            v.memset(grow[:, :, :, :], 0.0).then_inc(zeroed, 1)
            own.add(v.memset(wgp[:, :, :, :], 0.0))
            own.add(v.memset(v1[:, :, :, DH:DV], 1.0))
            own.wait()
            v.wait_ge(sq_ready, 1)
            own.link(v.reciprocal(rstd, sum_sq))
            for i in range(NT):
                v.tensor_scalar(xn[:, i, :], x[:, i, :], rstd[:, i:i + 1], None, ALU.mult).then_inc(xn_ready, 1)

            def ada_evac(i):
                if i == 0:
                    v.wait_ge(rows_in, 16 * 8)
                wait_chunk(v, f"a{i}")
                v.tensor_tensor(modrow[:, i, :], bank(6 + i % 2, P * (i % 4), P * (i % 4) + P), modrow[:, i, :], ALU.add)\
                    .then_inc(mod_ready, 1)

            def one_plus(i, g):
                return v.scalar_tensor_tensor(modrow[:, i:i + 2, :], modrow[:, i:i + 2, :], 1.0, grow[:, g, :, :],
                                              ALU.add, ALU.mult)

            for i in range(4):
                ada_evac(i)
            v.wait_ge(mod_ready, 4)
            one_plus(2, 0).then_inc(mod_a_ready, 1)
            v.wait_ge(gate_in, 16 * 5)
            for d in range(2):
                for g in range(2):
                    v.tensor_copy(wgp[:, :, g, 32 * d:32 * d + H], wgs[:, :, 8 * d + 4 * g:8 * d + 4 * g + H])\
                        .then_inc(wgp_ready, 1)
            v.wait_ge(modT_done, 1)
            v.tensor_copy(modT[:, :, :, :].rearrange("p a c m -> p (a c m)"), bank(6, P, P + 32)).then_inc(modT_ready, 1)
            v.wait_ge(modT_ready, 1)
            for c in range(NC // 2):
                for m, (lo, hi) in enumerate(((0, T_CTX), (T_CTX, T))):
                    v.tensor_scalar(hT[:, c, lo:hi], psum[:, T * c + lo:T * c + hi], modT[:, 1, c, m:m + 1],
                                    modT[:, 0, c, m:m + 1], ALU.mult, ALU.add).then_inc(h1_dve, 1)

            v.wait_ge(gates_done, 1)
            for b, dst in enumerate((g_in, g_lf)):
                own.add(v.tensor_scalar(dst[0:32, :], bank(b, 0, T)[0:32, :], b_gate[0:32, b:b + 1], None, ALU.add))
                for tile in range(NT):
                    ins = v.tensor_scalar(dst[32:36, P * tile:P * tile + P],
                                          bank(b, 0, T)[32:36, natural(1, tile)],
                                          b_gate[32:36, b:b + 1], None, ALU.add)
                    own.add(ins)
            own.wait()
            v.scalar_tensor_tensor(g_t[:, :], g_lf[:, :], -1.0, g_lf[:, :], ALU.mult, ALU.max).then_inc(abs_ready, 1)
            own.link(v.tensor_scalar(g_lf[:, :], g_lf[:, :], 0.0, None, ALU.min))
            v.wait_ge(soft_ready, 1)
            own.link(v.tensor_tensor(g_lf[:, :], g_lf[:, :], g_t[:, :], ALU.subtract))
            SEG = ((0, T_CTX), (T_CTX, T))
            for lo, hi in SEG:
                own.add(v.tensor_tensor_scan(g_b[:, lo:hi], g_lf[:, lo:hi], g_lf[:, lo:hi], 0.0, ALU.add, ALU.bypass))
            own.wait()
            own.link(v.tensor_tensor(g_u[:, :], g_in[:, :], g_b[:, :], ALU.subtract))
            for (lo, hi), init in zip(SEG, (0.0, m0)):
                own.add(v.tensor_tensor_scan(g_mx[:, lo:hi], g_u[:, lo:hi], g_u[:, lo:hi], init, ALU.max, ALU.max))
            own.wait()
            own.add(v.tensor_scalar(g_lf[:, :], g_mx[:, :], -1.0, None, ALU.mult))
            own.wait()
            v.tensor_tensor(g_b[:, :], g_b[:, :], g_mx[:, :], ALU.add).then_inc(scans_ready, 1)
            v.wait_ge(scans_ready, 1)
            v.wait_ge(w_ready, 2)
            for n, rows in enumerate((g_u, g_b, g_t)):
                v.tensor_copy(g_nat[0:32, n, :], rows[0:32, :]).then_inc(nat_ready, 1)
                v.tensor_copy(g_nat[32:36, n, 0:T_CTX], rows[32:36, natural(1, 0)]).then_inc(nat_ready, 1)
                v.tensor_copy(g_nat[32:36, n, T_CTX:T], rows[32:36, T - 1:T_CTX - 1:-1]).then_inc(nat_ready, 1)
            for i in range(4, 8):
                ada_evac(i)
            for n in range(8, 11):
                wait_unit(v, n)
                v.tensor_copy(v1[:, z_units[n][1], :, 0:DH], bank(2 + n % 4).rearrange("p (h e) -> p h e", h=H))\
                    .then_inc(z_dve, 1)
            v.wait_ge(gT_done, 1)
            v.tensor_copy(gT[:, :, :, :].rearrange("p a i r -> p (a i r)"), bank(1, T, T + 72)).then_inc(gT_ready, 1)
            for i in range(8, 10):
                ada_evac(i)
            v.wait_ge(mod_ready, 10)
            v.tensor_tensor(modrow[:, 4:6, :], modrow[:, 4:6, :], grow[:, 1, :, :], ALU.mult).then_inc(mods_final, 1)
            one_plus(8, 2).then_inc(mods_final, 1)
            for n in range(14, 17):
                wait_unit(v, n)
                v.tensor_copy(u_tok[:, z_units[n][1], :], bank(2 + n % 4)).then_inc(z_dve, 1)

            def outputs(n):
                h, d = divmod(n, 2)
                row = H * d + h
                t = nd[n % 2]
                v.wait_ge(nd_ready, NT * (n + 1))
                v.tensor_tensor(t[:, 1:NT, :], t[:, 1:NT, :],
                                bank(6, DV, 3 * DV).rearrange("p (i e) -> p i e", i=2), ALU.add).then_inc(pv_read, 1)
                v.wait_ge(pv_read, n + 1)
                raw = t[:, :, DH:DV].rearrange("p i o -> p (i o)")
                own.link(v.scalar_tensor_tensor(den, raw, -1.0, raw, ALU.mult, ALU.max))
                own.link(v.tensor_tensor(den, den, emT[:, :, row:row + 1].rearrange("p i o -> p (i o)"), ALU.max))
                own.link(v.reciprocal(rden, den))
                for i in range(NT):
                    dst = hsum[:, i, DH * h:DH * (h + 1)]
                    if d == 0:
                        ins = v.tensor_scalar(dst, t[:, i, 0:DH], rden[:, i:i + 1], None, ALU.mult)
                    else:
                        ins = v.scalar_tensor_tensor(dst, t[:, i, 0:DH], rden[:, i:i + 1], dst, ALU.mult, ALU.add)
                    if i < NT - 1:
                        own.add(ins)
                ins.then_inc(unit_ready, 1)
                own.wait()

            v.wait_ge(em_ready, 1)
            v.wait_ge(yp_ready, 4)
            def masked_maxima(n):
                d = n % 2
                v.wait_ge(nm_done, n + 1)
                if n >= 2:
                    v.wait_ge(e_ready, n - 1)
                v.tensor_tensor(em[d][:, :, :], bank(4 + d, 0, T).rearrange("p (i t) -> p i t", i=NT),
                                mask(d).unsqueeze(1).broadcast_to([P, NT, P]), ALU.add).then_inc(masked, 1)

            def probabilities(n):
                h, d = divmod(n, 2)
                v.wait_ge(e_ready, n + 1)
                v.wait_ge(st_done, h + 1)
                if n >= 2:
                    v.wait_ge(pv_done, n - 1)
                sa, sb = 2 * (h % 2), 2 * (h % 2) + 1
                cut = 3 if d == 0 else 2
                rest = bank(sb, P * (cut - 2), 2 * P)
                own.add(v.tensor_tensor(p_t[n % 2][:, 0:cut, :], e_t[n % 2][:, 0:cut, :],
                                        bank(sa, 0, P * cut).rearrange("p (b t) -> p b t", b=cut), ALU.mult))
                v.tensor_tensor(p_t[n % 2][:, cut:4, :], e_t[n % 2][:, cut:4, :],
                                rest.rearrange("p (b t) -> p b t", b=4 - cut), ALU.mult).then_inc(p_ready, 1)

            masked_maxima(0)
            masked_maxima(1)
            for n in range(2 * H):
                probabilities(n)
                if n >= 1:
                    outputs(n - 1)
                if n + 2 < 2 * H:
                    masked_maxima(n + 2)
            outputs(2 * H - 1)
            v.wait_ge(unit_ready, 2 * H)
            for i in range(NT):
                v.tensor_tensor(hsum[:, i, :], hsum[:, i, :], o_tok[:, i, :], ALU.mult).then_inc(yml_ready, 1)

            def bcast(k, i):
                return bc[:, k + 3 * (i > 0), :]

            def mix_normed(i):
                v.wait_ge(msq, i + 1)
                own.link(v.reciprocal(rstd[:, i:i + 1], sum_sq[:, i:i + 1]))
                v.wait_ge(bc_ready, 1 if i == 0 else 4)
                if i:
                    v.wait_ge(x1_ready, i)
                v.scalar_tensor_tensor(tn[:, :], bank(2 * i, 0, 1024), rstd[:, i:i + 1], bcast(0, i), ALU.mult, ALU.mult)\
                    .then_inc(tn_ready, 1)

            def modulated(i):
                v.wait_ge(xsq, i + 1)
                own.link(v.reciprocal(rstd2[:, i:i + 1], sum_sq2[:, i:i + 1]))
                v.wait_ge(bc_ready, 3 if i == 0 else 6)
                if i:
                    v.wait_ge(h2T_done, i)
                    v.wait_ge(hi_ready, i)
                    v.wait_ge(lo_ready, i)
                flat = hp[:, :, :].rearrange("p c q -> p q c")
                own.link(v.scalar_tensor_tensor(flat, x[:, i, :].rearrange("p (q c) -> p q c", c=NC), rstd2[:, i:i + 1],
                                                bcast(1, i).rearrange("p (q c) -> p q c", c=NC), ALU.mult, ALU.mult))
                v.tensor_tensor(flat, flat, bcast(2, i).rearrange("p (q c) -> p q c", c=NC), ALU.add).then_inc(hp_ready, 1)

            mix_normed(0)
            mix_normed(1)
            modulated(0)
            for i in range(10, 12):
                ada_evac(i)
            mix_normed(2)
            modulated(1)
            modulated(2)

            def sh_a(i):
                v.wait_ge(silu_ready, i + 1)
                if i:
                    v.wait_ge(aT_done, i)
                v.tensor_tensor(act[:, :, :].rearrange("s j q -> s q j"), sil[:, :].rearrange("s (q j) -> s q j", j=2),
                                bank(SH_BANK[i], F, 2 * F).rearrange("s (q j) -> s q j", j=2), ALU.mult)\
                    .then_inc(a_ready, 1)

            sh_a(0)
            v.wait_ge(prob_ready, 1)
            v.wait_ge(router_in, 32)
            own.link(v.tensor_tensor(biased[:, :, :], s_prob[:, :, :], b_router[:, :].unsqueeze(1).broadcast_to([P, NT, NE]),
                                     ALU.add))
            for i in range(NT):
                for g in range(NG):
                    own.add(v.max(top2[:, NG * i + g, :], biased[:, i, NG * g:NG * g + NG]))
            own.add(v.memset(gext[:, :, NG:NG + 4], BIG))
            own.add(v.memset(ext[:, :, NE:NE + 2], BIG))
            own.wait()
            own.link(v.tensor_tensor(gext[:, :, 0:NG], top2[:, :, 0:1].rearrange("p (i g) o -> p i (g o)", i=NT),
                                     top2[:, :, 1:2].rearrange("p (i g) o -> p i (g o)", i=NT), ALU.add))
            for i in range(NT):
                own.add(v.max(best[:, i, :], gext[:, i, 0:NG]))
            own.wait()
            own.link(v.memset(best[:, :, TOPG:8], BIG))
            for i in range(NT):
                own.add(v.match_replace(gout[:, i, :], best[:, i, :], gext[:, i, :], NEG))
            own.wait()
            gsel = gout[:, :, 0:NG]
            own.link(v.tensor_scalar(gsel, gsel, NEG, None, ALU.is_equal))
            own.link(v.tensor_scalar(gext[:, :, 0:NG], gsel, BIG, NEG, ALU.mult, ALU.add))
            for i in range(NT):
                own.add(v.tensor_tensor(ext[:, i, 0:NE].rearrange("p (g e) -> p g e", g=NG),
                                        biased[:, i, :].rearrange("p (g e) -> p g e", g=NG),
                                        gsel[:, i, :].unsqueeze(2).broadcast_to([P, NG, NE // NG]), ALU.mult))
            own.wait()
            for i in range(NT):
                own.add(v.tensor_tensor(ext[:, i, 0:NE].rearrange("p (g e) -> p g e", g=NG),
                                        ext[:, i, 0:NE].rearrange("p (g e) -> p g e", g=NG),
                                        gext[:, i, 0:NG].unsqueeze(2).broadcast_to([P, NG, NE // NG]), ALU.add))
            own.wait()
            for i in range(NT):
                own.add(v.max(best[:, i, :], ext[:, i, 0:NE]))
            own.wait()
            own.link(v.memset(best[:, :, TOPK:8], BIG))
            for i in range(NT):
                own.add(v.match_replace(chosen[:, i, :], best[:, i, :], ext[:, i, :], 3 * NEG))
            own.wait()
            v.tensor_scalar(emask[:, :, :], chosen[:, :, 0:NE], 3 * NEG, None, ALU.is_equal).then_inc(emask_ready, 1)
            v.wait_ge(emask_ready, 1)

            def f_first(i):
                if i == 0:
                    v.wait_ge(out_sem, 32)
                for n in range(2):
                    if (i, n) != (NT - 1, 1):
                        v.wait_ge(f_done, 2 * i + n + 1)
                    else:
                        v.wait_ge(dn_used[SLOTS - 1], 1)
                    v.tensor_copy(f_acc[:, i, 512 * n:512 * (n + 1)], bank(5 + n)).then_inc(f_added, 1)

            sh_a(1)
            own.link(v.tensor_tensor(comb[:, :, :], s_prob[:, :, :], emask[:, :, :], ALU.mult))
            own.link(v.tensor_reduce(wsum, comb[:, :, :], AX.X, ALU.add))
            own.link(v.reciprocal(wsum, wsum))
            for i in range(NT):
                own.add(v.tensor_scalar(comb[:, i, :], comb[:, i, :], wsum[:, i:i + 1], ROUTED_SCALE, ALU.mult, ALU.mult))
            own.wait()
            own.link(v.tensor_copy(comb2[:, :, :, 0], comb[:, :, :]))
            own.link(v.tensor_tensor(comb2[:, :, :, 1], comb[:, :, :], comb2[:, :, :, 0].bitcast(F32), ALU.subtract))
            v.wait_ge(pos_done, 1)
            ranks = bank(3, 0, NT * NE).rearrange("p (i e) -> p i e", i=NT)
            own.link(v.scalar_tensor_tensor(posm[:, :, :], ranks, 1.0, emask[:, :, :], ALU.add, ALU.mult))
            own.link(v.tensor_scalar(posm[:, :, :], posm[:, :, :], -1.0, None, ALU.add))
            own.add(v.tensor_copy(table_e[0:1, 0:NE], const[0:1, C_IOTA:C_IOTA + NE]))
            own.add(v.memset(rank0[:, 0:NE], 0.0))
            own.wait()

            def make_onehot(p, par):
                for half in range(2):
                    item = p * 2 + half
                    e = v.value_load(table_e[0:1, bass.ds(item, 1)], min_val=0, max_val=NE - 1)
                    own.add(v.tensor_copy(cpair[:, :, 2 * half:2 * half + 2],
                                          comb2[:, :, bass.ds(e, 1), :].rearrange("p i o w -> p i (o w)")))
                    for i in range(NT):
                        ins = v.tensor_scalar(onehot[par][:, i, CAP * half:CAP * (half + 1)], iota,
                                              rank0[:, bass.ds(item, 1)], posm[:, i, bass.ds(e, 1)], ALU.add, ALU.is_equal)
                        if (half, i) != (1, NT - 1):
                            own.add(ins)
                ins.then_inc(oh_ready, 1)

            def slot_weights(p, par):
                v.wait_ge(wsl_done, p + 1)
                for half in range(2):
                    q = slice(CAP * half, CAP * (half + 1))
                    two = bank(7, 500 + 2 * half, 502 + 2 * half)
                    v.tensor_reduce(wsl[q, par:par + 1], two[q, :], AX.X, ALU.add).then_inc(wsl_ready, 1)

            f_first(0)
            sh_a(2)
            make_onehot(0, 0)
            f_first(1)
            slot_weights(0, 0)
            counts = bank(3, NT * NE, NT * NE + NE)[0:NE, :]
            for r in range(ROUNDS):
                own.add(v.tensor_scalar(flags[:, r, :], counts, float(CAP * (r + 1)), None, ALU.is_gt))
            own.wait()
            fl = flags[:, :, :].rearrange("p r e -> p (r e)")
            ix = index[:, :, :].rearrange("p r e -> p (r e)")
            own.link(v.tensor_tensor_scan(ix, fl, fl, 0.0, ALU.add, ALU.bypass))
            mt = match[:, :, :].rearrange("p r e -> p (r e)")
            own.link(v.scalar_tensor_tensor(mt, ix, const[0:NE, C_RANK:C_RANK + 1], fl, ALU.is_equal, ALU.mult))
            own.link(v.tensor_tensor(match2[:, :, :], match[:, :, :],
                                     const[0:NE, C_IOTA:C_IOTA + NE].unsqueeze(1).broadcast_to([NE, ROUNDS, NE]), ALU.mult))
            own.link(v.tensor_reduce(items[:, 0:1], match2[:, :, :].rearrange("p r e -> p (r e)"), AX.X, ALU.add))
            own.link(v.tensor_tensor(match2[:, :, :], match[:, :, :],
                                     const[0:NE, C_ROUND:C_END].unsqueeze(2).broadcast_to([NE, ROUNDS, NE]), ALU.mult))
            own.link(v.tensor_reduce(items[:, 1:2], match2[:, :, :].rearrange("p r e -> p (r e)"), AX.X, ALU.add))
            own.link(v.tensor_scalar(items[:, 1:2], items[:, 1:2], FAR, None, ALU.add))
            own.add(v.tensor_scalar(diag_e[:, :], ident[0:NE, 0:NE], items[:, 0:1], None, ALU.mult))
            v.tensor_scalar(diag_r[:, :], ident[0:NE, 0:NE], items[:, 1:2], None, ALU.mult).then_inc(item_ready, 1)
            v.wait_ge(tab_done, 1)
            own.add(v.tensor_copy(table_e[0:1, NE:N_TAB], bank(4, 0, N_TAB - NE)[0:1, :]))
            own.add(v.tensor_copy(rank0[:, NE:N_TAB], bank(4, NE, NE + N_TAB - NE)))
            own.link(v.tensor_scalar(match[0:1, 0, 0:OVER_PAIRS], const[0:1, C_IOTA:C_IOTA + OVER_PAIRS], 2.0,
                                     index[0:1, ROUNDS - 1, NE - 1:NE], ALU.mult, ALU.is_lt))
            own.link(v.tensor_reduce(items[0:1, 2:3], match[0:1, 0, 0:OVER_PAIRS], AX.X, ALU.add))
            v.tensor_copy(table_e[0:1, N_TAB:N_TAB + 1], items[0:1, 2:3]).then_inc(tab_ready, 1)
            v.wait_ge(tab_ready, 1)
            own.wait()

            f_first(2)
            count0 = own.count

            def pair(it, q):
                p = it * 2 + q
                own.count = it * (2 * STEPS) + (count0 + q * STEPS)
                v.wait_ge(wsl_done, p + 1)
                make_onehot(p + 1, (q + 1) % 2)
                v.wait_ge(silu_ready, p + (NT + 1))
                v.wait_ge(aT_done, p + NT)
                v.wait_ge(wsl_ready, p * 2 + 2)
                v.scalar_tensor_tensor(act[:, :, :].rearrange("s j q -> s q j"), sil[:, :].rearrange("s (q j) -> s q j", j=2),
                                       wsl[:, q:q + 1], bank(2, F, 2 * F).rearrange("s (q j) -> s q j", j=2),
                                       ALU.mult, ALU.mult).then_inc(a_ready, 1)
                slot_weights(p + 1, (q + 1) % 2)
                f_add(p)
                v.wait_ge(ohT_done, p + 1)
                v.tensor_copy(onehotT[:, :], bank(2, 0, T)).then_inc(ohT_ready, 1)
                v.wait_ge(yhi_ready, p + 1)
                v.wait_ge(y_ready, p + 1)
                v.tensor_tensor(y_lo[:, :], bank(3, 0, 1024), y_hi[:, :].bitcast(F32), ALU.subtract).then_inc(y_ready, 1)

            def f_add(p):
                for c in range(6):
                    i, n = divmod(c, 2)
                    v.wait_ge(f_done, p * 6 + (5 + c + 1))
                    v.wait_ge(f_added, p * 6 + (c + 1))
                    dst = f_acc[:, i, 512 * n:512 * (n + 1)]
                    v.tensor_tensor(dst, dst, bank(5 + n), ALU.add).then_inc(f_added, 1)

            with v.Fori(0, MAIN_PAIRS // 2) as it:
                for q in range(2):
                    pair(it, q)
            n_pairs = v.value_load(table_e[0:1, N_TAB:N_TAB + 1], min_val=0, max_val=OVER_PAIRS)
            with v.If(n_pairs > 0):
                pair(MAIN_PAIRS // 2, 0)
            with v.Else():
                v.nop()
            with v.If(n_pairs > 1):
                pair(MAIN_PAIRS // 2, 1)
                with v.Fori(1, OVER_PAIRS // 2) as jj:
                    for q in range(2):
                        with v.If(jj * 2 + q < n_pairs):
                            pair(jj + MAIN_PAIRS // 2, q)
                        with v.Else():
                            v.nop()
            with v.Else():
                v.nop()
            own.count = n_pairs * STEPS + (count0 + STEPS * MAIN_PAIRS)
            v.wait_ge(grow2_in, 32)
            v.tensor_tensor(modrow[:, 10:12, :], modrow[:, 10:12, :], grow[:, 0, :, :], ALU.mult).then_inc(grow2_ready, 1)
            f_add(n_pairs + MAIN_PAIRS)
            for i in range(NT):
                v.wait_ge(fsq, i + 1)
                own.link(v.reciprocal(rstd[:, i:i + 1], sum_sq[:, i:i + 1]))
                if i == 0:
                    v.wait_ge(gf_done, 1)
                own.link(v.scalar_tensor_tensor(f_acc[:, i, :], f_acc[:, i, :], rstd[:, i:i + 1],
                                                bank(0 if i == 0 else 2, 0, 1024), ALU.mult, ALU.mult))
                v.tensor_tensor(x[:, i, :], x[:, i, :], f_acc[:, i, :], ALU.add).then_inc(y_out, 1)

        @block.gpsimd
        def _(g):
            for i in range(NT):
                g.wait_ge(tn_ready, i + 1)
                g.tensor_tensor(x[:, i, :], x[:, i, :], tn[:, :], ALU.add).then_inc(x1_ready, 1)
                g.wait_ge(hi_ready, i + 1)
                g.tensor_tensor(h_lo[:, i, :, :], hp[:, :, :], h_hi[:, i, :, :].bitcast(F32), ALU.subtract)\
                    .then_inc(lo_ready, 1)
            g.wait_ge(hp_ready, NT)
            g.memset(y_hi[:, :].bitcast(F32), 0.0).then_inc(zeroed, 1)
            g.memset(y_lo[:, :].bitcast(F32), 0.0).then_inc(zeroed, 1)
            g.wait_ge(zeroed, 4)
            g.memset(onehotT[:, :].bitcast(F32), 0.0).then_inc(ohT_ready, 1)
            g.wait_ge(ohT_ready, 1)
            g.nop().then_inc(y_ready, 1)

        @block.tensor
        def _(t):
            t.wait_ge(const_in, 16)
            def ada(i):
                n = chunk[f"a{i}"]
                s = n % SLOTS
                if i == 0:
                    t.wait_ge(sc_ready, 1)
                t.wait_ge(gu_in[s], 16 * (n // SLOTS + 1))
                if i >= 2:
                    t.wait_ge(mod_ready, i - 1)
                for c in range(NC):
                    for j in range(4):
                        ins = t.matmul(bank(6 + i % 2, P * (i % 4), P * (i % 4) + P)[32 * j:32 * j + 32, :],
                                       scT[:, c, :], w_gu[s][:, c, P * j:P * j + P],
                                       start=(c == 0), stop=(c == NC - 1), tile_position=(0, 32 * j))
                ins.then_inc(gu_used[s], 1)

            ada(0)
            ada(1)
            for i in range(NT):
                t.wait_ge(xn_ready, i + 1)
                for c in range(NC):
                    ins = t.transpose(psum[:, T * c + P * i:T * c + P * i + P], xn[:, i, P * c:P * c + P], ident)
            ins.then_inc(xT_done, 1)
            ada(2)
            ada(3)
            t.wait_ge(mod_a_ready, 1)
            for i in range(4):
                ins = t.matmul(bank(6, P + 8 * i, P + 8 * i + 8), modrow[:, i, :],
                               ident.rearrange("p (j r) -> p j r", j=4)[:, :, 0:2], start=True, stop=True)
            ins.then_inc(modT_done, 1)

            t.wait_ge(wgp_ready, 4)
            t.wait_ge(h1_act, NC)
            t.wait_ge(h1_dve, NC)
            for g in range(2):
                for c in range(NC):
                    ins = t.matmul(bank(g, 0, T)[0:36, :], wgp[:, c, g, :], hT[:, c, :], start=(c == 0), stop=(c == NC - 1))
            ins.then_inc(gates_done, 1)

            def z_unit(n):
                w, i = z_units[n]
                k = chunk[w]
                s = k % SLOTS
                t.wait_ge(gu_in[s], 16 * (k // SLOTS + 1))
                if n >= 4:
                    if n - 4 in by_act:
                        t.wait_ge(z_act, by_act.index(n - 4) + 1)
                    else:
                        t.wait_ge(z_dve, by_dve.index(n - 4) + 1)
                for c in range(NC):
                    if w in "qk":
                        ins = t.matmul(bank(2 + n % 4, 0, T), w_gu[s][:, c, DH * i:DH * (i + 1)], hT[:, c, :],
                                       start=(c == 0), stop=(c == NC - 1))
                    else:
                        ins = t.matmul(bank(2 + n % 4), hT[:, c, P * i:P * (i + 1)], w_gu[s][:, c, :],
                                       start=(c == 0), stop=(c == NC - 1))
                ins.then_inc(gu_used[s] if n in ends else z_done, 1)

            for n in range(len(z_units)):
                z_unit(n)
                if n == 3:
                    ada(4)
                    ada(5)
                if n == 7:
                    ada(6)
                    ada(7)
                if n == 10:
                    t.wait_ge(w_ready, 2)
                    t.wait_ge(nat_ready, 9)
                    for a_ in range(3):
                        for tile in range(NT):
                            col = T + 24 * a_ + 8 * tile
                            ins = t.matmul(bank(1, col, col + 2 * H), g_nat[:, a_, P * tile:P * tile + P],
                                           ident[0:36, 0:64].rearrange("p (d r) -> p d r", d=2)[:, :, 0:H],
                                           start=True, stop=True)
                    ins.then_inc(gT_done, 1)
                    ada(8)
                    ada(9)
            t.wait_ge(z_act, 8)
            t.wait_ge(abs_ready, 1)
            for h in range(H):
                ins = t.transpose(bank(0, DH * h, DH * (h + 1)), kT[:, h, 0:P], ident)
            ins.then_inc(ktok_done, 1)
            t.wait_ge(pool_in, 48)
            t.wait_ge(z_act, 11)
            t.wait_ge(z_dve, 6)
            for g in range(4):
                if g >= 2:
                    t.wait_ge(dT_ready, g - 1)
                cols = slice(P * g, P * g + P)
                b = bank(2 + g % 2, 0, T)
                t.matmul(b[:, 0:T_CTX], u_tok[:, 0, cols], poolm[:, g, 0:T_CTX], start=True, stop=True)
                for k in range(2):
                    ins = t.matmul(b[:, T_CTX:T], u_tok[:, 1 + k, cols],
                                   poolm[:, g, T_CTX + T_LAT * k:T_CTX + T_LAT * (k + 1)], start=(k == 0), stop=(k == 1))
                ins.then_inc(dT_done, 1)
                t.wait_ge(dT_ready, g + 1)
                if g >= 2:
                    t.wait_ge(yp_ready, g - 1)
                t.matmul(bank(4 + g % 2, 0, T), w_pool[:, g, :], dT[g % 2][:, :], start=True, stop=True).then_inc(yp_done, 1)

            t.wait_ge(state_in, 32)
            t.wait_ge(yp_ready, 4)
            t.wait_ge(ktok_ready, 1)
            t.wait_ge(mod_ready, 10)
            def scores(h):
                if h >= 2:
                    t.wait_ge(p_ready, 2 * (h - 1))
                sa, sb = 2 * (h % 2), 2 * (h % 2) + 1
                t.matmul(bank(sa, 0, P), kT[:, h, 0:P], qT[:, h, 0:P], start=True, stop=True)
                t.matmul(bank(sa, P, 3 * P), kT[:, h, P:2 * P], qT[:, h, P:T], start=True, stop=True)
                t.matmul(bank(sb, 0, 2 * P), kT[:, h, 2 * P:T], qT[:, h, P:T], start=True, stop=True)\
                    .then_inc(st_done, 1)

            def minus_maxima(n):
                h, d = divmod(n, 2)
                if n >= 2:
                    t.wait_ge(e_ready, n - 1)
                q = slice(32 * d, 32 * d + H)
                for tile in range(NT):
                    ins = t.matmul(bank(4 + d, P * tile, P * tile + P),
                                   const[q, C_IDENT + 32 * d + h:C_IDENT + 32 * d + h + 1].broadcast_to([H, P]),
                                   g_lf[q, natural(d, tile)], start=True, stop=True)
                ins.then_inc(nm_done, 1)

            minus_maxima(0)
            minus_maxima(1)
            scores(0)
            scores(1)
            for n in range(2 * H):
                if n + 2 < 2 * H:
                    minus_maxima(n + 2)
                products(t, n)
                if n % 2 and n // 2 + 2 < H:
                    scores(n // 2 + 2)

            for i in range(NT):
                t.wait_ge(yml_ready, i + 1)
                if i == 0:
                    t.wait_ge(unit_ready, 2 * H)
                    t.wait_ge(c_ready, 2 * H)
                if i == 2:
                    t.wait_ge(mT_ready, 1)
                for h in range(H):
                    ins = t.transpose(bank(6 + i % 2, P * h, P * h + P), hsum[:, i, DH * h:DH * (h + 1)], ident)
                ins.then_inc(mT_done, 1)

            BC_ROWS = ((4, 0), (8, 0), (6, 0), (4, 1), (8, 1), (6, 1))

            def rows_over_partitions(first, m, b):
                for k in range(2):
                    for j in range(4):
                        row = 32 * j + m
                        ins = t.matmul(bank(b + k, P * j, P * j + P), ident[:, row:row + 1].broadcast_to([P, P]),
                                       modrow[:, first + k, :], start=True, stop=True)
                return ins

            t.wait_ge(mods_final, 2)
            t.wait_ge(mT_ready, NT)
            for k in range(6):
                if k:
                    t.wait_ge(bc_ready, k)
                first, m = BC_ROWS[k]
                rows_over_partitions(first, m, 6).then_inc(bc_done, 1)
                i, n = divmod(k, 2)
                s = chunk[f"w{n}"] % SLOTS
                t.wait_ge(gu_in[s], 16 * (chunk[f"w{n}"] // SLOTS + 1))
                for c in range(NC):
                    ins = t.matmul(bank(2 * i + n), hT[:, c, P * i:P * i + P], w_gu[s][:, c, :],
                                   start=(c == 0), stop=(c == NC - 1))
                ins.then_inc(wo_done if i < NT - 1 else gu_used[s], 1)

            s_sh = SLOTS - 1

            def tokens_T(i):
                t.wait_ge(hp_ready, i + 1)
                for c in range(NC):
                    ins = t.transpose(bank(2 * i, P * c, P * c + P), hp[:, c, :], ident)
                ins.then_inc(h2T_done, 1)

            def sh_gu(i):
                t.wait_ge(h2T_ready, i + 1)
                t.wait_ge(gu_in[s_sh], 16 * PRE)
                for c in range(NC):
                    ins = t.matmul(bank(SH_BANK[i]), hT[:, c, P * i:P * i + P], w_gu[s_sh][:, c, :],
                                   start=(c == 0), stop=(c == NC - 1))
                ins.then_inc(sh_gu_done if i < NT - 1 else gu_used[s_sh], 1)

            def transposes(count):
                t.wait_ge(a_ready, count)
                for j in range(2):
                    ins = t.transpose(bank(7, P * j, P * j + P), act[:, j, :], ident)
                ins.then_inc(aT_done, 1)

            def sh_down(i):
                t.wait_ge(actT_ready, i + 1)
                t.wait_ge(dn_in[s_sh], 16)
                for n in range(2):
                    if i:
                        t.wait_ge(f_added, 2 * (i - 1) + n + 1)
                    for j in range(2):
                        ins = t.matmul(bank(5 + n), actT[:, j, :], w_dn[s_sh][:, j, 512 * n:512 * (n + 1)],
                                       start=(j == 0), stop=(j == 1))
                    ins.then_inc(f_done if (i, n) != (NT - 1, 1) else dn_used[s_sh], 1)

            t.wait_ge(bc_ready, 6)
            ada(10)
            ada(11)
            tokens_T(0)
            sh_gu(0)
            tokens_T(1)
            sh_gu(1)
            tokens_T(2)
            t.wait_ge(router_in, 32)
            t.wait_ge(h2T_ready, NT)
            t.wait_ge(mod_ready, 12)
            for i in range(NT):
                for c in range(NC):
                    ins = t.matmul(bank(6, NE * i, NE * (i + 1)), hT[:, c, P * i:P * i + P], w_router[:, c, :],
                                   start=(c == 0), stop=(c == NC - 1))
            ins.then_inc(logit_done, 1)
            transposes(1)
            sh_gu(2)
            t.wait_ge(emask_ready, 1)
            for i in range(NT):
                for k in range(i + 1):
                    t.matmul(bank(3, NE * i, NE * (i + 1)), tri if k == i else ones, emask[:, k, :],
                             start=(k == 0), stop=(k == i))
            for k in range(NT):
                ins = t.matmul(bank(3, NT * NE, NT * NE + NE), ones, emask[:, k, :], start=(k == 0), stop=(k == 2))
            ins.then_inc(pos_done, 1)
            t.wait_ge(prob_ready, 1)
            sh_down(0)
            transposes(2)
            sh_down(1)
            transposes(3)
            sh_down(2)

            def slot_weights(p, par):
                for i in range(NT):
                    ins = t.matmul(bank(7, 500, 504), onehot[par][:, i, :], cpair[:, i, :], start=(i == 0), stop=(i == NT - 1))
                ins.then_inc(wsl_done, 1)

            def gather(par, n, parts):
                every = [(i, part) for i in range(NT) for part in (h_hi, h_lo)]
                for k in parts:
                    i, part = every[k]
                    ins = t.matmul(bank(n), onehot[par][:, i, :], part[:, i, 4 * n:4 * n + 4, :],
                                   start=(k == 0), stop=(k == len(every) - 1))
                if every[k] == every[-1]:
                    ins.then_inc(gathered, 1)

            def gathered_T(p, n):
                t.wait_ge(hg_ready, p * 2 + (n + 1))
                for c in range(4):
                    ins = t.transpose(bank(n, P * c, P * c + P), hg[:, n, P * c:P * c + P], ident)
                ins.then_inc(hgT_done, 1)

            def combine(p, c):
                i, n = divmod(c, 2)
                t.wait_ge(f_added, p * 6 + (c + 5))
                for part in (y_hi, y_lo):
                    ins = t.matmul(bank(5 + n), onehotT[:, P * i:P * i + P], part[:, 512 * n:512 * (n + 1)],
                                   start=(part is y_hi), stop=(part is y_lo))
                ins.then_inc(f_done, 1)

            def pair(it, q):
                p = it * 2 + q
                slots = (2 * q, 2 * q + 1)
                t.wait_ge(hgT_ready, p * 2 + 2)
                t.wait_ge(a_ready, p + NT)
                t.wait_ge(ohT_ready, p + 1)
                for s in slots:
                    t.wait_ge(gu_in[s], it * 16 + 16 * (PRE + 1))
                for c in range(NC):
                    for half, s in enumerate(slots):
                        rows = slice(CAP * half, CAP * (half + 1))
                        ins = t.matmul(bank(2)[rows, :], hgT[:, c, rows], w_gu[s][:, c, :],
                                       start=(c == 0), stop=(c == NC - 1), tile_position=(0, CAP * half))
                        if c == NC - 1:
                            ins.then_inc(gu_used[s], 1)
                t.wait_ge(oh_ready, p + 2)
                t.wait_ge(wsl_ready, p * 2 + 2)
                nxt = (q + 1) % 2
                slot_weights(p + 1, nxt)
                t.wait_ge(y_ready, p + 1)
                gather(nxt, 0, (0, 1, 2))
                combine(p, 0)
                gather(nxt, 0, (3, 4, 5))
                combine(p, 1)
                gather(nxt, 1, (0, 1, 2))
                combine(p, 2)
                gather(nxt, 1, (3, 4, 5))
                combine(p, 3)
                t.wait_ge(wsl_ready, p * 2 + 4)
                transposes(p + (NT + 1))
                combine(p, 4)
                gathered_T(p + 1, 0)
                combine(p, 5)
                gathered_T(p + 1, 1)
                for i in range(NT):
                    ins = t.transpose(bank(2, P * i, P * i + P), onehot[q][:, i, :].bitcast(F32), ident)
                ins.then_inc(ohT_done, 1)
                t.wait_ge(actT_ready, p + (NT + 1))
                for s in slots:
                    t.wait_ge(dn_in[s], it * 16 + 16 * (1 + dn_base(s)))
                for n in range(2):
                    for j in range(2):
                        for half, s in enumerate(slots):
                            rows = slice(CAP * half, CAP * (half + 1))
                            ins = t.matmul(bank(3 + n)[rows, :], actT[:, j, rows], w_dn[s][:, j, 512 * n:512 * (n + 1)],
                                           start=(j == 0), stop=(j == 1), tile_position=(0, CAP * half))
                            if n == 1 and j == 1:
                                ins.then_inc(dn_used[s], 1)

            t.wait_ge(hi_ready, NT)
            t.wait_ge(lo_ready, NT)
            t.wait_ge(oh_ready, 1)
            t.wait_ge(a_ready, 2)
            slot_weights(0, 0)
            for n in range(2):
                gather(0, n, range(6))
            for n in range(2):
                gathered_T(0, n)
            t.wait_ge(item_ready, 1)
            t.matmul(bank(4, 0, NE), ones[0:NE, :], diag_e[:, :], start=True, stop=True)
            t.matmul(bank(4, NE, 2 * NE), ones[0:NE, :], diag_r[:, :], start=True, stop=True).then_inc(tab_done, 1)
            with t.Fori(0, MAIN_PAIRS // 2) as it:
                for q in range(2):
                    pair(it, q)
            t.wait_ge(tab_ready, 1)
            n_pairs = t.value_load(table_e[0:1, N_TAB:N_TAB + 1], min_val=0, max_val=OVER_PAIRS)
            with t.If(n_pairs > 0):
                pair(MAIN_PAIRS // 2, 0)
            with t.Else():
                t.nop()
            with t.If(n_pairs > 1):
                pair(MAIN_PAIRS // 2, 1)
                with t.Fori(1, OVER_PAIRS // 2) as jj:
                    for q in range(2):
                        with t.If(jj * 2 + q < n_pairs):
                            pair(jj + MAIN_PAIRS // 2, q)
                        with t.Else():
                            t.nop()
            with t.Else():
                t.nop()
            t.wait_ge(grow2_ready, 1)
            t.wait_ge(hgT_ready, n_pairs * 2 + (2 * MAIN_PAIRS + 2))
            t.wait_ge(y_ready, n_pairs + (MAIN_PAIRS + 1))
            t.wait_ge(ohT_ready, n_pairs + (MAIN_PAIRS + 1))
            rows_over_partitions(10, 0, 0)
            rows_over_partitions(10, 1, 2).then_inc(gf_done, 1)
            for c in range(6):
                combine(n_pairs + MAIN_PAIRS, c)



_INS = ["x_prompt", "x_sample", "state_C", "state_n", "state_m", "c", "c_ctx", "w_ada", "b_ada", "g_pre_mix", "w_in",
        "b_gate", "w_pool", "pool_scale", "w_out", "g_post_mix", "g_pre_ffn", "w_router", "b_router", "w_expert_gu",
        "w_expert_down", "w_shared_gu", "w_shared_down", "g_post_ffn"]
_OUTS = [(1, T_CTX, D), (1, T_LAT, D), (1, 1, 2, H, DH, DH), (1, 1, 2, H, DH), (1, 1, 2, H)]


def kernel(**inputs):
    import concourse.bacc as _bacc
    from concourse.bass_utils import run_bass_kernel_spmd as _run

    nc = _bacc.Bacc("TRN2", target_bir_lowering=False, num_devices=1)
    arrays, t_in = {}, {}
    for name in _INS:
        arrays[f"in_{name}"] = np.ascontiguousarray(inputs[name])
    arrays["in_shape_constants"] = shape_constants()
    arrays["in_pool_constants"] = pool_constants()
    for key, a in arrays.items():
        t_in[key[3:]] = nc.dram_tensor(key, a.shape, mybir.dt.from_np(a.dtype), kind="ExternalInput").ap()
    t_out = [nc.dram_tensor(f"out_{i}", shape, F32, kind="ExternalOutput").ap() for i, shape in enumerate(_OUTS)]
    build_layer(nc, t_in, t_out)
    r = _run(nc, [arrays], core_ids=[0])
    return tuple(r.results[0][f"out_{i}"] for i in range(len(_OUTS)))
```

```python
from contextlib import ExitStack

import numpy as np
import concourse.bass as bass
from concourse import mybir

P = 128
D = 1024
NC = D // P
T_CTX, T_LAT = 128, 256
T = T_CTX + T_LAT
NT = T // P
GRID_W = 64
WINDOWS = (2, 4, 8, 16)
H = 4
DH = 128
DV = DH + 1
MW = H * DH
NE = 64
NG = 8
TOPK = 6
TOPG = 4
F = 256
CAP = 64
EPS = 1e-6
ROUTED_SCALE = 2.5
NEG = -1e30
BIG = 1e30
FAR = 4096.0
ROUNDS = T // CAP - 1
N_OVER = (T * TOPK) // (CAP + 1) + 1
N_OVER += N_OVER % 2
N_TAB = NE + N_OVER + 2
MAIN_PAIRS = NE // 2
OVER_PAIRS = N_OVER // 2
SLOTS = 4

F32 = mybir.dt.float32
F32R = mybir.dt.float32r
I32 = mybir.dt.int32
ALU = mybir.AluOpType
ACT = mybir.ActivationFunctionType
AX = mybir.AxisListType

C_IDENT = 0
C_TRI = C_IDENT + P
C_ONES = C_TRI + P
C_MASK = C_ONES + P
C_IOTA = C_MASK + 2 * P
C_RANK = C_IOTA + NE
C_ROUND = C_RANK + 1
C_END = C_ROUND + ROUNDS


def shape_constants():
    c = np.zeros((P, C_END), np.float32)
    i = np.arange(P)
    c[:, C_IDENT:C_IDENT + P] = np.eye(P)
    c[:, C_TRI:C_TRI + P] = i[:, None] < i[None, :]
    c[:, C_ONES:C_ONES + P] = 1.0
    c[:, C_MASK:C_MASK + P] = np.where(i[:, None] > i[None, :], NEG, 0.0)
    c[:, C_MASK + P:C_MASK + 2 * P] = np.where(i[:, None] < i[None, :], NEG, 0.0)
    c[:, C_IOTA:C_IOTA + NE] = np.arange(NE)
    c[:, C_RANK] = i + 1
    c[:, C_ROUND:C_END] = CAP * np.arange(1, ROUNDS + 1) - FAR
    return c


def box(n, w):
    m = np.zeros((n, n))
    for t in range(n):
        lo, hi = max(t - w // 2, 0), min(t + w - w // 2, n)
        m[t, lo:hi] = 1.0 / (hi - lo)
    return m


def pool_constants():
    c = np.zeros((P, len(WINDOWS), T_CTX + 2 * T_LAT), np.float32)
    for g, w in enumerate(WINDOWS):
        c[:, g, 0:T_CTX] = (box(T_CTX, w) - np.eye(T_CTX)).T
        lat = (np.kron(box(T_LAT // GRID_W, w), box(GRID_W, w)) - np.eye(T_LAT)).T
        c[:, g, T_CTX:] = lat.reshape(2, P, T_LAT).transpose(1, 0, 2).reshape(P, 2 * T_LAT)
    return c.reshape(P, -1)


class Chain:

    def __init__(self, engine, semaphore, count=0):
        self.engine, self.semaphore, self.count = engine, semaphore, count

    def add(self, instruction):
        instruction.then_inc(self.semaphore, 1)
        self.count = self.count + 1

    def wait(self):
        self.engine.wait_ge(self.semaphore, self.count)

    def link(self, instruction):
        self.add(instruction)
        self.wait()


def build_layer(nc, t_in, t_out):
    with ExitStack() as ctx:
        cursor = [(nc.sbuf_base + 31) // 32 * 32]

        def at(name, shape, offset, dt=F32):
            return nc.alloc_sbuf_tensor_at(name, shape, dt, offset=offset)

        def place(name, shape, dt=F32):
            n = int(np.prod(shape[1:])) * 4
            n = (n + 31) // 32 * 32
            o = cursor[0]
            cursor[0] += n
            return nc.alloc_sbuf_tensor_at(name, shape, dt, offset=o)

        def region(nbytes):
            o = cursor[0]
            cursor[0] += nbytes
            return o

        def sem(name):
            return ctx.enter_context(nc.semaphore(name))

        w_gu, w_dn, w_lo, tail = [], [], [], []
        for s in range(SLOTS):
            w_lo.append(at(f"w_lo{s}", [P, NC, 2 * F], cursor[0], F32R))
            w_gu.append(place(f"w_gu{s}", [P, NC, 2 * F]))
            tail.append(cursor[0])
            w_dn.append(place(f"w_dn{s}", [P, 2, D]))
        x = place("x", [P, NT, D])
        tT_lo = at("tT_lo", [P, NC, T], cursor[0], F32R)
        hT_at = cursor[0]
        hT = place("hT", [P, NC, T])
        w_hi = [at(f"w_hi{k}", [P, NC // 2, MW], tail[k], F32R) for k in range(2)]
        tT_hi = [at(f"tT_hi{k}", [P, NC // 2, T], tail[2 + k], F32R) for k in range(2)]
        const = place("const", [P, C_END])
        modrow = place("modrow", [P, 12, P])
        ident_w = at("ident_w", [P, NT, P + 4], cursor[0] + 1024, F32R)
        grow = place("grow", [P, 3, 2, P])
        w_router = place("w_router", [P, NC, NE])
        b_router = place("b_router", [P, NE])
        small = place("small", [P, 48])
        scT = place("scT", [P, NC, 32])
        table_e = place("table_e", [1, N_TAB + 2], I32)
        BC = region(24576)
        Z = region(49152)
        assert cursor[0] <= nc.sbuf_usable_end, (cursor[0], nc.sbuf_usable_end)

        ident = const[:, C_IDENT:C_IDENT + P]
        tri = const[:, C_TRI:C_TRI + P]
        ones = const[:, C_ONES:C_ONES + P]
        iota = const[:, C_IOTA:C_IOTA + NE]

        def mask(d):
            return const[:, C_MASK + d * P:C_MASK + (d + 1) * P]

        xn = at("xn", [P, NT, D], BC)
        g_in = at("g_in", [36, T], BC)
        g_lf = at("g_lf", [36, T], BC + 1536)
        g_t = at("g_t", [36, T], BC + 3072)
        g_b = at("g_b", [36, T], BC + 4608)
        g_u = at("g_u", [36, T], BC + 6144)
        g_mx = at("g_mx", [36, T], BC + 7680)
        em = [at("em0", [P, NT, P], BC), at("em1", [P, NT, P], BC + 9280)]
        nd = [at("nd0", [P, NT, DV], BC + 6144), at("nd1", [P, NT, DV], BC + 7712)]
        kw = [at("kw0", [P, DH], BC + 10816), at("kw1", [P, DH], BC + 11328)]
        wgp = at("wgp", [P, NC, 100], BC + 12288)
        wgs = at("wgs", [P, NC, 16], BC + 15488)
        e_t = [at("e0", [P, 4, P], BC + 15104), at("e1", [P, 4, P], BC + 17152)]
        p_t = [at("p0", [P, 4, P], BC + 19200), at("p1", [P, 4, P], BC + 21248)]
        dT = [at("dT0", [P, T], BC + 15104), at("dT1", [P, T], BC + 17152)]
        w_pool = at("w_pool", [P, len(WINDOWS), P], BC + 21248)
        g_nat = at("g_nat", [36, 3, T], BC + 15104)
        bc = at("bc", [P, 6, D], BC)
        hgT = at("hgT", [P, NC, P], BC)
        y_hi = at("y_hi", [P, D], BC + 4096, F32R)
        y_lo = at("y_lo", [P, D], BC + 8192, F32R)
        sil = at("sil", [P, F], BC + 12288)
        act = at("act", [P, 2, P], BC + 13312)
        actT = at("actT", [P, 2, P], BC + 14336)
        onehot = [at("onehot0", [P, NT, P], BC + 15360, F32R), at("onehot1", [P, NT, P], BC + 16896, F32R)]
        onehotT = [at("onehotT0", [P, NT, P], BC + 18432, F32R), at("onehotT1", [P, NT, P], Z + 24576, F32R)]
        posm = at("posm", [P, NT, NE], BC + 19968)
        comb = at("comb", [P, NT, NE], BC + 20736)
        comb2 = at("comb2", [P, NT, NE, 2], BC + 21984, F32R)
        wsl = at("wsl", [P, 2], BC + 21536)
        rank0 = at("rank0", [P, N_TAB], BC + 21568)

        u_tok = at("u_tok", [P, NT, MW], Z)
        hsum = at("hsum", [P, NT, MW], Z)
        o_tok = at("o_tok", [P, NT, MW], Z + 6144)
        qT = at("qT", [P, H, T], Z + 12288)
        kT = at("kT", [P, H, T], Z + 18432)
        v1 = at("v1", [P, NT, H, DV], Z + 24576)
        k_tok = at("k_tok", [P, MW], Z + 30784)
        poolm = at("poolm", [P, len(WINDOWS), T_CTX + 2 * T_LAT], Z + 32832)
        c0n = at("c0n", [P, 2 * H, DV], Z + 43072)
        gT = at("gT", [P, 3, NT, 2 * H], Z + 47200)
        emT = at("emT", [P, NT, 2 * H], Z + 47488)
        modT = at("modT", [P, 2, NC, 2], Z + 47584)
        h_hi = at("h_hi", [P, NT, NC, P], Z, F32R)
        h_lo = at("h_lo", [P, NT, NC, P], Z + 12288, F32R)
        gate_rows = at("gate_rows", [P, 2, D], hT_at)
        junk = at("junk", [P, D], Z + 36864)
        tn = at("tn", [P, D], Z + 24576)
        hp = at("hp", [P, NC, P], Z + 28672)
        hg = at("hg", [P, 2, 512], Z + 32768)
        f_acc = at("f_acc", [P, NT, D], Z + 36864)
        R = Z + 32768
        s_prob = at("s_prob", [P, NT, NE], R)
        biased = at("biased", [P, NT, NE], R + 768)
        ext = at("ext", [P, NT, NE + 2], R + 1536)
        chosen = at("chosen", [P, NT, NE + 2], R + 2336)
        emask = at("emask", [P, NT, NE], R + 3136)
        top2 = at("top2", [P, NT * NG, 8], Z + 24576)
        gext = at("gext", [P, NT, NG + 4], Z + 25344)
        gout = at("gout", [P, NT, NG + 4], Z + 25536)
        best = at("best", [P, NT, 8], Z + 25728)
        flags = at("flags", [NE, ROUNDS, NE], Z + 26112)
        index = at("index", [NE, ROUNDS, NE], Z + 27392)
        match = at("match", [NE, ROUNDS, NE], Z + 28672)
        match2 = at("match2", [NE, ROUNDS, NE], Z + 29952)
        items = at("items", [NE, 8], Z + 31232)
        diag_e = at("diag_e", [NE, NE], Z + 31264)
        diag_r = at("diag_r", [NE, NE], Z + 31520)

        sum_sq = small[:, 0:3]
        rstd = small[:, 3:6]
        den = small[:, 6:9]
        rden = small[:, 9:12]
        wsum = small[:, 12:15]
        m0 = small[0:36, 15:16]
        b_gate = small[0:36, 16:18]
        pool_scale = small[:, 18:22]
        ct = small[:, 22:38].rearrange("p (m c) -> p m c", m=2)
        eps = small[:, 38:39]
        sum_sq2 = small[:, 40:43]
        rstd2 = small[:, 43:46]

        psum = ctx.enter_context(nc.psum_tensor("psum", [P, 8 * 512], F32))

        def bank(b, a=0, z=512):
            return psum[:, 512 * b + a:512 * b + z]

        x_in, ct_in, const_in = sem("x_in"), sem("ct_in"), sem("const_in")
        rows_in, gate_in, pool_in = sem("rows_in"), sem("gate_in"), sem("pool_in")
        state_in, router_in, grow2_in = sem("state_in"), sem("router_in"), sem("grow2_in")
        gu_in = [sem(f"gu_in{s}") for s in range(SLOTS)]
        dn_in = [sem(f"dn_in{s}") for s in range(SLOTS)]
        gu_used = [sem(f"gu_used{s}") for s in range(SLOTS)]
        dn_used = [sem(f"dn_used{s}") for s in range(SLOTS)]
        out_sem, m_out = sem("out_sem"), sem("m_out")
        dve_own, act_own = sem("dve_own"), sem("act_own")
        zeroed, sc_ready, sq_ready, xn_ready = sem("zeroed"), sem("sc_ready"), sem("sq_ready"), sem("xn_ready")
        mod_ready, modT_done, modT_ready = sem("mod_ready"), sem("modT_done"), sem("modT_ready")
        mod_a_ready, h1_act, h1_dve = sem("mod_a_ready"), sem("h1_act"), sem("h1_dve")
        wgp_ready, gates_done, z_done, z_act, z_dve = (
            sem("wgp_ready"), sem("gates_done"), sem("z_done"), sem("z_act"), sem("z_dve"))
        abs_ready, soft_ready, scans_ready, w_ready, nat_ready = (
            sem("abs_ready"), sem("soft_ready"), sem("scans_ready"), sem("w_ready"), sem("nat_ready"))
        gT_done, gT_ready, em_ready, ktok_done, ktok_ready = (
            sem("gT_done"), sem("gT_ready"), sem("em_ready"), sem("ktok_done"), sem("ktok_ready"))
        w_hi_ready, w_lo_ready, half_used = sem("w_hi_ready"), sem("w_lo_ready"), sem("half_used")
        th_ready, tl_ready, mhi_ready = sem("th_ready"), sem("tl_ready"), sem("mhi_ready")
        dT_done, dT_ready, yp_done, yp_ready = sem("dT_done"), sem("dT_ready"), sem("yp_done"), sem("yp_ready")
        st_done, nm_done, masked, e_ready, p_ready = (
            sem("st_done"), sem("nm_done"), sem("masked"), sem("e_ready"), sem("p_ready"))
        pv_read, state_done = sem("pv_read"), sem("state_done")
        pv_done, nd_ready, unit_ready, kw_ready, c_ready = (
            sem("pv_done"), sem("nd_ready"), sem("unit_ready"), sem("kw_ready"), sem("c_ready"))
        yml_ready, mT_done, mT_ready, mods_out, mods_final = (
            sem("yml_ready"), sem("mT_done"), sem("mT_ready"), sem("mods_out"), sem("mods_final"))
        bc_in = [sem("bc_ctx_in"), sem("bc_lat_in")]
        wo_done, msq, tn_ready, x1_ready, xsq, hp_ready, hi_ready, lo_ready = (
            sem("wo_done"), sem("msq"), sem("tn_ready"), sem("x1_ready"), sem("xsq"), sem("hp_ready"),
            sem("hi_ready"), sem("lo_ready"))
        h2T_done, h2T_ready = sem("h2T_done"), sem("h2T_ready")
        logit_done, prob_ready, emask_ready, pos_done, item_ready, tab_done, tab_ready = (
            sem("logit_done"), sem("prob_ready"), sem("emask_ready"), sem("pos_done"), sem("item_ready"),
            sem("tab_done"), sem("tab_ready"))
        sh_gu_done = sem("sh_gu_done")
        silu_ready, a_ready, aT_done, actT_ready = (
            sem("silu_ready"), sem("a_ready"), sem("aT_done"), sem("actT_ready"))
        f_done, f_added = sem("f_done"), sem("f_added")
        oh_ready, gathered, hg_ready, wsl_ready = sem("oh_ready"), sem("gathered"), sem("hg_ready"), sem("wsl_ready")
        hgT_done, hgT_ready, ident_ready = sem("hgT_done"), sem("hgT_ready"), sem("ident_ready")
        ohT_done, ohT_ready, yhi_ready, y_ready = sem("ohT_done"), sem("ohT_ready"), sem("yhi_ready"), sem("y_ready")
        grow2_ready, gate_out, gate_rows_in, total_done, fsq, y_out = (
            sem("grow2_ready"), sem("gate_out"), sem("gate_rows_in"), sem("total_done"),
            sem("fsq"), sem("y_out"))

        mod_dram = nc.dram_tensor("mod_rows", [2, 12, 512], F32).ap()

        def rows_to_dram(engine, m, first, end, semaphore):
            engine.dma_start(mod_dram[m, first:end, :].rearrange("i (j x) -> j i x", j=4), modrow[m:m + 97:32, first:end, :])\
                .then_inc(semaphore, 16)

        def row_from_dram(engine, dst, m, first, semaphore):
            engine.dma_start(dst, mod_dram[m:m + 1, first:first + 2, :].rearrange("m i x -> m (i x)").broadcast_to([P, D]))\
                .then_inc(semaphore, 16)

        w_ada = t_in["w_ada"][0].rearrange("(p c) n -> p c n", c=NC)
        w_in = t_in["w_in"][0].rearrange("(c p) n -> p c n", p=P)
        w_out = t_in["w_out"][0].rearrange("(c p) n -> p c n", p=P)
        w_sgu = t_in["w_shared_gu"][0].rearrange("(p c) n -> p c n", c=NC)
        w_sdn = t_in["w_shared_down"][0].rearrange("(p j) n -> p j n", j=2)
        w_egu = t_in["w_expert_gu"][0].rearrange("e (p c) n -> e p c n", c=NC)
        w_edn = t_in["w_expert_down"][0].rearrange("e (p j) n -> e p j n", j=2)
        COL = {"u": 0, "q": MW, "k": 2 * MW, "v": 3 * MW, "o": 4 * MW}
        order = ["a0", "a1", "a2", "a3", "q", "a4", "a5", "k", "a6", "a7", "v", "a8", "a9", "o", "u",
                 "w0", "w1", "a10", "a11", "s"]
        chunk = {name: i for i, name in enumerate(order)}
        PRE = len(order) // SLOTS
        assert len(order) % SLOTS == 0 and chunk["s"] % SLOTS == SLOTS - 1

        def chunk_source(name):
            if name[0] == "a" and name != "a":
                i = int(name[1:])
                return w_ada[:, :, 512 * i:512 * (i + 1)]
            if name[0] == "w":
                i = int(name[1:])
                return w_out[:, :, 512 * i:512 * (i + 1)]
            if name == "s":
                return w_sgu
            return w_in[:, :, COL[name]:COL[name] + MW]

        def dn_base(s):
            return 1 if s == SLOTS - 1 else 0

        z_units = ([("q", i) for i in range(H)] + [("k", i) for i in range(H)] + [("v", i) for i in range(NT)]
                   + [("o", i) for i in range(NT)] + [("u", i) for i in range(NT)])
        by_act = [n for n, (w, _) in enumerate(z_units) if w in "qko"]
        by_dve = [n for n, (w, _) in enumerate(z_units) if w in "vu"]

        ends = {n: w for n, (w, _) in enumerate(z_units) if n + 1 == len(z_units) or z_units[n + 1][0] != w}

        def wait_chunk(engine, name):
            engine.wait_ge(gu_used[chunk[name] % SLOTS], chunk[name] // SLOTS + 1)

        def wait_unit(engine, n):
            if n in ends:
                wait_chunk(engine, ends[n])
            else:
                engine.wait_ge(z_done, n + 1 - sum(m < n for m in ends))

        def z_bank(n):
            return 2 + z_units[n][1]

        def before(n):
            same = [m for m in range(n) if z_units[m][1] == z_units[n][1]]
            return same[-1] if same else None

        SPLIT = [(w, half) for w in ("q", "k", "v", "o", "u", "w0", "w1") for half in range(2)]

        def half_free(engine, k):
            if k >= 2:
                w, half = SPLIT[k - 2]
                if half == 0:
                    engine.wait_ge(half_used, k // 2)
                else:
                    wait_chunk(engine, w)

        def low(engine, k):
            w, half = SPLIT[k]
            s = chunk[w] % SLOTS
            cs = slice(4 * half, 4 * half + 4)
            engine.wait_ge(w_hi_ready, k + 1)
            engine.tensor_tensor(w_lo[s][:, cs, :], w_gu[s][:, cs, :], w_hi[half][:, :, :].bitcast(F32), ALU.subtract)\
                .then_inc(w_lo_ready, 1)

        def three(t, out, lhs, rhs, start, stop):
            t.matmul(out, lhs[0], rhs[0], start=start, stop=False)
            t.matmul(out, lhs[0], rhs[1], start=False, stop=False)
            return t.matmul(out, lhs[1], rhs[0], start=False, stop=stop)

        SH_BANK = [0, 2, 4]
        STEPS = 7

        def natural(d, tile):
            if d == 0:
                return slice(P * tile, P * tile + P)
            first = T_CTX - 1 if tile == 0 else T - 1 - P * (tile - 1)
            last = first - P
            return slice(first, last if last >= 0 else None, -1)

        def blocks(d):
            return [(0, 0), (1, 1), (1, 2) if d == 0 else (2, 1), (2, 2)]

        def products(t, n):
            h, d = divmod(n, 2)
            row = H * d + h
            if n >= 1:
                t.wait_ge(c_ready, n)
            for i in range(1, NT):
                ins = t.matmul(bank(7, DV * (i - 1), DV * i), qT[:, h, P * i:P * i + P], c0n[:, row, :],
                               start=True, stop=True)
            t.wait_ge(kw_ready, n + 1)
            t.matmul(bank(7, 2 * DV, 3 * DV), kw[n % 2][:, :], v1[:, 0, h, :], start=True, stop=True).then_inc(state_done, 1)
            t.wait_ge(p_ready, n + 1)
            if n >= 1:
                t.wait_ge(pv_read, 2 * n)
            pt = p_t[n % 2]
            bl = blocks(d)
            for qs in range(NT):
                mine = [b for b in range(4) if bl[b][1] == qs]
                for b in mine:
                    ins = t.matmul(bank(6, DV * qs, DV * (qs + 1)), pt[:, b, :], v1[:, bl[b][0], h, :],
                                   start=(b == mine[0]), stop=(b == mine[-1]))
            ins.then_inc(pv_done, 1)

        block = ctx.enter_context(nc.Block())

        @block.sync
        def _(sp):
            for i in range(NT):
                src = t_in["x_prompt"][0] if i == 0 else t_in["x_sample"][0, P * (i - 1):P * i, :]
                sp.dma_start(x[:, i, :], src).then_inc(x_in, 16)
            for i, name in enumerate(order):
                s = i % SLOTS
                if i >= SLOTS:
                    sp.wait_ge(gu_used[s], i // SLOTS)
                sp.dma_start(w_gu[s][:, :, :], chunk_source(name)).then_inc(gu_in[s], 16)
                if name == "s":
                    wait_chunk(sp, "w1")
                    sp.dma_start(w_dn[s][:, :, :], w_sdn).then_inc(dn_in[s], 16)
            for e in range(SLOTS):
                sp.wait_ge(gu_used[e], PRE)
                sp.dma_start(w_gu[e][:, :, :], w_egu[e]).then_inc(gu_in[e], 16)
                if dn_base(e):
                    sp.wait_ge(dn_used[e], dn_base(e))
                sp.dma_start(w_dn[e][:, :, :], w_edn[e]).then_inc(dn_in[e], 16)
            with sp.Fori(1, NE // SLOTS) as it:
                for s in range(SLOTS):
                    sp.wait_ge(gu_used[s], it + PRE)
                    sp.dma_start(w_gu[s][:, :, :], w_egu[bass.ds(it * SLOTS + s, 1)].rearrange("e p c n -> p (e c) n"))\
                        .then_inc(gu_in[s], 16)
                    sp.wait_ge(dn_used[s], it + dn_base(s))
                    sp.dma_start(w_dn[s][:, :, :], w_edn[bass.ds(it * SLOTS + s, 1)].rearrange("e p j n -> p (e j) n"))\
                        .then_inc(dn_in[s], 16)
            sp.wait_ge(tab_ready, 1)
            n_pairs = sp.value_load(table_e[0:1, N_TAB:N_TAB + 1], min_val=0, max_val=OVER_PAIRS)

            def over_pair(jj, q):
                for half in range(2):
                    s = 2 * q + half
                    e = sp.value_load(table_e[0:1, bass.ds(jj * 4 + (NE + s), 1)], min_val=0, max_val=NE - 1)
                    sp.wait_ge(gu_used[s], jj + (PRE + NE // SLOTS))
                    sp.dma_start(w_gu[s][:, :, :], w_egu[bass.ds(e, 1)].rearrange("e p c n -> p (e c) n"))\
                        .then_inc(gu_in[s], 16)
                    sp.wait_ge(dn_used[s], jj + (NE // SLOTS + dn_base(s)))
                    sp.dma_start(w_dn[s][:, :, :], w_edn[bass.ds(e, 1)].rearrange("e p j n -> p (e j) n"))\
                        .then_inc(dn_in[s], 16)

            with sp.If(n_pairs > 0):
                over_pair(0, 0)
            with sp.Else():
                sp.nop()
            with sp.If(n_pairs > 1):
                over_pair(0, 1)
                with sp.Fori(1, OVER_PAIRS // 2) as jj:
                    for q in range(2):
                        with sp.If(jj * 2 + q < n_pairs):
                            over_pair(jj, q)
                        with sp.Else():
                            sp.nop()
            with sp.Else():
                sp.nop()
            for i in range(NT):
                sp.wait_ge(y_out, i + 1)
                dst = t_out[0][0] if i == 0 else t_out[1][0, P * (i - 1):P * i, :]
                sp.dma_start(dst, x[:, i, :]).then_inc(out_sem, 16)
            sp.wait_ge(out_sem, 16 * (NT + 2))
            sp.wait_ge(m_out, 32)

        @block.scalar
        def _(a):
            own = Chain(a, act_own)
            a.wait_ge(zeroed, 1)
            for m, name in enumerate(("c_ctx", "c")):
                src = (t_in["c_ctx"] if m == 0 else t_in["c"][0]).rearrange("(p c) -> p c", c=NC)
                a.dma_start(ct[:, m, :], src).then_inc(ct_in, 16)
            a.dma_start(const[:, :], t_in["shape_constants"]).then_inc(const_in, 16)
            a.wait_ge(ct_in, 32)
            a.activation(scT[:, :, 0:2], ct.rearrange("p m c -> p c m"), ACT.Silu).then_inc(sc_ready, 1)
            a.wait_ge(x_in, 16 * NT)
            for i in range(NT):
                own.link(a.activation(hT[:, 0:4, 0:D // 4], x[:, i, :].rearrange("p (a b) -> p a b", a=4), ACT.Square,
                                      accum_out=sum_sq[:, i:i + 1]))
            a.activation(sum_sq, sum_sq, ACT.Sqrt, bias=eps, scale=1.0 / D).then_inc(sq_ready, 1)
            def high(k):
                w, half = SPLIT[k]
                i = chunk[w]
                a.wait_ge(gu_in[i % SLOTS], 16 * (i // SLOTS + 1))
                half_free(a, k)
                a.activation(w_hi[half][:, :, :], w_gu[i % SLOTS][:, 4 * half:4 * half + 4, :], ACT.Copy)\
                    .then_inc(w_hi_ready, 1)

            a.wait_ge(modT_ready, 1)
            for c in range(NC // 2, NC):
                for m, (lo, hi) in enumerate(((0, T_CTX), (T_CTX, T))):
                    a.activation(hT[:, c, lo:hi], psum[:, T * c + lo:T * c + hi], ACT.Identity,
                                 bias=modT[:, 0, c, m:m + 1], scale=modT[:, 1, c, m:m + 1]).then_inc(h1_act, 1)

            high(0)
            a.wait_ge(h1_dve, NC)
            a.activation(tT_hi[0][:, :, :], hT[:, 0:4, :], ACT.Copy).then_inc(th_ready, 1)
            a.wait_ge(h1_act, NC)
            a.activation(tT_hi[1][:, :, :], hT[:, 4:8, :], ACT.Copy).then_inc(th_ready, 1)

            high(1)
            a.dma_start(poolm[:, :, :].rearrange("p g n -> p (g n)"), t_in["pool_constants"]).then_inc(pool_in, 16)
            a.dma_start(w_pool[:, :, :], t_in["w_pool"][0].rearrange("g c e -> c g e")).then_inc(pool_in, 16)
            a.dma_start(c0n[:, :, 0:DH], t_in["state_C"][0, 0].rearrange("d h k v -> k (d h) v")).then_inc(state_in, 16)
            with nc.allow_non_contiguous_dma(reason="a few hundred single values"):
                a.dma_start(pool_scale, t_in["pool_scale"][0].rearrange("(g e) -> e g", e=P)).then_inc(pool_in, 16)
                a.dma_start(c0n[:, :, DH:DV].rearrange("p r o -> p (r o)"),
                            t_in["state_n"][0, 0].rearrange("d h k -> k (d h)")).then_inc(state_in, 16)
            a.dma_start(w_router[:, :, :], t_in["w_router"][0].rearrange("(p c) n -> p c n", c=NC)).then_inc(router_in, 16)
            a.dma_start(b_router[:, :], t_in["b_router"][0:1, :].broadcast_to([P, NE])).then_inc(router_in, 16)

            def z_evac(n):
                w, i = z_units[n]
                wait_unit(a, n)
                if w == "q":
                    a.activation(qT[:, i, :], bank(z_bank(n), 0, T), ACT.Copy).then_inc(z_act, 1)
                elif w == "k":
                    a.activation(kT[:, i, :], bank(z_bank(n), 0, T), ACT.Copy, scale=DH ** -0.5).then_inc(z_act, 1)
                else:
                    a.activation(o_tok[:, i, :], bank(z_bank(n)), ACT.Sigmoid).then_inc(z_act, 1)

            a.wait_ge(abs_ready, 1)
            own.link(a.activation(g_t[:, :], g_t[:, :], ACT.Exp, scale=-1.0))
            a.activation(g_t[:, :], g_t[:, :], ACT.Ln, bias=1.0).then_inc(soft_ready, 1)
            high(2)
            for n in range(4):
                z_evac(n)
            high(3)
            a.wait_ge(scans_ready, 1)
            a.activation(g_t[:, 0:T_CTX], g_u[:, 0:T_CTX], ACT.Exp, bias=g_lf[:, T_CTX - 1:T_CTX]).then_inc(w_ready, 1)
            a.activation(g_t[:, T_CTX:T], g_lf[:, T_CTX:T], ACT.Exp, bias=m0).then_inc(w_ready, 1)
            for d in range(2):
                a.dma_start(t_out[4][0, 0, d].rearrange("(h o) -> h o", o=1),
                            g_b[32 * d:32 * d + H, T_CTX - 1:T_CTX]).then_inc(m_out, 16)
            high(4)
            for n in range(4, 8):
                z_evac(n)
            high(5)
            a.wait_ge(mod_a_ready, 1)
            for m in range(2):
                a.dma_start(grow[m:m + 97:32, 0, :, :], t_in["g_post_ffn"][0].rearrange("(i j x) -> j i x", i=2, j=4))\
                    .then_inc(grow2_in, 16)
            high(6)
            high(7)
            a.wait_ge(gT_ready, 1)
            a.activation(emT[:, :, :], gT[:, 1, :, :], ACT.Exp, scale=-1.0).then_inc(em_ready, 1)
            high(8)
            for n in range(11, 14):
                z_evac(n)
            high(9)
            high(10)
            high(11)
            a.wait_ge(ktok_done, 1)
            a.activation(k_tok[:, :], bank(0), ACT.Copy).then_inc(ktok_ready, 1)
            a.wait_ge(pool_in, 48)
            def pool_out(g):
                a.wait_ge(yp_done, g + 1)
                a.activation(hT[:, g, :], bank(4 + g % 2, 0, T), ACT.Copy, scale=pool_scale[:, g:g + 1])\
                    .then_inc(yp_ready, 1)

            for g in range(4):
                a.wait_ge(dT_done, g + 1)
                if g >= 2:
                    a.wait_ge(yp_done, g - 1)
                a.activation(dT[g % 2][:, :], bank(2 + g % 2, 0, T), ACT.Copy).then_inc(dT_ready, 1)
                if g >= 1:
                    pool_out(g - 1)
            pool_out(3)
            a.wait_ge(mods_final, 2)
            for m in range(2):
                rows_to_dram(a, m, 4, 10, mods_out)
            a.wait_ge(yp_ready, 4)
            a.activation(tT_hi[0][:, :, :], hT[:, 0:4, :], ACT.Copy).then_inc(th_ready, 1)

            def numerators(n):
                h, d = divmod(n, 2)
                row = H * d + h
                a.wait_ge(state_done, n + 1)
                if n >= 2:
                    a.wait_ge(unit_ready, n - 1)
                for i in range(1, NT):
                    a.activation(nd[n % 2][:, i, :], bank(7, DV * (i - 1), DV * i), ACT.Copy,
                                 scale=gT[:, 2, i, row:row + 1]).then_inc(nd_ready, 1)
                a.activation(c0n[:, row, :], bank(7, 2 * DV, 3 * DV), ACT.Copy).then_inc(c_ready, 1)

            def exponentials(n):
                h, d = divmod(n, 2)
                row = H * d + h
                if n >= 2:
                    a.wait_ge(state_done, n - 1)
                a.activation(kw[n % 2][:, :], k_tok[:, DH * h:DH * (h + 1)], ACT.Copy,
                             scale=gT[:, 2, 0, row:row + 1]).then_inc(kw_ready, 1)
                a.wait_ge(masked, n + 1)
                if n >= 2:
                    a.wait_ge(p_ready, n - 1)
                for b, (ks, qs) in enumerate(blocks(d)):
                    src = em[d][:, qs, :] if ks == qs else bank(4 + d, P * qs, P * qs + P)
                    ins = a.activation(e_t[n % 2][:, b, :], src, ACT.Exp, bias=gT[:, 0, ks, row:row + 1])
                ins.then_inc(e_ready, 1)

            exponentials(0)
            exponentials(1)
            for n in range(2 * H):
                numerators(n)
                if n + 2 < 2 * H:
                    exponentials(n + 2)
            own.link(a.activation(sum_sq2[:, 0:1], eps, ACT.Sqrt))
            a.wait_ge(c_ready, 2 * H)
            a.dma_start(t_out[2][0, 0].rearrange("d h k v -> k (d h) v"), c0n[:, :, 0:DH]).then_inc(out_sem, 16)
            with nc.allow_non_contiguous_dma(reason="a few hundred single values"):
                a.dma_start(t_out[3][0, 0].rearrange("d h k -> k (d h)"),
                            c0n[:, :, DH:DV].rearrange("p r o -> p (r o)")).then_inc(out_sem, 16)

            a.wait_ge(mods_out, 32)
            a.wait_ge(m_out, 32)
            a.wait_ge(unit_ready, 2 * H)
            for m in range(2):
                for k, first in enumerate((4, 8, 6)):
                    row_from_dram(a, bc[:, 3 * m + k, :], m, first, bc_in[m])
            for i in range(NT):
                a.wait_ge(mT_done, i + 1)
                a.activation(tT_hi[1][:, :, P * i:P * i + P], bank(6 + i % 2).rearrange("p (h t) -> p h t", h=H), ACT.Copy)\
                    .then_inc(mhi_ready, 1)

            def norm_mix(i):
                if i < NT - 1:
                    a.wait_ge(wo_done, i + 1)
                else:
                    wait_chunk(a, "w1")
                own.link(a.activation(junk[:, :], bank(2 * i, 0, 1024), ACT.Square, accum_out=sum_sq[:, i:i + 1]))
                a.activation(sum_sq[:, i:i + 1], sum_sq[:, i:i + 1], ACT.Sqrt, bias=eps, scale=1.0 / D)\
                    .then_inc(msq, 1)

            def norm_x1(i):
                a.wait_ge(x1_ready, i + 1)
                own.link(a.activation(junk[:, :], x[:, i, :], ACT.Square, accum_out=sum_sq2[:, i:i + 1]))
                a.activation(sum_sq2[:, i:i + 1], sum_sq2[:, i:i + 1], ACT.Sqrt, bias=eps, scale=1.0 / D)\
                    .then_inc(xsq, 1)

            def high_part(i):
                a.wait_ge(hp_ready, i + 1)
                a.activation(h_hi[:, i, :, :], hp[:, :, :], ACT.Copy).then_inc(hi_ready, 1)

            def h2T_evac(i):
                for half in range(2):
                    a.wait_ge(h2T_done, 2 * i + half + 1)
                    a.activation(hT[:, 4 * half:4 * half + 4, P * i:P * i + P],
                                 bank(2 * i + half).rearrange("p (c t) -> p c t", c=4), ACT.Copy).then_inc(h2T_ready, 1)

            def sh_silu(i):
                if i < NT - 1:
                    a.wait_ge(sh_gu_done, i + 1)
                else:
                    wait_chunk(a, "s")
                if i:
                    a.wait_ge(a_ready, i)
                a.activation(sil[:, :], bank(SH_BANK[i], 0, F), ACT.Silu).then_inc(silu_ready, 1)

            high(12)
            high(13)
            norm_mix(0)
            norm_x1(0)
            norm_mix(1)
            high_part(0)
            h2T_evac(0)
            norm_x1(1)
            norm_mix(2)
            high_part(1)
            h2T_evac(1)
            norm_x1(2)
            sh_silu(0)
            high_part(2)
            h2T_evac(2)
            a.wait_ge(logit_done, 1)
            a.activation(s_prob[:, :, :], bank(6, 0, NT * NE).rearrange("p (i e) -> p i e", i=NT), ACT.Sigmoid)\
                .then_inc(prob_ready, 1)

            def actT_evac(count):
                a.wait_ge(aT_done, count)
                a.activation(actT[:, :, :], bank(7, 0, F).rearrange("p (j s) -> p j s", j=2), ACT.Copy)\
                    .then_inc(actT_ready, 1)

            for i in range(NT):
                if i:
                    sh_silu(i)
                actT_evac(i + 1)

            def hg_evac(p):
                for n in range(2):
                    a.wait_ge(gathered, p * 2 + (n + 1))
                    a.activation(hg[:, n, :], bank(n), ACT.Copy).then_inc(hg_ready, 1)

            def hgT_evac(p):
                for n in range(2):
                    a.wait_ge(hgT_done, p * 2 + (n + 1))
                    a.activation(hgT[:, 4 * n:4 * n + 4, :].rearrange("p c s -> p (c s)"), bank(n), ACT.Copy)\
                        .then_inc(hgT_ready, 1)

            def pair(it, q):
                p = it * 2 + q
                sb = 2 * q + 1
                a.wait_ge(gu_used[sb], it + (PRE + 1))
                a.wait_ge(a_ready, p + NT)
                a.activation(sil[:, :], bank(2, 0, F), ACT.Silu).then_inc(silu_ready, 1)
                hg_evac(p + 1)
                actT_evac(p + (NT + 1))
                hgT_evac(p + 1)
                a.wait_ge(dn_used[sb], it + (1 + dn_base(sb)))
                a.activation(y_hi[:, :], bank(3, 0, 1024), ACT.Copy).then_inc(yhi_ready, 1)

            hg_evac(0)
            hgT_evac(0)
            with a.Fori(0, MAIN_PAIRS // 2) as it:
                for q in range(2):
                    pair(it, q)
            a.wait_ge(tab_ready, 1)
            n_pairs = a.value_load(table_e[0:1, N_TAB:N_TAB + 1], min_val=0, max_val=OVER_PAIRS)
            with a.If(n_pairs > 0):
                pair(MAIN_PAIRS // 2, 0)
            with a.Else():
                a.nop()
            with a.If(n_pairs > 1):
                pair(MAIN_PAIRS // 2, 1)
                with a.Fori(1, OVER_PAIRS // 2) as jj:
                    for q in range(2):
                        with a.If(jj * 2 + q < n_pairs):
                            pair(jj + MAIN_PAIRS // 2, q)
                        with a.Else():
                            a.nop()
            with a.Else():
                a.nop()
            own.link(a.activation(sum_sq2[:, 0:1], eps, ACT.Sqrt))
            for i in range(NT):
                a.wait_ge(total_done, i + 1)
                own.link(a.activation(hp[:, :, :].rearrange("p c q -> p (c q)"), bank(2 * i, 0, 1024), ACT.Square,
                                      accum_out=sum_sq[:, i:i + 1]))
                a.activation(sum_sq[:, i:i + 1], sum_sq[:, i:i + 1], ACT.Sqrt, bias=eps, scale=1.0 / D)\
                    .then_inc(fsq, 1)

        @block.vector
        def _(v):
            own = Chain(v, dve_own)
            own.add(v.memset(scT[:, :, :], 0.0))
            own.add(v.memset(small[:, :], 0.0))
            own.wait()
            v.memset(eps, EPS).then_inc(zeroed, 1)
            own.add(v.memset(modrow[:, :, :], 0.0))
            v.memset(grow[:, :, :, :], 0.0).then_inc(zeroed, 1)
            own.add(v.memset(wgp[:, :, :], 0.0))
            own.add(v.memset(v1[:, :, :, DH:DV], 1.0))
            own.wait()
            v.wait_ge(sq_ready, 1)
            own.link(v.reciprocal(rstd, sum_sq))
            for i in range(NT):
                v.tensor_scalar(xn[:, i, :], x[:, i, :], rstd[:, i:i + 1], None, ALU.mult).then_inc(xn_ready, 1)

            def ada_evac(i):
                if i == 0:
                    v.wait_ge(rows_in, 16 * 8)
                wait_chunk(v, f"a{max(i, 3)}")
                b = 6 + i % 2
                v.tensor_tensor(modrow[:, i, :], bank(b, P * (i % 4), P * (i % 4) + P), modrow[:, i, :], ALU.add)\
                    .then_inc(mod_ready, 1)

            def one_plus(i, g):
                return v.scalar_tensor_tensor(modrow[:, i:i + 2, :], modrow[:, i:i + 2, :], 1.0, grow[:, g, :, :],
                                              ALU.add, ALU.mult)

            for i in range(4):
                ada_evac(i)
            v.wait_ge(mod_ready, 4)
            one_plus(2, 0).then_inc(mod_a_ready, 1)
            v.wait_ge(gate_in, 16 * 5)
            for d in range(2):
                for g in range(2):
                    v.tensor_copy(wgp[:, :, 64 * g + 32 * d:64 * g + 32 * d + H], wgs[:, :, 8 * d + 4 * g:8 * d + 4 * g + H])\
                        .then_inc(wgp_ready, 1)
            v.wait_ge(modT_done, 1)
            v.tensor_copy(modT[:, :, :, :].rearrange("p a c m -> p (a c m)"), bank(6, P, P + 32)).then_inc(modT_ready, 1)
            v.wait_ge(modT_ready, 1)
            for c in range(NC // 2):
                for m, (lo, hi) in enumerate(((0, T_CTX), (T_CTX, T))):
                    v.tensor_scalar(hT[:, c, lo:hi], psum[:, T * c + lo:T * c + hi], modT[:, 1, c, m:m + 1],
                                    modT[:, 0, c, m:m + 1], ALU.mult, ALU.add).then_inc(h1_dve, 1)

            low(v, 0)
            for half in range(2):
                cs = slice(4 * half, 4 * half + 4)
                v.wait_ge(gates_done, half + 1)
                v.wait_ge(th_ready, half + 1)
                v.tensor_tensor(tT_lo[:, cs, :], hT[:, cs, :], tT_hi[half][:, :, :].bitcast(F32), ALU.subtract)\
                    .then_inc(tl_ready, 1)

            v.wait_ge(gates_done, 2)
            for b, dst in enumerate((g_in, g_lf)):
                own.add(v.tensor_scalar(dst[0:32, :], bank(0, 0, T)[64 * b:64 * b + 32, :], b_gate[0:32, b:b + 1], None, ALU.add))
                for tile in range(NT):
                    ins = v.tensor_scalar(dst[32:36, P * tile:P * tile + P],
                                          bank(0, 0, T)[64 * b + 32:64 * b + 36, natural(1, tile)],
                                          b_gate[32:36, b:b + 1], None, ALU.add)
                    own.add(ins)
            own.wait()
            v.scalar_tensor_tensor(g_t[:, :], g_lf[:, :], -1.0, g_lf[:, :], ALU.mult, ALU.max).then_inc(abs_ready, 1)
            own.link(v.tensor_scalar(g_lf[:, :], g_lf[:, :], 0.0, None, ALU.min))
            v.wait_ge(soft_ready, 1)
            own.link(v.tensor_tensor(g_lf[:, :], g_lf[:, :], g_t[:, :], ALU.subtract))
            SEG = ((0, T_CTX), (T_CTX, T))
            for lo, hi in SEG:
                own.add(v.tensor_tensor_scan(g_b[:, lo:hi], g_lf[:, lo:hi], g_lf[:, lo:hi], 0.0, ALU.add, ALU.bypass))
            own.wait()
            own.link(v.tensor_tensor(g_u[:, :], g_in[:, :], g_b[:, :], ALU.subtract))
            for (lo, hi), init in zip(SEG, (0.0, m0)):
                own.add(v.tensor_tensor_scan(g_mx[:, lo:hi], g_u[:, lo:hi], g_u[:, lo:hi], init, ALU.max, ALU.max))
            own.wait()
            own.add(v.tensor_scalar(g_lf[:, :], g_mx[:, :], -1.0, None, ALU.mult))
            own.wait()
            v.tensor_tensor(g_b[:, :], g_b[:, :], g_mx[:, :], ALU.add).then_inc(scans_ready, 1)
            v.wait_ge(scans_ready, 1)
            v.wait_ge(w_ready, 2)
            for n, rows in enumerate((g_u, g_b, g_t)):
                v.tensor_copy(g_nat[0:32, n, :], rows[0:32, :]).then_inc(nat_ready, 1)
                v.tensor_copy(g_nat[32:36, n, 0:T_CTX], rows[32:36, natural(1, 0)]).then_inc(nat_ready, 1)
                v.tensor_copy(g_nat[32:36, n, T_CTX:T], rows[32:36, T - 1:T_CTX - 1:-1]).then_inc(nat_ready, 1)
            for i in range(4, 8):
                ada_evac(i)
            for n in range(8, 11):
                wait_unit(v, n)
                v.tensor_copy(v1[:, z_units[n][1], :, 0:DH], bank(z_bank(n)).rearrange("p (h e) -> p h e", h=H))\
                    .then_inc(z_dve, 1)
            v.wait_ge(gT_done, 1)
            v.tensor_copy(gT[:, :, :, :].rearrange("p a i r -> p (a i r)"), bank(1, T, T + 72)).then_inc(gT_ready, 1)
            for i in range(8, 10):
                ada_evac(i)
            v.wait_ge(mod_ready, 10)
            v.tensor_tensor(modrow[:, 4:6, :], modrow[:, 4:6, :], grow[:, 1, :, :], ALU.mult).then_inc(mods_final, 1)
            one_plus(8, 2).then_inc(mods_final, 1)
            for n in range(14, 17):
                wait_unit(v, n)
                v.tensor_copy(u_tok[:, z_units[n][1], :], bank(z_bank(n))).then_inc(z_dve, 1)

            def outputs(n):
                h, d = divmod(n, 2)
                row = H * d + h
                t = nd[n % 2]
                v.wait_ge(nd_ready, (NT - 1) * (n + 1))
                v.wait_ge(pv_done, n + 1)
                v.tensor_tensor(t[:, 1:NT, :], t[:, 1:NT, :],
                                bank(6, DV, 3 * DV).rearrange("p (i e) -> p i e", i=2), ALU.add).then_inc(pv_read, 1)
                v.tensor_copy(t[:, 0, :], bank(6, 0, DV)).then_inc(pv_read, 1)
                v.wait_ge(pv_read, 2 * (n + 1))
                raw = t[:, :, DH:DV].rearrange("p i o -> p (i o)")
                own.link(v.scalar_tensor_tensor(den, raw, -1.0, raw, ALU.mult, ALU.max))
                own.link(v.tensor_tensor(den, den, emT[:, :, row:row + 1].rearrange("p i o -> p (i o)"), ALU.max))
                own.link(v.reciprocal(rden, den))
                for i in range(NT):
                    dst = hsum[:, i, DH * h:DH * (h + 1)]
                    if d == 0:
                        ins = v.tensor_scalar(dst, t[:, i, 0:DH], rden[:, i:i + 1], None, ALU.mult)
                    else:
                        ins = v.scalar_tensor_tensor(dst, t[:, i, 0:DH], rden[:, i:i + 1], dst, ALU.mult, ALU.add)
                    if i < NT - 1:
                        own.add(ins)
                ins.then_inc(unit_ready, 1)
                own.wait()

            v.wait_ge(em_ready, 1)
            v.wait_ge(yp_ready, 4)
            def masked_maxima(n):
                d = n % 2
                v.wait_ge(nm_done, n + 1)
                if n >= 2:
                    v.wait_ge(e_ready, n - 1)
                v.tensor_tensor(em[d][:, :, :], bank(4 + d, 0, T).rearrange("p (i t) -> p i t", i=NT),
                                mask(d).unsqueeze(1).broadcast_to([P, NT, P]), ALU.add).then_inc(masked, 1)

            def probabilities(n):
                h, d = divmod(n, 2)
                v.wait_ge(e_ready, n + 1)
                v.wait_ge(st_done, h + 1)
                if n >= 2:
                    v.wait_ge(pv_done, n - 1)
                sa, sb = 2 * (h % 2), 2 * (h % 2) + 1
                cut = 3 if d == 0 else 2
                rest = bank(sb, P * (cut - 2), 2 * P)
                own.add(v.tensor_tensor(p_t[n % 2][:, 0:cut, :], e_t[n % 2][:, 0:cut, :],
                                        bank(sa, 0, P * cut).rearrange("p (b t) -> p b t", b=cut), ALU.mult))
                v.tensor_tensor(p_t[n % 2][:, cut:4, :], e_t[n % 2][:, cut:4, :],
                                rest.rearrange("p (b t) -> p b t", b=4 - cut), ALU.mult).then_inc(p_ready, 1)

            masked_maxima(0)
            masked_maxima(1)
            for n in range(2 * H):
                probabilities(n)
                if n >= 1:
                    outputs(n - 1)
                if n + 2 < 2 * H:
                    masked_maxima(n + 2)
            outputs(2 * H - 1)
            v.wait_ge(unit_ready, 2 * H)
            for i in range(NT):
                v.tensor_tensor(hsum[:, i, :], hsum[:, i, :], o_tok[:, i, :], ALU.mult).then_inc(yml_ready, 1)

            for i in range(NT):
                v.wait_ge(mhi_ready, i + 1)
                v.tensor_tensor(tT_lo[:, 4:8, P * i:P * i + P], bank(6 + i % 2).rearrange("p (h t) -> p h t", h=H),
                                tT_hi[1][:, :, P * i:P * i + P].bitcast(F32), ALU.subtract).then_inc(mT_ready, 1)

            def bcast(k, i):
                return bc[:, k + 3 * (i > 0), :]

            def mix_normed(i):
                v.wait_ge(msq, i + 1)
                own.link(v.reciprocal(rstd[:, i:i + 1], sum_sq[:, i:i + 1]))
                v.wait_ge(bc_in[min(i, 1)], 48)
                if i:
                    v.wait_ge(x1_ready, i)
                v.scalar_tensor_tensor(tn[:, :], bank(2 * i, 0, 1024), rstd[:, i:i + 1], bcast(0, i), ALU.mult, ALU.mult)\
                    .then_inc(tn_ready, 1)

            def modulated(i):
                v.wait_ge(xsq, i + 1)
                own.link(v.reciprocal(rstd2[:, i:i + 1], sum_sq2[:, i:i + 1]))
                if i:
                    v.wait_ge(h2T_done, 2 * i)
                    v.wait_ge(hi_ready, i)
                    v.wait_ge(lo_ready, i)
                flat = hp[:, :, :].rearrange("p c q -> p q c")
                own.link(v.scalar_tensor_tensor(flat, x[:, i, :].rearrange("p (q c) -> p q c", c=NC), rstd2[:, i:i + 1],
                                                bcast(1, i).rearrange("p (q c) -> p q c", c=NC), ALU.mult, ALU.mult))
                v.tensor_tensor(flat, flat, bcast(2, i).rearrange("p (q c) -> p q c", c=NC), ALU.add).then_inc(hp_ready, 1)

            def residual(i):
                v.wait_ge(tn_ready, i + 1)
                v.tensor_tensor(x[:, i, :], x[:, i, :], tn[:, :], ALU.add).then_inc(x1_ready, 1)

            def low_part(i):
                v.wait_ge(hi_ready, i + 1)
                v.tensor_tensor(h_lo[:, i, :, :], hp[:, :, :], h_hi[:, i, :, :].bitcast(F32), ALU.subtract)\
                    .then_inc(lo_ready, 1)

            mix_normed(0)
            residual(0)
            mix_normed(1)
            modulated(0)
            residual(1)
            ada_evac(10)
            ada_evac(11)
            low_part(0)
            v.wait_ge(mod_ready, 12)
            mix_normed(2)
            modulated(1)
            residual(2)
            low_part(1)
            modulated(2)
            low_part(2)

            def sh_a(i):
                v.wait_ge(silu_ready, i + 1)
                if i:
                    v.wait_ge(aT_done, i)
                v.tensor_tensor(act[:, :, :].rearrange("s j q -> s q j"), sil[:, :].rearrange("s (q j) -> s q j", j=2),
                                bank(SH_BANK[i], F, 2 * F).rearrange("s (q j) -> s q j", j=2), ALU.mult)\
                    .then_inc(a_ready, 1)

            sh_a(0)
            v.wait_ge(prob_ready, 1)
            v.wait_ge(router_in, 32)
            own.link(v.tensor_tensor(biased[:, :, :], s_prob[:, :, :], b_router[:, :].unsqueeze(1).broadcast_to([P, NT, NE]),
                                     ALU.add))
            for i in range(NT):
                for g in range(NG):
                    own.add(v.max(top2[:, NG * i + g, :], biased[:, i, NG * g:NG * g + NG]))
            own.add(v.memset(gext[:, :, NG:NG + 4], BIG))
            own.add(v.memset(ext[:, :, NE:NE + 2], BIG))
            own.wait()
            own.link(v.tensor_tensor(gext[:, :, 0:NG], top2[:, :, 0:1].rearrange("p (i g) o -> p i (g o)", i=NT),
                                     top2[:, :, 1:2].rearrange("p (i g) o -> p i (g o)", i=NT), ALU.add))
            for i in range(NT):
                own.add(v.max(best[:, i, :], gext[:, i, 0:NG]))
            own.wait()
            own.link(v.memset(best[:, :, TOPG:8], BIG))
            for i in range(NT):
                own.add(v.match_replace(gout[:, i, :], best[:, i, :], gext[:, i, :], NEG))
            own.wait()
            gsel = gout[:, :, 0:NG]
            own.link(v.tensor_scalar(gsel, gsel, NEG, None, ALU.is_equal))
            own.link(v.tensor_scalar(gext[:, :, 0:NG], gsel, BIG, NEG, ALU.mult, ALU.add))
            for i in range(NT):
                own.add(v.tensor_tensor(ext[:, i, 0:NE].rearrange("p (g e) -> p g e", g=NG),
                                        biased[:, i, :].rearrange("p (g e) -> p g e", g=NG),
                                        gsel[:, i, :].unsqueeze(2).broadcast_to([P, NG, NE // NG]), ALU.mult))
            own.wait()
            for i in range(NT):
                own.add(v.tensor_tensor(ext[:, i, 0:NE].rearrange("p (g e) -> p g e", g=NG),
                                        ext[:, i, 0:NE].rearrange("p (g e) -> p g e", g=NG),
                                        gext[:, i, 0:NG].unsqueeze(2).broadcast_to([P, NG, NE // NG]), ALU.add))
            own.wait()
            for i in range(NT):
                own.add(v.max(best[:, i, :], ext[:, i, 0:NE]))
            own.wait()
            own.link(v.memset(best[:, :, TOPK:8], BIG))
            for i in range(NT):
                own.add(v.match_replace(chosen[:, i, :], best[:, i, :], ext[:, i, :], 3 * NEG))
            own.wait()
            v.tensor_scalar(emask[:, :, :], chosen[:, :, 0:NE], 3 * NEG, None, ALU.is_equal).then_inc(emask_ready, 1)
            v.wait_ge(emask_ready, 1)

            def f_first(i):
                if i == 0:
                    v.wait_ge(out_sem, 32)
                for n in range(2):
                    if (i, n) != (NT - 1, 1):
                        v.wait_ge(f_done, 2 * i + n + 1)
                    else:
                        v.wait_ge(dn_used[SLOTS - 1], 1)
                    v.tensor_copy(f_acc[:, i, 512 * n:512 * (n + 1)], bank(5 + n)).then_inc(f_added, 1)

            sh_a(1)
            v.wait_ge(grow2_in, 32)
            v.tensor_tensor(modrow[:, 10:12, :], modrow[:, 10:12, :], grow[:, 0, :, :], ALU.mult).then_inc(grow2_ready, 1)
            own.link(v.tensor_tensor(comb[:, :, :], s_prob[:, :, :], emask[:, :, :], ALU.mult))
            own.link(v.tensor_reduce(wsum, comb[:, :, :], AX.X, ALU.add))
            own.link(v.reciprocal(wsum, wsum))
            for i in range(NT):
                own.add(v.tensor_scalar(comb[:, i, :], comb[:, i, :], wsum[:, i:i + 1], ROUTED_SCALE, ALU.mult, ALU.mult))
            own.wait()
            own.link(v.tensor_copy(comb2[:, :, :, 0], comb[:, :, :]))
            own.link(v.tensor_tensor(comb2[:, :, :, 1], comb[:, :, :], comb2[:, :, :, 0].bitcast(F32), ALU.subtract))
            v.wait_ge(pos_done, 1)
            ranks = bank(3, 0, NT * NE).rearrange("p (i e) -> p i e", i=NT)
            own.link(v.scalar_tensor_tensor(posm[:, :, :], ranks, 1.0, emask[:, :, :], ALU.add, ALU.mult))
            own.link(v.tensor_scalar(posm[:, :, :], posm[:, :, :], -1.0, None, ALU.add))
            own.add(v.tensor_copy(table_e[0:1, 0:NE], const[0:1, C_IOTA:C_IOTA + NE]))
            own.add(v.memset(rank0[:, 0:NE], 0.0))
            own.wait()

            def make_onehot(p, par):
                for half in range(2):
                    item = p * 2 + half
                    e = v.value_load(table_e[0:1, bass.ds(item, 1)], min_val=0, max_val=NE - 1)
                    own.add(v.tensor_copy(ident_w[:, :, P + 2 * half:P + 2 * half + 2],
                                          comb2[:, :, bass.ds(e, 1), :].rearrange("p i o w -> p i (o w)")))
                    for i in range(NT):
                        ins = v.tensor_scalar(onehot[par][:, i, CAP * half:CAP * (half + 1)], iota,
                                              rank0[:, bass.ds(item, 1)], posm[:, i, bass.ds(e, 1)], ALU.add, ALU.is_equal)
                        if (half, i) != (1, NT - 1):
                            own.add(ins)
                ins.then_inc(oh_ready, 1)

            def onehot_T(p, par):
                v.wait_ge(ohT_done, p + 1)
                tiles = bank(2, 0, (P + 4) * NT).rearrange("p (i x) -> p i x", i=NT)
                v.tensor_copy(onehotT[par][:, :, :], tiles[:, :, 0:P]).then_inc(ohT_ready, 1)
                for half in range(2):
                    q = slice(CAP * half, CAP * (half + 1))
                    v.tensor_reduce(wsl[q, par:par + 1], tiles[q, :, P + 2 * half:P + 2 * half + 2], AX.XY, ALU.add)\
                        .then_inc(wsl_ready, 1)

            counts = bank(3, NT * NE, NT * NE + NE)[0:NE, :]
            for r in range(ROUNDS):
                own.add(v.tensor_scalar(flags[:, r, :], counts, float(CAP * (r + 1)), None, ALU.is_gt))
            own.wait()
            fl = flags[:, :, :].rearrange("p r e -> p (r e)")
            ix = index[:, :, :].rearrange("p r e -> p (r e)")
            own.link(v.tensor_tensor_scan(ix, fl, fl, 0.0, ALU.add, ALU.bypass))
            mt = match[:, :, :].rearrange("p r e -> p (r e)")
            own.link(v.scalar_tensor_tensor(mt, ix, const[0:NE, C_RANK:C_RANK + 1], fl, ALU.is_equal, ALU.mult))
            f_first(0)
            sh_a(2)
            make_onehot(0, 0)
            f_first(1)
            onehot_T(0, 0)
            own.link(v.tensor_tensor(match2[:, :, :], match[:, :, :],
                                     const[0:NE, C_IOTA:C_IOTA + NE].unsqueeze(1).broadcast_to([NE, ROUNDS, NE]), ALU.mult))
            own.link(v.tensor_reduce(items[:, 0:1], match2[:, :, :].rearrange("p r e -> p (r e)"), AX.X, ALU.add))
            own.link(v.tensor_tensor(match2[:, :, :], match[:, :, :],
                                     const[0:NE, C_ROUND:C_END].unsqueeze(2).broadcast_to([NE, ROUNDS, NE]), ALU.mult))
            own.link(v.tensor_reduce(items[:, 1:2], match2[:, :, :].rearrange("p r e -> p (r e)"), AX.X, ALU.add))
            own.link(v.tensor_scalar(items[:, 1:2], items[:, 1:2], FAR, None, ALU.add))
            own.add(v.tensor_scalar(diag_e[:, :], ident[0:NE, 0:NE], items[:, 0:1], None, ALU.mult))
            v.tensor_scalar(diag_r[:, :], ident[0:NE, 0:NE], items[:, 1:2], None, ALU.mult).then_inc(item_ready, 1)
            v.wait_ge(tab_done, 1)
            own.add(v.tensor_copy(table_e[0:1, NE:N_TAB], bank(4, 0, N_TAB - NE)[0:1, :]))
            own.add(v.tensor_copy(rank0[:, NE:N_TAB], bank(4, NE, NE + N_TAB - NE)))
            own.link(v.tensor_scalar(match[0:1, 0, 0:OVER_PAIRS], const[0:1, C_IOTA:C_IOTA + OVER_PAIRS], 2.0,
                                     index[0:1, ROUNDS - 1, NE - 1:NE], ALU.mult, ALU.is_lt))
            own.link(v.tensor_reduce(items[0:1, 2:3], match[0:1, 0, 0:OVER_PAIRS], AX.X, ALU.add))
            by_parity = match[0:1, 0, 0:OVER_PAIRS + OVER_PAIRS % 2].rearrange("p (n two) -> p two n", two=2)
            own.link(v.tensor_reduce(items[0:1, 3:5], by_parity, AX.X, ALU.add))
            own.link(v.tensor_tensor(items[0:1, 3:4], items[0:1, 3:4], items[0:1, 4:5], ALU.subtract))
            own.link(v.tensor_copy(table_e[0:1, N_TAB + 1:N_TAB + 2], items[0:1, 3:4]))
            v.tensor_copy(table_e[0:1, N_TAB:N_TAB + 1], items[0:1, 2:3]).then_inc(tab_ready, 1)
            v.wait_ge(tab_ready, 1)
            own.wait()

            f_first(2)
            count0 = own.count

            def pair(it, q):
                p = it * 2 + q
                own.count = it * (2 * STEPS) + (count0 + q * STEPS)
                v.wait_ge(ohT_done, p + 1)
                make_onehot(p + 1, (q + 1) % 2)
                v.wait_ge(silu_ready, p + (NT + 1))
                v.wait_ge(aT_done, p + NT)
                v.wait_ge(wsl_ready, p * 2 + 2)
                v.scalar_tensor_tensor(act[:, :, :].rearrange("s j q -> s q j"), sil[:, :].rearrange("s (q j) -> s q j", j=2),
                                       wsl[:, q:q + 1], bank(2, F, 2 * F).rearrange("s (q j) -> s q j", j=2),
                                       ALU.mult, ALU.mult).then_inc(a_ready, 1)
                f_add(p)
                onehot_T(p + 1, (q + 1) % 2)
                v.wait_ge(yhi_ready, p + 1)
                v.wait_ge(y_ready, p + 1)
                v.tensor_tensor(y_lo[:, :], bank(3, 0, 1024), y_hi[:, :].bitcast(F32), ALU.subtract).then_inc(y_ready, 1)

            def f_add(p):
                for c in range(6):
                    i, n = divmod(c, 2)
                    v.wait_ge(f_done, p * 6 + (5 + c + 1))
                    v.wait_ge(f_added, p * 6 + (c + 1))
                    dst = f_acc[:, i, 512 * n:512 * (n + 1)]
                    v.tensor_tensor(dst, dst, bank(5 + n), ALU.add).then_inc(f_added, 1)

            with v.Fori(0, MAIN_PAIRS // 2) as it:
                for q in range(2):
                    pair(it, q)
            n_pairs = v.value_load(table_e[0:1, N_TAB:N_TAB + 1], min_val=0, max_val=OVER_PAIRS)
            with v.If(n_pairs > 0):
                pair(MAIN_PAIRS // 2, 0)
            with v.Else():
                v.nop()
            with v.If(n_pairs > 1):
                pair(MAIN_PAIRS // 2, 1)
                with v.Fori(1, OVER_PAIRS // 2) as jj:
                    for q in range(2):
                        with v.If(jj * 2 + q < n_pairs):
                            pair(jj + MAIN_PAIRS // 2, q)
                        with v.Else():
                            v.nop()
            with v.Else():
                v.nop()
            own.count = n_pairs * STEPS + (count0 + STEPS * MAIN_PAIRS)
            v.wait_ge(gate_rows_in, 32)

            def gated(i):
                v.wait_ge(fsq, i + 1)
                own.link(v.tensor_tensor(hg[:, :, :].rearrange("p n x -> p (n x)"), bank(2 * i, 0, 1024),
                                         gate_rows[:, min(i, 1), :], ALU.mult))

            def result(i):
                own.link(v.reciprocal(rstd[:, i:i + 1], sum_sq[:, i:i + 1]))
                v.scalar_tensor_tensor(x[:, i, :], hg[:, :, :].rearrange("p n x -> p (n x)"), rstd[:, i:i + 1], x[:, i, :],
                                       ALU.mult, ALU.add)\
                    .then_inc(y_out, 1)
                v.wait_ge(y_out, i + 1)

            for i in range(NT):
                gated(i)
                result(i)

        @block.gpsimd
        def _(g):
            g.wait_ge(zeroed, 2)
            ada_rows = t_in["b_ada"][0].rearrange("(i j x) -> j i x", i=12, j=4)
            for m in range(2):
                g.dma_start(modrow[m:m + 97:32, :, :], ada_rows).then_inc(rows_in, 16)
                for n, name in enumerate(("g_pre_mix", "g_post_mix", "g_pre_ffn")):
                    g.dma_start(grow[m:m + 97:32, n, :, :], t_in[name][0].rearrange("(i j x) -> j i x", i=2, j=4))\
                        .then_inc(rows_in, 16)
            g.dma_start(wgs[:, :, :], w_in[:, :, 5 * MW:5 * MW + 16]).then_inc(gate_in, 16)
            with nc.allow_non_contiguous_dma(reason="a few single gate and state values"):
                for d in range(2):
                    g.dma_start(b_gate[32 * d:32 * d + H, :], t_in["b_gate"][0, d].rearrange("g h -> h g"))\
                        .then_inc(gate_in, 16)
                    g.dma_start(m0[32 * d:32 * d + H, :], t_in["state_m"][0, 0, d].rearrange("(h o) -> h o", o=1))\
                        .then_inc(gate_in, 16)

            g.wait_ge(w_lo_ready, 1)
            for k in range(1, 12):
                low(g, k)
            g.wait_ge(th_ready, 3)
            g.tensor_tensor(tT_lo[:, 0:4, :], hT[:, 0:4, :], tT_hi[0][:, :, :].bitcast(F32), ALU.subtract).then_inc(tl_ready, 1)
            low(g, 12)
            low(g, 13)
            g.wait_ge(hp_ready, NT)
            g.memset(y_hi[:, :].bitcast(F32), 0.0).then_inc(zeroed, 1)
            g.memset(y_lo[:, :].bitcast(F32), 0.0).then_inc(zeroed, 1)
            g.wait_ge(mods_final, 2)
            for i in range(NT):
                g.tensor_copy(ident_w[:, i, 0:P], ident).then_inc(zeroed, 1)
            g.wait_ge(zeroed, 4 + NT)
            g.nop().then_inc(ident_ready, 1)
            g.wait_ge(emask_ready, 1)
            g.memset(onehotT[1][:, :, :].bitcast(F32), 0.0).then_inc(y_ready, 1)
            g.wait_ge(grow2_ready, 1)
            for m in range(2):
                rows_to_dram(g, m, 10, 12, gate_out)
            g.wait_ge(gate_out, 32)
            wait_chunk(g, "s")
            for m in range(2):
                row_from_dram(g, gate_rows[:, m, :], m, 10, gate_rows_in)

        @block.tensor
        def _(t):
            def ada(i):
                n = chunk[f"a{i}"]
                s = n % SLOTS
                if i == 0:
                    t.wait_ge(sc_ready, 1)
                t.wait_ge(gu_in[s], 16 * (n // SLOTS + 1))
                b = 6 + i % 2
                if i >= 4:
                    t.wait_ge(mod_ready, max(i - 1, 4))
                for c in range(NC):
                    for j in range(4):
                        ins = t.matmul(bank(b, P * (i % 4), P * (i % 4) + P)[32 * j:32 * j + 32, :],
                                       scT[:, c, :], w_gu[s][:, c, P * j:P * j + P],
                                       start=(c == 0), stop=(c == NC - 1), tile_position=(0, 32 * j))
                ins.then_inc(gu_used[s], 1)

            ada(0)
            ada(1)
            t.wait_ge(const_in, 16)
            for i in range(NT):
                t.wait_ge(xn_ready, i + 1)
                for c in range(NC):
                    ins = t.transpose(psum[:, T * c + P * i:T * c + P * i + P], xn[:, i, P * c:P * c + P], ident)
            ada(2)
            ada(3)
            t.wait_ge(mod_a_ready, 1)
            for i in range(4):
                ins = t.matmul(bank(6, P + 8 * i, P + 8 * i + 8), modrow[:, i, :],
                               ident.rearrange("p (j r) -> p j r", j=4)[:, :, 0:2], start=True, stop=True)
            ins.then_inc(modT_done, 1)

            t.wait_ge(wgp_ready, 4)
            t.wait_ge(h1_act, NC)
            t.wait_ge(h1_dve, NC)
            for c in range(NC):
                ins = t.matmul(bank(0, 0, T)[0:100, :], wgp[:, c, :], hT[:, c, :], start=(c == 0), stop=(c == NC - 1))
                if c % 4 == 3:
                    ins.then_inc(gates_done, 1)

            def z_chunk(w):
                units = [n for n, (name, _) in enumerate(z_units) if name == w]
                s = chunk[w] % SLOTS
                for half in range(2):
                    t.wait_ge(w_lo_ready, SPLIT.index((w, half)) + 1)
                    if w == "q":
                        t.wait_ge(tl_ready, half + 1)
                    for n in units:
                        i = z_units[n][1]
                        prior = before(n)
                        if half == 0 and prior is not None:
                            if prior in by_act:
                                t.wait_ge(z_act, by_act.index(prior) + 1)
                            else:
                                t.wait_ge(z_dve, by_dve.index(prior) + 1)
                        for j in range(4):
                            c = 4 * half + j
                            if w in "qk":
                                cols = slice(DH * i, DH * (i + 1))
                                ins = three(t, bank(z_bank(n), 0, T), (w_hi[half][:, j, cols], w_lo[s][:, c, cols]),
                                            (tT_hi[half][:, j, :], tT_lo[:, c, :]), c == 0, c == NC - 1)
                            else:
                                cols = slice(P * i, P * (i + 1))
                                ins = three(t, bank(z_bank(n)), (tT_hi[half][:, j, cols], tT_lo[:, c, cols]),
                                            (w_hi[half][:, j, :], w_lo[s][:, c, :]), c == 0, c == NC - 1)
                        if half:
                            ins.then_inc(gu_used[s] if n in ends else z_done, 1)
                    if half == 0:
                        ins.then_inc(half_used, 1)

            for w in "qkvou":
                z_chunk(w)
                if w == "q":
                    ada(4)
                    ada(5)
                if w == "k":
                    ada(6)
                    ada(7)
                if w == "v":
                    t.wait_ge(w_ready, 2)
                    t.wait_ge(nat_ready, 9)
                    for a_ in range(3):
                        for tile in range(NT):
                            col = T + 24 * a_ + 8 * tile
                            ins = t.matmul(bank(1, col, col + 2 * H), g_nat[:, a_, P * tile:P * tile + P],
                                           ident[0:36, 0:64].rearrange("p (d r) -> p d r", d=2)[:, :, 0:H],
                                           start=True, stop=True)
                    ins.then_inc(gT_done, 1)
                    ada(8)
                    ada(9)
            t.wait_ge(z_act, 8)
            t.wait_ge(abs_ready, 1)
            for h in range(H):
                ins = t.transpose(bank(0, DH * h, DH * (h + 1)), kT[:, h, 0:P], ident)
            ins.then_inc(ktok_done, 1)
            t.wait_ge(pool_in, 48)
            t.wait_ge(z_act, 11)
            t.wait_ge(z_dve, 6)
            def differences(g):
                if g >= 2:
                    t.wait_ge(dT_ready, g - 1)
                cols = slice(P * g, P * g + P)
                b = bank(2 + g % 2, 0, T)
                t.matmul(b[:, 0:T_CTX], u_tok[:, 0, cols], poolm[:, g, 0:T_CTX], start=True, stop=True)
                for k in range(2):
                    ins = t.matmul(b[:, T_CTX:T], u_tok[:, 1 + k, cols],
                                   poolm[:, g, T_CTX + T_LAT * k:T_CTX + T_LAT * (k + 1)], start=(k == 0), stop=(k == 1))
                ins.then_inc(dT_done, 1)

            differences(0)
            for g in range(4):
                if g < 3:
                    differences(g + 1)
                t.wait_ge(dT_ready, g + 1)
                if g >= 2:
                    t.wait_ge(yp_ready, g - 1)
                t.matmul(bank(4 + g % 2, 0, T), w_pool[:, g, :], dT[g % 2][:, :], start=True, stop=True).then_inc(yp_done, 1)

            t.wait_ge(state_in, 32)
            t.wait_ge(yp_ready, 4)
            t.wait_ge(ktok_ready, 1)
            t.wait_ge(mod_ready, 10)
            def scores(h):
                if h >= 2:
                    t.wait_ge(p_ready, 2 * (h - 1))
                sa, sb = 2 * (h % 2), 2 * (h % 2) + 1
                t.matmul(bank(sa, 0, P), kT[:, h, 0:P], qT[:, h, 0:P], start=True, stop=True)
                t.matmul(bank(sa, P, 3 * P), kT[:, h, P:2 * P], qT[:, h, P:T], start=True, stop=True)
                t.matmul(bank(sb, 0, 2 * P), kT[:, h, 2 * P:T], qT[:, h, P:T], start=True, stop=True)\
                    .then_inc(st_done, 1)

            def minus_maxima(n):
                h, d = divmod(n, 2)
                if n >= 2:
                    t.wait_ge(e_ready, n - 1)
                q = slice(32 * d, 32 * d + H)
                for tile in range(NT):
                    ins = t.matmul(bank(4 + d, P * tile, P * tile + P),
                                   const[q, C_IDENT + 32 * d + h:C_IDENT + 32 * d + h + 1].broadcast_to([H, P]),
                                   g_lf[q, natural(d, tile)], start=True, stop=True)
                ins.then_inc(nm_done, 1)

            minus_maxima(0)
            minus_maxima(1)
            scores(0)
            scores(1)
            for n in range(2 * H):
                if n + 2 < 2 * H:
                    minus_maxima(n + 2)
                products(t, n)
                if n % 2 and n // 2 + 2 < H:
                    scores(n // 2 + 2)

            def wo_step(n, half, i):
                s = chunk[f"w{n}"] % SLOTS
                for j in range(4):
                    c = 4 * half + j
                    cols = slice(P * i, P * (i + 1))
                    ins = three(t, bank(2 * i + n), (tT_hi[half][:, j, cols], tT_lo[:, c, cols]),
                                (w_hi[half][:, j, :], w_lo[s][:, c, :]), c == 0, c == NC - 1)
                if half == 0 and i == NT - 1:
                    ins.then_inc(half_used, 1)
                elif half == 1 and i == NT - 1:
                    ins.then_inc(gu_used[s], 1)
                elif half == 1 and n == 1:
                    ins.then_inc(wo_done, 1)

            t.wait_ge(w_lo_ready, SPLIT.index(("w0", 0)) + 1)
            t.wait_ge(tl_ready, 3)
            t.wait_ge(p_ready, 2 * H)
            for i in range(NT):
                wo_step(0, 0, i)
            for i in range(NT):
                t.wait_ge(yml_ready, i + 1)
                if i == 0:
                    t.wait_ge(unit_ready, 2 * H)
                    t.wait_ge(c_ready, 2 * H)
                if i == 2:
                    t.wait_ge(mT_ready, 1)
                for h in range(H):
                    ins = t.transpose(bank(6 + i % 2, P * h, P * h + P), hsum[:, i, DH * h:DH * (h + 1)], ident)
                ins.then_inc(mT_done, 1)

            rest = [(0, 1), (1, 0), (1, 1)]
            for step in range(3 * NT):
                (n, half), i = rest[step // NT], step % NT
                if step < NT:
                    t.wait_ge(mT_ready, i + 1)
                if i == 0:
                    t.wait_ge(w_lo_ready, SPLIT.index((f"w{n}", half)) + 1)
                wo_step(n, half, i)

            s_sh = SLOTS - 1

            def tokens_T(i):
                t.wait_ge(hp_ready, i + 1)
                for c in range(NC):
                    ins = t.transpose(bank(2 * i, P * c, P * c + P), hp[:, c, :], ident)
                    if c % 4 == 3:
                        ins.then_inc(h2T_done, 1)

            def sh_gu(i):
                t.wait_ge(gu_in[s_sh], 16 * PRE)
                for c in range(NC):
                    if c % 4 == 0:
                        t.wait_ge(h2T_ready, 2 * i + c // 4 + 1)
                    ins = t.matmul(bank(SH_BANK[i]), hT[:, c, P * i:P * i + P], w_gu[s_sh][:, c, :],
                                   start=(c == 0), stop=(c == NC - 1))
                ins.then_inc(sh_gu_done if i < NT - 1 else gu_used[s_sh], 1)

            def transposes(count):
                t.wait_ge(a_ready, count)
                for j in range(2):
                    ins = t.transpose(bank(7, P * j, P * j + P), act[:, j, :], ident)
                ins.then_inc(aT_done, 1)

            def sh_down(i):
                t.wait_ge(actT_ready, i + 1)
                t.wait_ge(dn_in[s_sh], 16)
                for n in range(2):
                    if i:
                        t.wait_ge(f_added, 2 * (i - 1) + n + 1)
                    for j in range(2):
                        ins = t.matmul(bank(5 + n), actT[:, j, :], w_dn[s_sh][:, j, 512 * n:512 * (n + 1)],
                                       start=(j == 0), stop=(j == 1))
                    ins.then_inc(f_done if (i, n) != (NT - 1, 1) else dn_used[s_sh], 1)

            t.wait_ge(mT_ready, NT)
            ada(10)
            ada(11)
            tokens_T(0)
            sh_gu(0)
            tokens_T(1)
            sh_gu(1)
            tokens_T(2)
            t.wait_ge(router_in, 32)
            t.wait_ge(h2T_ready, 2 * NT)
            t.wait_ge(mod_ready, 12)
            for i in range(NT):
                for c in range(NC):
                    ins = t.matmul(bank(6, NE * i, NE * (i + 1)), hT[:, c, P * i:P * i + P], w_router[:, c, :],
                                   start=(c == 0), stop=(c == NC - 1))
            ins.then_inc(logit_done, 1)
            transposes(1)
            sh_gu(2)
            t.wait_ge(emask_ready, 1)
            for i in range(NT):
                for k in range(i + 1):
                    t.matmul(bank(3, NE * i, NE * (i + 1)), tri if k == i else ones, emask[:, k, :],
                             start=(k == 0), stop=(k == i))
            for k in range(NT):
                ins = t.matmul(bank(3, NT * NE, NT * NE + NE), ones, emask[:, k, :], start=(k == 0), stop=(k == 2))
            ins.then_inc(pos_done, 1)
            t.wait_ge(prob_ready, 1)
            sh_down(0)
            transposes(2)
            sh_down(1)
            transposes(3)
            sh_down(2)

            def onehot_T(par):
                for i in range(NT):
                    ins = t.matmul(bank(2, (P + 4) * i, (P + 4) * (i + 1)), onehot[par][:, i, :], ident_w[:, i, :],
                                   start=True, stop=True)
                ins.then_inc(ohT_done, 1)

            def gather(par, n, parts):
                every = [(i, part) for i in range(NT) for part in (h_hi, h_lo)]
                for k in parts:
                    i, part = every[k]
                    ins = t.matmul(bank(n), onehot[par][:, i, :], part[:, i, 4 * n:4 * n + 4, :],
                                   start=(k == 0), stop=(k == len(every) - 1))
                if every[k] == every[-1]:
                    ins.then_inc(gathered, 1)

            def gathered_T(p, n):
                t.wait_ge(hg_ready, p * 2 + (n + 1))
                for c in range(4):
                    ins = t.transpose(bank(n, P * c, P * c + P), hg[:, n, P * c:P * c + P], ident)
                ins.then_inc(hgT_done, 1)

            def combine(p, c, par):
                i, n = divmod(c, 2)
                t.wait_ge(f_added, p * 6 + (c + 5))
                for part in (y_hi, y_lo):
                    ins = t.matmul(bank(5 + n), onehotT[par][:, i, :], part[:, 512 * n:512 * (n + 1)],
                                   start=(part is y_hi), stop=(part is y_lo))
                ins.then_inc(f_done, 1)

            def pair(it, q):
                p = it * 2 + q
                slots = (2 * q, 2 * q + 1)
                t.wait_ge(hgT_ready, p * 2 + 2)
                t.wait_ge(wsl_ready, p * 2 + 2)
                for s in slots:
                    t.wait_ge(gu_in[s], it * 16 + 16 * (PRE + 1))
                for c in range(NC):
                    for half, s in enumerate(slots):
                        rows = slice(CAP * half, CAP * (half + 1))
                        ins = t.matmul(bank(2)[rows, :], hgT[:, c, rows], w_gu[s][:, c, :],
                                       start=(c == 0), stop=(c == NC - 1), tile_position=(0, CAP * half))
                        if c == NC - 1:
                            ins.then_inc(gu_used[s], 1)
                t.wait_ge(oh_ready, p + 2)
                nxt = (q + 1) % 2
                t.wait_ge(y_ready, p + 1)
                gather(nxt, 0, (0, 1, 2))
                combine(p, 0, nxt)
                gather(nxt, 0, (3, 4, 5))
                combine(p, 1, nxt)
                gather(nxt, 1, (0, 1, 2))
                combine(p, 2, nxt)
                gather(nxt, 1, (3, 4, 5))
                combine(p, 3, nxt)
                transposes(p + (NT + 1))
                combine(p, 4, nxt)
                gathered_T(p + 1, 0)
                combine(p, 5, nxt)
                gathered_T(p + 1, 1)
                onehot_T(nxt)
                t.wait_ge(actT_ready, p + (NT + 1))
                for s in slots:
                    t.wait_ge(dn_in[s], it * 16 + 16 * (1 + dn_base(s)))
                for n in range(2):
                    for j in range(2):
                        for half, s in enumerate(slots):
                            rows = slice(CAP * half, CAP * (half + 1))
                            ins = t.matmul(bank(3 + n)[rows, :], actT[:, j, rows], w_dn[s][:, j, 512 * n:512 * (n + 1)],
                                           start=(j == 0), stop=(j == 1), tile_position=(0, CAP * half))
                            if n == 1 and j == 1:
                                ins.then_inc(dn_used[s], 1)

            t.wait_ge(hi_ready, NT)
            t.wait_ge(lo_ready, NT)
            t.wait_ge(oh_ready, 1)
            t.wait_ge(a_ready, 2)
            t.wait_ge(ident_ready, 1)
            onehot_T(0)
            for n in range(2):
                gather(0, n, range(6))
            for n in range(2):
                gathered_T(0, n)
            t.wait_ge(item_ready, 1)
            t.matmul(bank(4, 0, NE), ones[0:NE, :], diag_e[:, :], start=True, stop=True)
            t.matmul(bank(4, NE, 2 * NE), ones[0:NE, :], diag_r[:, :], start=True, stop=True).then_inc(tab_done, 1)
            with t.Fori(0, MAIN_PAIRS // 2) as it:
                for q in range(2):
                    pair(it, q)
            t.wait_ge(tab_ready, 1)
            n_pairs = t.value_load(table_e[0:1, N_TAB:N_TAB + 1], min_val=0, max_val=OVER_PAIRS)
            odd = t.value_load(table_e[0:1, N_TAB + 1:N_TAB + 2], min_val=0, max_val=1)
            with t.If(n_pairs > 0):
                pair(MAIN_PAIRS // 2, 0)
            with t.Else():
                t.nop()
            with t.If(n_pairs > 1):
                pair(MAIN_PAIRS // 2, 1)
                with t.Fori(1, OVER_PAIRS // 2) as jj:
                    for q in range(2):
                        with t.If(jj * 2 + q < n_pairs):
                            pair(jj + MAIN_PAIRS // 2, q)
                        with t.Else():
                            t.nop()
            with t.Else():
                t.nop()

            def total_so_far(c):
                i, n = divmod(c, 2)
                t.matmul(bank(c), ident, f_acc[:, i, 512 * n:512 * (n + 1)], start=True, stop=False)

            def last_outputs(par, i):
                for n in range(2):
                    t.matmul(bank(2 * i + n), onehotT[par][:, i, :], y_hi[:, 512 * n:512 * (n + 1)], start=False, stop=False)
                    ins = t.matmul(bank(2 * i + n), onehotT[par][:, i, :], y_lo[:, 512 * n:512 * (n + 1)],
                                   start=False, stop=True)
                ins.then_inc(total_done, 1)

            def all_outputs(par):
                last_outputs(par, 0)
                total_so_far(3)
                last_outputs(par, 1)
                total_so_far(4)
                total_so_far(5)
                last_outputs(par, 2)

            t.wait_ge(f_added, n_pairs * 6 + (6 * MAIN_PAIRS + 6))
            t.wait_ge(hgT_ready, n_pairs * 2 + (2 * MAIN_PAIRS + 2))
            total_so_far(0)
            total_so_far(1)
            t.wait_ge(wsl_ready, n_pairs * 2 + (2 * MAIN_PAIRS + 2))
            total_so_far(2)
            t.wait_ge(ohT_ready, n_pairs + (MAIN_PAIRS + 1))
            t.wait_ge(y_ready, n_pairs + (MAIN_PAIRS + 1))
            with t.If(odd > 0):
                all_outputs(0)
            with t.Else():
                all_outputs(1)



_INS = ["x_prompt", "x_sample", "state_C", "state_n", "state_m", "c", "c_ctx", "w_ada", "b_ada", "g_pre_mix", "w_in",
        "b_gate", "w_pool", "pool_scale", "w_out", "g_post_mix", "g_pre_ffn", "w_router", "b_router", "w_expert_gu",
        "w_expert_down", "w_shared_gu", "w_shared_down", "g_post_ffn"]
_OUTS = [(1, T_CTX, D), (1, T_LAT, D), (1, 1, 2, H, DH, DH), (1, 1, 2, H, DH), (1, 1, 2, H)]


def kernel(**inputs):
    import concourse.bacc as _bacc
    from concourse.bass_utils import run_bass_kernel_spmd as _run

    nc = _bacc.Bacc("TRN2", target_bir_lowering=False, num_devices=1)
    arrays, t_in = {}, {}
    for name in _INS:
        arrays[f"in_{name}"] = np.ascontiguousarray(inputs[name])
    arrays["in_shape_constants"] = shape_constants()
    arrays["in_pool_constants"] = pool_constants()
    for key, a in arrays.items():
        t_in[key[3:]] = nc.dram_tensor(key, a.shape, mybir.dt.from_np(a.dtype), kind="ExternalInput").ap()
    t_out = [nc.dram_tensor(f"out_{i}", shape, F32, kind="ExternalOutput").ap() for i, shape in enumerate(_OUTS)]
    build_layer(nc, t_in, t_out)
    r = _run(nc, [arrays], core_ids=[0])
    return tuple(r.results[0][f"out_{i}"] for i in range(len(_OUTS)))
```
